# Optimizing a Trainium2 kernel written in Bass

```python
import math
import jax, jax.numpy as jnp
from jax import lax
import numpy as np

D_MODEL = 1024
BATCH = 1
SEQ = 256
DEPTH = 2

N_HEADS = 16
HEAD_DIM = D_MODEL // N_HEADS
Q_BLOCK = 128
POOL_WINDOWS = (2, 4, 8, 16)
N_POOL_GROUPS = len(POOL_WINDOWS)
POOL_CH = D_MODEL // N_POOL_GROUPS
N_EXPERTS = 32
N_EXPERT_GROUPS = 4
EXPERTS_PER_GROUP = N_EXPERTS // N_EXPERT_GROUPS
TOPK_GROUPS = 1
TOP_K = 2
D_FF_EXPERT = D_MODEL // 2
EXPERT_BLOCK = 256
N_MIXERS = 2
N_ATTN = (DEPTH + 1) // 2
N_POOL = DEPTH // 2
RMS_EPS = 1e-6


def rmsnorm(x, g):
    xf = x.astype(jnp.float32)
    xf = xf * lax.rsqrt(jnp.mean(xf * xf, axis=-1, keepdims=True) + RMS_EPS)
    return (xf * g.astype(jnp.float32)).astype(x.dtype)

def modulate(h, shift, scale):
    return h * (1.0 + scale[:, None, :]) + shift[:, None, :]

def fox_attention(h, w_in, f_bias, w_o):
    B, S, D = h.shape
    proj = h @ w_in
    q, k, v, f = jnp.split(proj, [D, 2 * D, 3 * D], axis=-1)
    to_heads = lambda t: t.reshape(B, S, N_HEADS, HEAD_DIM).transpose(0, 2, 1, 3)
    q, k, v = to_heads(q), to_heads(k), to_heads(v)
    log_f = jax.nn.log_sigmoid(f.astype(jnp.float32) + f_bias.astype(jnp.float32))
    F = jnp.cumsum(log_f, axis=1).transpose(0, 2, 1)
    scale = 1.0 / math.sqrt(HEAD_DIM)
    kpos = jnp.arange(S)
    n_blocks = S // Q_BLOCK

    def q_block(i):
        start = i * Q_BLOCK
        qb = lax.dynamic_slice_in_dim(q, start, Q_BLOCK, axis=2)
        Fq = lax.dynamic_slice_in_dim(F, start, Q_BLOCK, axis=2)
        logits = jnp.einsum('bhqd,bhkd->bhqk', qb, k).astype(jnp.float32) * scale
        logits = logits + Fq[..., :, None] - F[:, :, None, :]
        qpos = start + jnp.arange(Q_BLOCK)
        causal = kpos[None, :] <= qpos[:, None]
        logits = jnp.where(causal[None, None], logits, -jnp.inf)
        p = jax.nn.softmax(logits, axis=-1)
        return jnp.einsum('bhqk,bhkd->bhqd', p.astype(v.dtype), v)

    o = lax.map(q_block, jnp.arange(n_blocks))
    o = o.transpose(1, 0, 3, 2, 4).reshape(B, S, D)
    return (o @ w_o).astype(h.dtype)

def pool_mixer(h, w_pool, ch_scale):
    B, S, D = h.shape
    hf = h.astype(jnp.float32)
    cs = jnp.cumsum(hf, axis=1)
    t = jnp.arange(S)
    outs = []
    for g, win in enumerate(POOL_WINDOWS):
        sl = slice(g * POOL_CH, (g + 1) * POOL_CH)
        csg = cs[..., sl]
        shifted = jnp.pad(csg, ((0, 0), (win, 0), (0, 0)))[:, :S]
        count = jnp.minimum(t + 1, win).astype(jnp.float32)[None, :, None]
        outs.append((csg - shifted) / count - hf[..., sl])
    pooled = jnp.stack(outs, axis=2).astype(h.dtype)
    y = jnp.einsum('bsgc,gce->bsge', pooled, w_pool).reshape(B, S, D)
    return (y * ch_scale).astype(h.dtype)

def grouped_moe(h, router_w, router_bias, w1, w3, w2):
    B, S, D = h.shape
    T = B * S
    hf = h.reshape(T, D)
    scores = jax.nn.sigmoid((hf @ router_w).astype(jnp.float32))
    sel = scores + router_bias.astype(jnp.float32)
    sel_g = sel.reshape(T, N_EXPERT_GROUPS, EXPERTS_PER_GROUP)
    group_score = lax.top_k(sel_g, TOP_K)[0].sum(-1)
    _, g_idx = lax.top_k(group_score, TOPK_GROUPS)
    g_mask = jnp.any(g_idx[..., None] == jnp.arange(N_EXPERT_GROUPS), axis=1)
    e_mask = jnp.repeat(g_mask, EXPERTS_PER_GROUP, axis=1)
    _, e_idx = lax.top_k(jnp.where(e_mask, sel, -jnp.inf), TOP_K)
    gate = jnp.take_along_axis(scores, e_idx, axis=1)
    gate = gate / jnp.sum(gate, axis=-1, keepdims=True)

    A = T * TOP_K
    e_flat = e_idx.reshape(A)
    tok_flat = jnp.repeat(jnp.arange(T, dtype=jnp.int32), TOP_K)
    w_flat = gate.reshape(A)
    order = jnp.argsort(e_flat)
    e_sorted = e_flat[order]
    counts = jnp.bincount(e_flat, length=N_EXPERTS)
    padded = ((counts + EXPERT_BLOCK - 1) // EXPERT_BLOCK) * EXPERT_BLOCK
    starts = jnp.cumsum(counts) - counts
    pends = jnp.cumsum(padded)
    pstarts = pends - padded
    rank = jnp.arange(A) - starts[e_sorted]
    dest = pstarts[e_sorted] + rank
    n_blocks = A // EXPERT_BLOCK + N_EXPERTS
    P = n_blocks * EXPERT_BLOCK
    row_tok = jnp.full((P,), T, dtype=jnp.int32).at[dest].set(tok_flat[order])
    row_w = jnp.zeros((P,), jnp.float32).at[dest].set(w_flat[order])
    block_e = jnp.minimum(
        jnp.searchsorted(pends, jnp.arange(n_blocks) * EXPERT_BLOCK, side='right'),
        N_EXPERTS - 1)
    x_rows = jnp.concatenate([hf, jnp.zeros((1, D), hf.dtype)], axis=0)[row_tok]
    x_rows = x_rows.reshape(n_blocks, EXPERT_BLOCK, D)

    def expert_block(args):
        xb, e = args
        return (jax.nn.silu(xb @ w1[e]) * (xb @ w3[e])) @ w2[e]

    y = lax.map(expert_block, (x_rows, block_e)).reshape(P, D)
    out = jax.ops.segment_sum(y.astype(jnp.float32) * row_w[:, None], row_tok,
                              num_segments=T + 1)[:T]
    return out.reshape(B, S, D).astype(h.dtype)

def first_inputs(seed: int = 0) -> dict:
    key = jax.random.key(seed)
    ks = jax.random.split(key, 20)
    D, H, E, Fd = D_MODEL, N_HEADS, N_EXPERTS, D_FF_EXPERT
    nrm = lambda k, shape, s: jax.random.normal(k, shape, jnp.float32) * s
    return {
        "x": nrm(ks[0], (BATCH, SEQ, D), 1.0),
        "c": nrm(ks[1], (BATCH, D), 1.0),
        "norm_mix_g": 1.0 + nrm(ks[2], (DEPTH, D), 0.05),
        "norm_ffn_g": 1.0 + nrm(ks[3], (DEPTH, D), 0.05),
        "ada_w": nrm(ks[4], (DEPTH, D, 6 * D), 0.5 * D ** -0.5),
        "ada_b": nrm(ks[5], (DEPTH, 6 * D), 0.01),
        "attn_w_in": nrm(ks[6], (N_ATTN, D, 3 * D + H), D ** -0.5),
        "attn_f_bias": 2.0 + nrm(ks[7], (N_ATTN, H), 0.5),
        "attn_w_o": nrm(ks[8], (N_ATTN, D, D), D ** -0.5),
        "pool_w": nrm(ks[9], (N_POOL, N_POOL_GROUPS, POOL_CH, POOL_CH), POOL_CH ** -0.5),
        "pool_scale": 0.5 + nrm(ks[10], (N_POOL, D), 0.1),
        "router_w": nrm(ks[11], (D, E), D ** -0.5),
        "router_bias": nrm(ks[12], (E,), 0.01),
        "exp_w1": nrm(ks[13], (DEPTH, E, D, Fd), D ** -0.5),
        "exp_w3": nrm(ks[14], (DEPTH, E, D, Fd), D ** -0.5),
        "exp_w2": nrm(ks[15], (DEPTH, E, Fd, D), Fd ** -0.5),
        "norm_final_g": 1.0 + nrm(ks[16], (D,), 0.05),
    }

def first_block(x, c, norm_mix_g, norm_ffn_g, ada_w, ada_b, attn_w_in, attn_f_bias,
              attn_w_o, pool_w, pool_scale, router_w, router_bias, exp_w1, exp_w3,
              exp_w2, norm_final_g):
    c_act = jax.nn.silu(c)
    for i in range(DEPTH):
        mod = c_act @ ada_w[i] + ada_b[i]
        sh_m, sc_m, gt_m, sh_f, sc_f, gt_f = jnp.split(mod, 6, axis=-1)
        h = modulate(rmsnorm(x, norm_mix_g[i]), sh_m, sc_m)
        if i % N_MIXERS == 0:
            j = i // N_MIXERS
            y = fox_attention(h, attn_w_in[j], attn_f_bias[j], attn_w_o[j])
        else:
            j = i // N_MIXERS
            y = pool_mixer(h, pool_w[j], pool_scale[j])
        x = x + gt_m[:, None, :] * y
        h = modulate(rmsnorm(x, norm_ffn_g[i]), sh_f, sc_f)
        y = grouped_moe(h, router_w, router_bias, exp_w1[i], exp_w3[i], exp_w2[i])
        x = x + gt_f[:, None, :] * y
    return rmsnorm(x, norm_final_g)


N_EVEN = (DEPTH + 1) // 2
N_ODD = DEPTH // 2

M_WIDTH = D_MODEL // 2
M_HEADS = 4
M_HEAD_DIM = M_WIDTH // M_HEADS
M_CONV = 4
QKV_BLOCK = 4
M_CHUNK = 64
S_WIDTH = D_MODEL // 2
S_GROUP = 16
S_GROUPS = S_WIDTH // S_GROUP
S_STATE = 64
DT_MIN = 1e-3
DT_MAX = 1e-1
IN_EVEN = 2 * M_WIDTH + S_WIDTH
MIX_EVEN = M_WIDTH + S_WIDTH
H_EXPAND = 128
H_HEADS = D_MODEL // H_EXPAND
H_WIDTH = H_HEADS * H_EXPAND
H_CHUNK = 64
IN_ODD = 4 * H_WIDTH
D_FF = -(-8 * D_MODEL // (3 * 256)) * 256
EPS = 1e-6


def rmsnorm_2(x, g):
    xf = x.astype(jnp.float32)
    return xf * lax.rsqrt(jnp.mean(xf * xf, axis=-1, keepdims=True) + EPS) * g

def causal_dwconv(x, w, b):
    K, Cc = w.shape
    y = lax.conv_general_dilated(x, w[:, None, :].astype(x.dtype), window_strides=(1,), padding=[(K - 1, 0)],
                                 dimension_numbers=('NWC', 'WIO', 'NWC'), feature_group_count=Cc)
    return y + b

def swiglu(x, w1, w3, w2):
    return (jax.nn.silu(x @ w1) * (x @ w3)) @ w2

def mlstm_chunkwise(q, k, v, i_pre, f_pre):
    f32 = jnp.float32
    Bsz, H, L, Dh = q.shape
    C = M_CHUNK
    NC = L // C
    q, k, v = (t.astype(f32).reshape(Bsz, H, NC, C, Dh) for t in (q, k, v))
    log_f = jax.nn.log_sigmoid(f_pre.astype(f32)).reshape(Bsz, H, NC, C)
    log_i = i_pre.astype(f32).reshape(Bsz, H, NC, C)
    b = jnp.cumsum(log_f, axis=-1)
    b_last = b[..., -1]
    causal = jnp.tril(jnp.ones((C, C), dtype=bool))
    d_log = jnp.where(causal, b[..., :, None] - b[..., None, :] + log_i[..., None, :], -jnp.inf)
    m_intra = jnp.max(d_log, axis=-1)
    a = b_last[..., None] - b + log_i
    a_max = jnp.max(a, axis=-1)
    kw = k * jnp.exp(a - a_max[..., None])[..., None]
    U = jnp.einsum('bhcsk,bhcsv->bhckv', kw, v)
    un = jnp.sum(kw, axis=-2)

    def step(carry, inp):
        c_st, n_st, m_st = carry
        u_c, un_c, am_c, bl_c = inp
        m_new = jnp.maximum(bl_c + m_st, am_c)
        s_old = jnp.exp(bl_c + m_st - m_new)
        s_new = jnp.exp(am_c - m_new)
        c_new = s_old[..., None, None] * c_st + s_new[..., None, None] * u_c
        n_new = s_old[..., None] * n_st + s_new[..., None] * un_c
        return (c_new, n_new, m_new), (c_st, n_st, m_st)

    init = (jnp.zeros((Bsz, H, Dh, Dh), f32), jnp.zeros((Bsz, H, Dh), f32), jnp.zeros((Bsz, H), f32))
    xs = (jnp.moveaxis(U, 2, 0), jnp.moveaxis(un, 2, 0), jnp.moveaxis(a_max, 2, 0), jnp.moveaxis(b_last, 2, 0))
    _, (c_prev, n_prev, m_prev) = lax.scan(step, init, xs)
    c_prev = jnp.moveaxis(c_prev, 0, 2)
    n_prev = jnp.moveaxis(n_prev, 0, 2)
    m_prev = jnp.moveaxis(m_prev, 0, 2)
    inter_log = b + m_prev[..., None]
    m_t = jnp.maximum(inter_log, m_intra)
    s_inter = jnp.exp(inter_log - m_t)
    scores = jnp.einsum('bhctd,bhcsd->bhcts', q, k) * jnp.exp(d_log - m_t[..., None])
    num = jnp.einsum('bhcts,bhcsv->bhctv', scores, v) + s_inter[..., None] * jnp.einsum('bhctk,bhckv->bhctv', q, c_prev)
    den = jnp.sum(scores, axis=-1) + s_inter * jnp.einsum('bhctk,bhck->bhct', q, n_prev)
    h = num / jnp.maximum(jnp.abs(den), jnp.exp(-m_t))[..., None]
    return h.reshape(Bsz, H, L, Dh)

def _complex_affine_combine(e1, e2):
    a1r, a1i, b1r, b1i = e1
    a2r, a2i, b2r, b2i = e2
    return (a2r * a1r - a2i * a1i, a2r * a1i + a2i * a1r,
            a2r * b1r - a2i * b1i + b2r, a2r * b1i + a2i * b1r + b2i)

def s5_ssm(u, a_re, a_im, log_dt, b_re, b_im, c_re, c_im, d_skip):
    f32 = jnp.float32
    Bsz, L, _ = u.shape
    ug = u.astype(f32).reshape(Bsz, L, S_GROUPS, S_GROUP)
    a_re, a_im, b_re, b_im, c_re, c_im = (t.astype(f32) for t in (a_re, a_im, b_re, b_im, c_re, c_im))
    dt = jnp.exp(log_dt.astype(f32))[:, None]
    mag = jnp.exp(a_re * dt)
    ab_re = mag * jnp.cos(a_im * dt)
    ab_im = mag * jnp.sin(a_im * dt)
    inv = 1.0 / (a_re * a_re + a_im * a_im)
    g_re = ((ab_re - 1.0) * a_re + ab_im * a_im) * inv
    g_im = (ab_im * a_re - (ab_re - 1.0) * a_im) * inv
    bb_re = g_re[..., None] * b_re - g_im[..., None] * b_im
    bb_im = g_re[..., None] * b_im + g_im[..., None] * b_re
    bu_re = jnp.einsum('blgp,gnp->blgn', ug, bb_re)
    bu_im = jnp.einsum('blgp,gnp->blgn', ug, bb_im)
    shp = (1, L, S_GROUPS, S_STATE)
    a_seq_re = jnp.broadcast_to(ab_re, shp)
    a_seq_im = jnp.broadcast_to(ab_im, shp)
    _, _, x_re, x_im = lax.associative_scan(_complex_affine_combine, (a_seq_re, a_seq_im, bu_re, bu_im), axis=1)
    y = jnp.einsum('blgn,gpn->blgp', x_re, c_re) - jnp.einsum('blgn,gpn->blgp', x_im, c_im)
    y = y + d_skip.astype(f32).reshape(S_GROUPS, S_GROUP) * ug
    return y.reshape(Bsz, L, S_WIDTH)

def mixer_ab(x, w_in, conv_w, conv_b, wq, wk, wv, w_if, b_if, mh_gain, skip,
             a_re, a_im, log_dt, b_re, b_im, c_re, c_im, d_skip, w_glu, b_glu, w_out):
    Bsz, L, _ = x.shape
    proj = x @ w_in
    xm = proj[..., :M_WIDTH]
    zm = proj[..., M_WIDTH:2 * M_WIDTH]
    us = proj[..., 2 * M_WIDTH:]
    xc = jax.nn.silu(causal_dwconv(xm, conv_w, conv_b))
    nb = M_WIDTH // QKV_BLOCK
    xc_b = xc.reshape(Bsz, L, nb, QKV_BLOCK)
    xm_b = xm.reshape(Bsz, L, nb, QKV_BLOCK)
    q = jnp.einsum('blnd,nde->blne', xc_b, wq).reshape(Bsz, L, M_WIDTH)
    k = jnp.einsum('blnd,nde->blne', xc_b, wk).reshape(Bsz, L, M_WIDTH) * (M_HEAD_DIM ** -0.5)
    v = jnp.einsum('blnd,nde->blne', xm_b, wv).reshape(Bsz, L, M_WIDTH)
    gates = jnp.concatenate([q, k, v], axis=-1) @ w_if + b_if
    to_h = lambda t: t.reshape(Bsz, L, M_HEADS, M_HEAD_DIM).transpose(0, 2, 1, 3)
    h = mlstm_chunkwise(to_h(q), to_h(k), to_h(v),
                        gates[..., :M_HEADS].transpose(0, 2, 1), gates[..., M_HEADS:].transpose(0, 2, 1))
    mu = jnp.mean(h, axis=-1, keepdims=True)
    var = jnp.mean(jnp.square(h - mu), axis=-1, keepdims=True)
    hn = ((h - mu) * lax.rsqrt(var + EPS)).transpose(0, 2, 1, 3).reshape(Bsz, L, M_WIDTH) * mh_gain
    out_m = (hn + skip * xc) * jax.nn.silu(zm)
    y = jax.nn.gelu(s5_ssm(us, a_re, a_im, log_dt, b_re, b_im, c_re, c_im, d_skip))
    out_s = y * jax.nn.sigmoid(y @ w_glu + b_glu)
    return jnp.concatenate([out_m, out_s], axis=-1) @ w_out

def hgrn2_chunkwise(q, k, v, log_f):
    f32 = jnp.float32
    Bsz, H, L, E = q.shape
    C = H_CHUNK
    NC = L // C
    q, k, v, log_f = (t.astype(f32).reshape(Bsz, H, NC, C, E) for t in (q, k, v, log_f))
    b = jnp.cumsum(log_f, axis=3)
    b_last = b[:, :, :, -1:, :]
    q_inter = q * jnp.exp(b)
    k_state = k * jnp.exp(b_last - b)
    q_intra = q * jnp.exp(b - b_last)
    causal = jnp.tril(jnp.ones((C, C), dtype=bool))
    scores = jnp.where(causal, jnp.einsum('bhctk,bhcsk->bhcts', q_intra, k_state), 0.0)
    intra = jnp.einsum('bhcts,bhcsv->bhctv', scores, v)
    U = jnp.einsum('bhcsk,bhcsv->bhckv', k_state, v)
    decay = jnp.exp(b_last[:, :, :, 0, :])

    def step(s, inp):
        u_c, d_c = inp
        return d_c[..., None] * s + u_c, s

    _, s_prev = lax.scan(step, jnp.zeros((Bsz, H, E, E), f32), (jnp.moveaxis(U, 2, 0), jnp.moveaxis(decay, 2, 0)))
    s_prev = jnp.moveaxis(s_prev, 0, 2)
    inter = jnp.einsum('bhctk,bhckv->bhctv', q_inter, s_prev)
    return (intra + inter).reshape(Bsz, H, L, E)

def mixer_c(x, layer_idx, w_in, lb_raw, g_gain, w_out):
    Bsz, L, _ = x.shape
    proj = x @ w_in
    q = jax.nn.silu(proj[..., :H_WIDTH])
    f = proj[..., H_WIDTH:2 * H_WIDTH].astype(jnp.float32)
    i = proj[..., 2 * H_WIDTH:3 * H_WIDTH]
    g = proj[..., 3 * H_WIDTH:]
    lbs = jnp.cumsum(jax.nn.softmax(lb_raw.astype(jnp.float32), axis=0), axis=0)
    lb = lbs[layer_idx] - lbs[0]
    fg = lb + (1.0 - lb) * jax.nn.sigmoid(f)
    to_h = lambda t: t.reshape(Bsz, L, H_HEADS, H_EXPAND).transpose(0, 2, 1, 3)
    o = hgrn2_chunkwise(to_h(q), to_h(1.0 - fg), to_h(i), to_h(jnp.log(fg)))
    o = o * lax.rsqrt(jnp.mean(o * o, axis=-1, keepdims=True) + EPS)
    o = o.transpose(0, 2, 1, 3).reshape(Bsz, L, H_WIDTH) * g_gain * jax.nn.silu(g)
    return o @ w_out

def second_inputs(seed: int = 0) -> dict:
    key = jax.random.key(seed)
    ks = iter(jax.random.split(key, 48))
    f32 = jnp.float32
    nrm = lambda shape, scale: scale * jax.random.normal(next(ks), shape, f32)
    NE, NO = N_EVEN, N_ODD
    nb = M_WIDTH // QKV_BLOCK
    b_if = jnp.concatenate([nrm((NE, M_HEADS), 0.1),
                            jnp.broadcast_to(jnp.linspace(3.0, 6.0, M_HEADS, dtype=f32), (NE, M_HEADS)) + nrm((NE, M_HEADS), 0.01)], axis=-1)
    return {
        'x': nrm((BATCH, SEQ, D_MODEL), 1.0),
        'norm_g': 1.0 + nrm((DEPTH, 4, D_MODEL), 0.05),
        'ab_w_in': nrm((NE, D_MODEL, IN_EVEN), D_MODEL ** -0.5),
        'ab_conv_w': nrm((NE, M_CONV, M_WIDTH), M_CONV ** -0.5),
        'ab_conv_b': nrm((NE, M_WIDTH), 0.01),
        'ab_wq': nrm((NE, nb, QKV_BLOCK, QKV_BLOCK), QKV_BLOCK ** -0.5),
        'ab_wk': nrm((NE, nb, QKV_BLOCK, QKV_BLOCK), QKV_BLOCK ** -0.5),
        'ab_wv': nrm((NE, nb, QKV_BLOCK, QKV_BLOCK), QKV_BLOCK ** -0.5),
        'ab_w_if': nrm((NE, 3 * M_WIDTH, 2 * M_HEADS), 0.1 * (3 * M_WIDTH) ** -0.5),
        'ab_b_if': b_if,
        'ab_mh_gain': 1.0 + nrm((NE, M_WIDTH), 0.05),
        'ab_skip': 1.0 + nrm((NE, M_WIDTH), 0.05),
        'ab_a_re': -0.5 + nrm((NE, S_GROUPS, S_STATE), 0.01),
        'ab_a_im': jnp.pi * jnp.arange(S_STATE, dtype=f32) + nrm((NE, S_GROUPS, S_STATE), 0.01),
        'ab_log_dt': jax.random.uniform(next(ks), (NE, S_GROUPS), f32, math.log(DT_MIN), math.log(DT_MAX)),
        'ab_b_re': nrm((NE, S_GROUPS, S_STATE, S_GROUP), (2 * S_GROUP) ** -0.5),
        'ab_b_im': nrm((NE, S_GROUPS, S_STATE, S_GROUP), (2 * S_GROUP) ** -0.5),
        'ab_c_re': nrm((NE, S_GROUPS, S_GROUP, S_STATE), S_STATE ** -0.5),
        'ab_c_im': nrm((NE, S_GROUPS, S_GROUP, S_STATE), S_STATE ** -0.5),
        'ab_d': nrm((NE, S_WIDTH), 1.0),
        'ab_w_glu': nrm((NE, S_WIDTH, S_WIDTH), S_WIDTH ** -0.5),
        'ab_b_glu': nrm((NE, S_WIDTH), 0.01),
        'ab_w_out': nrm((NE, MIX_EVEN, D_MODEL), MIX_EVEN ** -0.5),
        'c_w_in': nrm((NO, D_MODEL, IN_ODD), D_MODEL ** -0.5),
        'c_lb_raw': nrm((DEPTH, H_WIDTH), 0.1),
        'c_g_gain': 1.0 + nrm((NO, H_WIDTH), 0.05),
        'c_w_out': nrm((NO, H_WIDTH, D_MODEL), H_WIDTH ** -0.5),
        'ffn_w1': nrm((DEPTH, D_MODEL, D_FF), D_MODEL ** -0.5),
        'ffn_w3': nrm((DEPTH, D_MODEL, D_FF), D_MODEL ** -0.5),
        'ffn_w2': nrm((DEPTH, D_FF, D_MODEL), D_FF ** -0.5),
    }

def second_block(x, norm_g, ab_w_in, ab_conv_w, ab_conv_b, ab_wq, ab_wk, ab_wv, ab_w_if, ab_b_if, ab_mh_gain, ab_skip,
              ab_a_re, ab_a_im, ab_log_dt, ab_b_re, ab_b_im, ab_c_re, ab_c_im, ab_d, ab_w_glu, ab_b_glu, ab_w_out,
              c_w_in, c_lb_raw, c_g_gain, c_w_out, ffn_w1, ffn_w3, ffn_w2):
    for layer in range(DEPTH):
        j = layer // 2
        h = rmsnorm_2(x, norm_g[layer, 0])
        if layer % 2 == 0:
            mix = mixer_ab(h, ab_w_in[j], ab_conv_w[j], ab_conv_b[j], ab_wq[j], ab_wk[j], ab_wv[j], ab_w_if[j],
                           ab_b_if[j], ab_mh_gain[j], ab_skip[j], ab_a_re[j], ab_a_im[j], ab_log_dt[j], ab_b_re[j],
                           ab_b_im[j], ab_c_re[j], ab_c_im[j], ab_d[j], ab_w_glu[j], ab_b_glu[j], ab_w_out[j])
        else:
            mix = mixer_c(h, layer, c_w_in[j], c_lb_raw, c_g_gain[j], c_w_out[j])
        x = x + rmsnorm_2(mix, norm_g[layer, 1])
        h = rmsnorm_2(x, norm_g[layer, 2])
        x = x + rmsnorm_2(swiglu(h, ffn_w1[layer], ffn_w3[layer], ffn_w2[layer]), norm_g[layer, 3])
    return x


def setup_inputs(seed=0):
    out = dict(first_inputs(seed))
    for name, value in second_inputs(seed + 1).items():
        if name != "x":
            out[name + "_2"] = value
    return out


def reference(
    x, c, norm_mix_g, norm_ffn_g, ada_w, ada_b, attn_w_in, attn_f_bias, attn_w_o, pool_w,
    pool_scale, router_w, router_bias, exp_w1, exp_w3, exp_w2, norm_final_g, norm_g_2,
    ab_w_in_2, ab_conv_w_2, ab_conv_b_2, ab_wq_2, ab_wk_2, ab_wv_2, ab_w_if_2, ab_b_if_2,
    ab_mh_gain_2, ab_skip_2, ab_a_re_2, ab_a_im_2, ab_log_dt_2, ab_b_re_2, ab_b_im_2, ab_c_re_2,
    ab_c_im_2, ab_d_2, ab_w_glu_2, ab_b_glu_2, ab_w_out_2, c_w_in_2, c_lb_raw_2, c_g_gain_2,
    c_w_out_2, ffn_w1_2, ffn_w3_2, ffn_w2_2,
):
    x = first_block(
        x, c, norm_mix_g, norm_ffn_g, ada_w, ada_b, attn_w_in, attn_f_bias, attn_w_o, pool_w,
        pool_scale, router_w, router_bias, exp_w1, exp_w3, exp_w2, norm_final_g,
    )
    return second_block(
        x, norm_g_2, ab_w_in_2, ab_conv_w_2, ab_conv_b_2, ab_wq_2, ab_wk_2, ab_wv_2, ab_w_if_2,
        ab_b_if_2, ab_mh_gain_2, ab_skip_2, ab_a_re_2, ab_a_im_2, ab_log_dt_2, ab_b_re_2,
        ab_b_im_2, ab_c_re_2, ab_c_im_2, ab_d_2, ab_w_glu_2, ab_b_glu_2, ab_w_out_2, c_w_in_2,
        c_lb_raw_2, c_g_gain_2, c_w_out_2, ffn_w1_2, ffn_w3_2, ffn_w2_2,
    )


_drawn_inputs = setup_inputs


def setup_inputs(seed=0):
    import zlib

    import numpy as np

    out = dict(_drawn_inputs(seed))
    spreads = {}
    factors = {'ab_conv_b_2': 4.808,
     'ab_a_re_2': 200.0,
     'ab_b_glu_2': 27.221,
     'c_lb_raw_2': 7.749,
     'ab_a_im_2': 31.6,
     'ab_log_dt_2': 34.472,
     'ab_b_re_2': 43.696,
     'ab_b_im_2': 43.944,
     'ab_c_re_2': 43.12,
     'ab_c_im_2': 44.504}
    for name, (base, spread) in spreads.items():
        noise = np.random.default_rng([zlib.crc32(name.encode()), seed]).standard_normal(out[name].shape)
        drawn = base * np.exp(spread * noise) if base else spread * noise
        out[name] = __import__('jax').numpy.asarray(drawn.astype(out[name].dtype))
    for name, factor in factors.items():
        out[name] = (out[name] * factor).astype(out[name].dtype)
    return out
```

```python
from contextlib import ExitStack

import numpy as np
import concourse.bass as bass
from concourse import mybir

ALU = mybir.AluOpType
ACT = mybir.ActivationFunctionType
F32 = mybir.dt.float32
I32 = mybir.dt.int32
U32 = mybir.dt.uint32
AX = mybir.AxisListType

P = 128
D = 1024
S = 256
TT = S // P
KD = D // P
N_HEADS, HEAD_DIM = 16, 64
WINDOWS = (2, 4, 8, 16)
N_EXPERTS, N_GROUPS, D_FF = 32, 4, 512
GROUP = N_EXPERTS // N_GROUPS
SLOTS = 64
BLOCKS = 40
PAIRS = BLOCKS // 2
M_WIDTH, M_HEADS, M_CONV = 512, 4, 4
M_DIM = M_WIDTH // M_HEADS
S_WIDTH, S_GROUPS, S_STATE, S_GROUP = 512, 32, 64, 16
S_PAIRS = S_GROUPS // 2
H_HEADS, H_CHUNK = 8, 64
F_FF = 2816
EPS = 1e-6
NEG = -1e30
UNIT = 4096
RING = 6


def shape_constants():
    p = np.arange(P)[:, None]
    c = np.arange(P)[None, :]
    t = np.arange(S)
    parts = {
        "ident": np.eye(P),
        "ones": np.ones((P, P)),
        "upto": (p <= c),
        "before": (p < c),
        "mask_ts": np.where(c > p, NEG, 0.0),
        "mask_st": np.where(p > c, NEG, 0.0),
        "iota": np.broadcast_to(c, (P, P)),
        "inverse_count": np.broadcast_to(
            np.stack([1.0 / np.minimum(t + 1, w) for w in WINDOWS]).reshape(1, -1), (P, 4 * S)),
        "quads": (np.repeat(np.arange(32), 4)[None, :] == p // 4),
        "half": (np.arange(2)[None, :] == p // 64),
        "odd16": (np.arange(2)[None, :] == (p // 16) % 2),
        "pair_width": np.full((P, 2), 2 * SLOTS),
        "iota4": np.broadcast_to(np.arange(4), (P, 4)),
        "iota40": np.broadcast_to(np.arange(BLOCKS), (P, BLOCKS)),
        "restart": np.broadcast_to((t % H_CHUNK != 0), (P, S)),
        "bits_chunk": ((p // H_CHUNK == c // H_CHUNK) & (p <= c)),
    }
    at, where = 0, {}
    for name, a in parts.items():
        where[name] = (at, a.shape[1])
        at += a.shape[1]
    return np.concatenate([np.asarray(a, np.float32) for a in parts.values()], 1), where


CONSTANTS, CONSTANT_AT = shape_constants()

VECTORS = [
    ("norm_mix_g", 16), ("norm_ffn_g", 16), ("c", 8), ("ab_conv_w_2", 16), ("ab_conv_b_2", 4),
    ("ab_mh_gain_2", 4), ("ab_skip_2", 4), ("ab_d_2", 4), ("ab_b_glu_2", 4), ("c_g_gain_2", 8),
    ("c_lb_raw_2", 16), ("norm_g_2", 64),
]


class Chain:

    def __init__(self, eng, sem):
        self.eng, self.sem, self.n = eng, sem, 0

    def __call__(self, ins):
        self.n += 1
        ins.then_inc(self.sem, 1)
        self.eng.wait_ge(self.sem, self.n)
        return ins


class WeightRing:

    def __init__(self, buffer, landed, used):
        self.buffer, self.landed, self.used = buffer, landed, used
        self.units = []
        self.next = 0

    def add(self, key, source, k, n):
        self.units.append((key, source, k, n))

    def view(self, n, k, m):
        return self.buffer[:, n % RING, 0:k * m].rearrange("p (k m) -> p k m", k=k)

    def take(self, pe, key):
        n = self.next
        self.next += 1
        want, _, k, m = self.units[n]
        assert want == key, (want, key)
        pe.wait_ge(self.landed[n % RING], 16 * (n // RING + 1))
        return self.view(n, k, m)


def columns(w, c0, n):
    return w[:, c0:c0 + n].rearrange("(k p) n -> p k n", p=P)


def build_program(nc, A, out):
    with ExitStack() as ctx:
        def sb(name, shape, dt=F32):
            return ctx.enter_context(nc.sbuf_tensor(name, shape, dt))

        def sem(name):
            return ctx.enter_context(nc.semaphore(name))

        consts = sb("consts", [P, CONSTANTS.shape[1]])
        ring_buffer = sb("ring_buffer", [P, RING, UNIT])
        x = sb("x", [P, TT, D])
        xn = sb("xn", [P, TT, D])
        hT = sb("hT", [P, KD, S])
        arena = sb("arena", [P, 17 * 1024])
        cols = sb("cols", [P, 256])
        mod = sb("mod", [P, 6, KD])
        gain = sb("gain", [P, 2, KD])
        gates = sb("gates", [P, 2, D])
        small = sb("small", [P, 64])
        ps = ctx.enter_context(nc.psum_tensor("ps", [P, 8, 512], F32))

        def const(name, rows=P):
            at, n = CONSTANT_AT[name]
            return consts[0:rows, at:at + n]

        ident, ones = const("ident"), const("ones")
        col_at, n = {}, 0
        for name, rows in VECTORS:
            if name == "norm_g_2":
                n = P
            col_at[name] = n
            n += rows

        def col(name, i, n=1):
            return cols[:, col_at[name] + i:col_at[name] + i + n]

        def carve():
            at = [0]

            def take(*shape, dt=F32):
                n = int(np.prod(shape))
                v = arena[:, at[0]:at[0] + n]
                at[0] += n
                assert at[0] <= 17 * 1024, at
                if dt is not F32:
                    v = v.bitcast(dt)
                names = "abcd"[:len(shape)]
                return v.rearrange(f"p ({' '.join(names)}) -> p {' '.join(names)}",
                                   **dict(zip(names, shape))) if len(shape) > 1 else v
            return take

        weights_landed = [sem(f"weights_landed{i}") for i in range(RING)]
        weights_used = sem("weights_used")
        stage_done = sem("stage_done")
        dve_step = sem("dve_step")
        ring = WeightRing(ring_buffer, weights_landed, weights_used)
        chain = {}
        uses = {"norm": 0, "turned norm": 0, "normed residual": 0}
        programs = {"pe": [], "act": [], "dve": [], "pool": []}
        stream = []

        def stage(pe=None, act=None, dve=None, pool=None):
            for name, f in (("pe", pe), ("act", act), ("dve", dve), ("pool", pool)):
                programs[name].append(f)

        def run_stages(name, eng):
            for n, f in enumerate(programs[name]):
                if n:
                    eng.wait_ge(stage_done, 4 * n)
                if f is not None:
                    f(eng)
                eng.drain().then_inc(stage_done, 1)

        def release(pe):
            pe.drain().then_inc(weights_used, 1)

        def stream_units(first, last):
            def f(sp):
                for n in range(first, last):
                    _, source, k, m = ring.units[n]
                    if n >= RING:
                        sp.wait_ge(weights_used, n - RING + 1)
                    sp.dma_start(ring.view(n, k, m), source).then_inc(weights_landed[n % RING], 16)
            return f

        loaded = sem("loaded")
        rows_turned, cols_ready = sem("rows_turned"), sem("cols_ready")
        rows_cleared = sem("rows_cleared")
        take = carve()
        vector_rows = take(2, P)
        n_loads = 2 + len(VECTORS)

        def start_act(act):
            act.wait_ge(rows_cleared, 1)
            act.dma_start(consts[:, :], A["consts"]).then_inc(loaded, 16)
            act.dma_start(x[:, :, :], A["x"][0].rearrange("(t p) d -> p t d", p=P)).then_inc(loaded, 16)
            for name, rows in VECTORS:
                a = A[name]
                flat = a.rearrange(" ".join("abcd"[:len(a.shape)]) + " -> (" + " ".join("abcd"[:len(a.shape)]) + ")")
                at = col_at[name]
                act.dma_start(vector_rows[at % P:at % P + rows, at // P, :],
                              flat.rearrange("(r n) -> r n", n=P)).then_inc(loaded, 16)
            act.wait_ge(cols_ready, 1)
            act.activation(col("c", 0, 8), col("c", 0, 8), ACT.Silu)

        def start_pe(pe):
            pe.wait_ge(loaded, 16 * n_loads)
            for j in range(2):
                pe.transpose(ps[:, 0, j * P:(j + 1) * P], vector_rows[:, j, :], ident).then_inc(rows_turned, 1)

        def start_dve(dve):
            v = chain["dve"]
            dve.memset(vector_rows[:, :, :], 0.0).then_inc(rows_cleared, 1)
            dve.wait_ge(rows_turned, 2)
            dve.tensor_copy(cols[:, :], ps[:, 0, 0:2 * P]).then_inc(cols_ready, 1)

        stage(start_pe, start_act, start_dve)

        conditioning_signals = [sem(f"cond_{n}") for n in ("row_ready", "row_taken", "cols_turned", "c_ready", "bias_loaded")]

        def conditioning(layer):
            n0 = len(ring.units)
            for c in range(12):
                ring.add(("ada", layer, c), columns(A["ada_w"][layer], 512 * c, 512), KD, 512)
            stream.append(stream_units(n0, len(ring.units)))
            row_ready, row_taken, cols_turned, c_ready, bias_loaded = conditioning_signals
            chunks0, turns0 = 12 * layer, 8 * layer
            take = carve()
            c_wide = take(KD, P)
            bias_rows = take(512)
            rows = take(2, 512)

            def turn(pe, c, m):
                pe.wait_ge(row_taken, chunks0 + c + 1)
                for j in range(4):
                    ins = pe.matmul(ps[:, 4, 4 * m + j:4 * m + j + 1], rows[:, m % 2, j * P:(j + 1) * P],
                                    ident[:, 0:1], start=True, stop=True)
                ins.then_inc(cols_turned, 1)

            def act_(act):
                act.dma_start(bias_rows[0:12, :], A["ada_b"][layer].rearrange("(c n) -> c n", n=512)).then_inc(bias_loaded, 16)

            def pe_(pe):
                m = 0
                pe.wait_ge(c_ready, layer + 1)
                pe.wait_ge(bias_loaded, 16 * (layer + 1))
                for c in range(12):
                    w = ring.take(pe, ("ada", layer, c))
                    if c >= 2:
                        pe.wait_ge(row_taken, chunks0 + c - 1)
                    bank = ps[:, c % 2, :]
                    for k in range(KD):
                        ins = pe.matmul(bank, c_wide[:, k, :], w[:, k, :], start=(k == 0), stop=False)
                    ins.then_inc(weights_used, 1)
                    pe.matmul(bank, ident[0:12, c:c + 1].to_broadcast([12, P]), bias_rows[0:12, :],
                              start=False, stop=True).then_inc(row_ready, 1)
                    if c >= 1 and (c - 1) % 6 < 4:
                        turn(pe, c - 1, m)
                        m += 1

            def dve_(dve):
                v = chain["dve"]
                m = 0
                for k in range(KD):
                    ins = dve.tensor_scalar(c_wide[:, k, :], ones, col("c", k), None, ALU.mult)
                ins.then_inc(c_ready, 1)
                for c in range(12):
                    dve.wait_ge(row_ready, chunks0 + c + 1)
                    if c % 6 < 4:
                        if m >= 2:
                            dve.wait_ge(cols_turned, turns0 + m - 1)
                        dve.tensor_copy(rows[:, m % 2, :], ps[:, c % 2, :]).then_inc(row_taken, 1)
                        m += 1
                    else:
                        g = gates[:, c // 6, :]
                        dve.tensor_copy(g[:, (c % 2) * 512:(c % 2 + 1) * 512], ps[:, c % 2, :]).then_inc(row_taken, 1)
                dve.wait_ge(cols_turned, turns0 + 8)
                for j, (i, source) in enumerate(((0, 0), (1, 8), (3, 16), (4, 24))):
                    ins = dve.tensor_copy(mod[:, i, :], ps[:, 4, source:source + 8])
                v(ins)
                for j, name in enumerate(("norm_mix_g", "norm_ffn_g")):
                    dve.scalar_tensor_tensor(out=gain[:, j, :], in0=mod[:, 3 * j + 1, :], scalar=1.0,
                                             in1=col(name, 8 * layer, 8), op0=ALU.add, op1=ALU.mult)

            stage(pe_, act_, dve_)

        norm_signals = [sem(f"norm_{n}") for n in ("summed", "meaned", "rooted", "scaled", "turned")]

        def norm( scale_cols, shift_cols=None, turn=True):
            summed, meaned, rooted, scaled, turned = norm_signals
            u, turns = uses["norm"], uses["turned norm"]
            uses["norm"] += 1
            uses["turned norm"] += turn
            ssq, ms, rt, rstd = small[:, 0:2], small[:, 2:4], small[:, 4:6], small[:, 6:8]

            def act_(act):
                for t in range(TT):
                    act.activation(xn[:, t, :], x[:, t, :], ACT.Square, accum_out=ssq[:, t:t + 1]).then_inc(summed, 1)
                act.wait_ge(meaned, u + 1)
                act.activation(rt, ms, ACT.Sqrt).then_inc(rooted, 1)
                if turn:
                    for k in (2, 3, 6, 7):
                        act.wait_ge(turned, 4 * turns + k // 2 + 1)
                        o, i = hT[:, k, :], ps[:, k // 2, (k % 2) * S:(k % 2 + 1) * S]
                        act.activation(o, i, ACT.Identity, scale=scale_cols[:, k:k + 1],
                                       bias=shift_cols[:, k:k + 1] if shift_cols is not None else 0.0)

            def dve_(dve):
                v = chain["dve"]
                dve.wait_ge(summed, TT * (u + 1))
                dve.tensor_scalar(ms, ssq, 1.0 / D, EPS, ALU.mult, ALU.add).then_inc(meaned, 1)
                dve.wait_ge(rooted, u + 1)
                v(dve.reciprocal(rstd, rt))
                for t in range(TT):
                    dve.tensor_scalar(xn[:, t, :], x[:, t, :], rstd[:, t:t + 1], None, ALU.mult).then_inc(scaled, 1)
                if turn:
                    for k in (0, 1, 4, 5):
                        dve.wait_ge(turned, 4 * turns + k // 2 + 1)
                        o, i = hT[:, k, :], ps[:, k // 2, (k % 2) * S:(k % 2 + 1) * S]
                        if shift_cols is not None:
                            dve.tensor_scalar(o, i, scale_cols[:, k:k + 1], shift_cols[:, k:k + 1], ALU.mult, ALU.add)
                        else:
                            dve.tensor_scalar(o, i, scale_cols[:, k:k + 1], None, ALU.mult)

            def pe_(pe):
                if not turn:
                    return
                pe.wait_ge(scaled, TT * (u + 1))
                for k in range(KD):
                    for t in range(TT):
                        ins = pe.transpose(ps[:, k // 2, (k % 2) * S + t * P:(k % 2) * S + (t + 1) * P],
                                           xn[:, t, k * P:(k + 1) * P], ident)
                    if k % 2:
                        ins.then_inc(turned, 1)

            stage(pe_, act_, dve_)

        def attention():
            w_in, w_o = A["attn_w_in"][0], A["attn_w_o"][0]
            n0 = len(ring.units)
            for c in range(6):
                ring.add(("attn_in", c), columns(w_in, 512 * c, 512), KD, 512)
            ring.add(("attn_f",), columns(w_in, 3 * D, N_HEADS), KD, N_HEADS)
            for c in range(2):
                ring.add(("attn_out", c), columns(w_o, 512 * c, 512), KD, 512)
            stream.append(stream_units(n0, len(ring.units)))
            take = carve()
            qkT = take(16, S)
            v_tok = take(TT, D)
            oT = take(KD, S)
            probs = take(2, 2, S)
            probsT = take(2, 512)
            lf = take(TT, N_HEADS)
            F = take(TT, N_HEADS)
            t1, t2, t3 = take(TT, N_HEADS), take(TT, N_HEADS), take(TT, N_HEADS)
            fbias = take(N_HEADS)
            nFT = take(S)
            mx, top, nb, rs, ri = (take(16, 2) for _ in range(5))

            p_ready, p_taken = sem("attn_proj_ready"), sem("attn_proj_taken")
            bias_loaded = sem("attn_bias_loaded")

            def proj_pe(pe):
                for c in range(4):
                    w = ring.take(pe, ("attn_in", c))
                    for j in range(4):
                        n = 4 * c + j
                        if n >= 8:
                            pe.wait_ge(p_taken, n - 7)
                        for k in range(KD):
                            ins = pe.matmul(ps[:, n % 8, 0:S], w[:, k, j * P:(j + 1) * P], hT[:, k, :],
                                            start=(k == 0), stop=(k == KD - 1))
                        ins.then_inc(p_ready, 1)
                    release(pe)
                for c in range(4, 6):
                    w = ring.take(pe, ("attn_in", c))
                    for t in range(TT):
                        n = 16 + 2 * (c - 4) + t
                        pe.wait_ge(p_taken, n - 7)
                        for k in range(KD):
                            ins = pe.matmul(ps[:, n % 8, :], hT[:, k, t * P:(t + 1) * P], w[:, k, :],
                                            start=(k == 0), stop=(k == KD - 1))
                        ins.then_inc(p_ready, 1)
                    release(pe)
                w = ring.take(pe, ("attn_f",))
                pe.wait_ge(p_taken, 13)
                for t in range(TT):
                    for k in range(KD):
                        ins = pe.matmul(ps[:, 4, t * 16:(t + 1) * 16], hT[:, k, t * P:(t + 1) * P], w[:, k, :],
                                        start=(k == 0), stop=(k == KD - 1))
                ins.then_inc(p_ready, 1)
                release(pe)

            def take_projection(eng, n, copy):
                eng.wait_ge(p_ready, n + 1)
                if n < 16:
                    copy(qkT[:, n, :], ps[:, n % 8, 0:S]).then_inc(p_taken, 1)
                else:
                    c, t = divmod(n - 16, 2)
                    copy(v_tok[:, t, c * 512:(c + 1) * 512], ps[:, n % 8, :]).then_inc(p_taken, 1)

            def proj_dve(dve):
                v = chain["dve"]
                for n in range(20):
                    take_projection(dve, n, dve.tensor_copy)
                dve.wait_ge(p_ready, 21)
                dve.wait_ge(bias_loaded, 16)
                v(dve.tensor_tensor(t1, ps[:, 4, 0:32].rearrange("p (t h) -> p t h", t=TT),
                                    fbias.unsqueeze(1).to_broadcast([P, TT, N_HEADS]), ALU.add))
                v(dve.tensor_scalar(t2, t1, -1.0, None, ALU.mult))
                dve.tensor_tensor(t2, t1, t2, ALU.min).then_inc(p_taken, 1)

            def proj_act(act):
                act.dma_start(fbias, A["attn_f_bias"].partition_broadcast(P).rearrange("p a h -> p (a h)")).then_inc(bias_loaded, 16)

            stage(proj_pe, proj_act, proj_dve)

            a, b, c_, d = sem("attn_exp"), sem("attn_ln"), sem("attn_logf"), sem("attn_F")
            e, f = sem("attn_F_taken"), sem("attn_FT")

            def gate_act(act):
                act.activation(t3, t2, ACT.Exp).then_inc(a, 1)
                act.wait_ge(a, 1)
                act.activation(t2, t3, ACT.Ln, bias=1.0).then_inc(b, 1)

            def gate_dve(dve):
                v = chain["dve"]
                v(dve.memset(nFT, 0.0))
                dve.wait_ge(b, 1)
                v(dve.tensor_scalar(t1, t1, 0.0, None, ALU.min))
                dve.tensor_tensor(lf, t1, t2, ALU.subtract).then_inc(c_, 1)
                dve.wait_ge(d, 1)
                dve.tensor_copy(F, ps[:, 0, 0:32].rearrange("p (t h) -> p t h", t=TT)).then_inc(e, 1)
                dve.wait_ge(f, 1)
                dve.tensor_scalar(nFT[0:N_HEADS, :], ps[0:N_HEADS, 1, 0:S], -8.0, None, ALU.mult)

            def gate_pe(pe):
                pe.wait_ge(c_, 1)
                pe.matmul(ps[:, 0, 0:16], const("upto"), lf[:, 0, :], start=True, stop=True)
                pe.matmul(ps[:, 0, 16:32], ones, lf[:, 0, :], start=True, stop=False)
                pe.matmul(ps[:, 0, 16:32], const("upto"), lf[:, 1, :], start=False, stop=True).then_inc(d, 1)
                pe.wait_ge(e, 1)
                for t in range(TT):
                    ins = pe.transpose(ps[0:N_HEADS, 1, t * P:(t + 1) * P], F[:, t, :], ident)
                ins.then_inc(f, 1)

            stage(gate_pe, gate_act, gate_dve)

            scored, biased, exped, normed = sem("attn_scored"), sem("attn_biased"), sem("attn_exped"), sem("attn_normed")
            turned, copied, mixed, stored = sem("attn_turned"), sem("attn_copied"), sem("attn_mixed"), sem("attn_stored")
            N = 16

            def scores(pe, i):
                qt, pair = divmod(i, 8)
                keys = (qt + 1) * P
                if i >= 2:
                    pe.wait_ge(exped, 2 * (i - 1))
                for j in range(2):
                    rows = slice(64 * j, 64 * j + 64)
                    bank = ps[:, 2 * (i % 2) + j, :]
                    o = bank[:, 0:keys]
                    pe.matmul(o, qkT[rows, pair, qt * P:(qt + 1) * P], qkT[rows, 8 + pair, 0:keys], start=True, stop=False)
                    h = 2 * pair + j
                    pe.matmul(o, ident[:, h:h + 1].to_broadcast([P, P]), nFT[:, 0:keys], start=False, stop=False)
                    ins = pe.matmul(bank[:, qt * P:keys], ident, const("mask_ts"), start=False, stop=True)
                ins.then_inc(scored, 1)

            def weigh(pe, i):
                qt, pair = divmod(i, 8)
                pe.wait_ge(normed, i + 1)
                if i >= 2:
                    pe.wait_ge(copied, i - 1)
                for j in range(2):
                    for kt in range(qt + 1):
                        m = j * (qt + 1) + kt
                        ins = pe.transpose(ps[:, 4 + i % 2, m * P:(m + 1) * P], probs[:, i % 2, j, kt * P:(kt + 1) * P], ident)
                ins.then_inc(turned, 1)

            def mix(pe, i):
                qt, pair = divmod(i, 8)
                pe.wait_ge(copied, i + 1)
                if i >= 2:
                    pe.wait_ge(stored, i - 1)
                for j in range(2):
                    h = 2 * pair + j
                    for kt in range(qt + 1):
                        m = j * (qt + 1) + kt
                        ins = pe.matmul(ps[64 * j:64 * j + 64, 6 + i % 2, 0:P], v_tok[:, kt, h * 64:(h + 1) * 64],
                                        probsT[:, i % 2, m * P:(m + 1) * P], start=(kt == 0), stop=(kt == qt))
                ins.then_inc(mixed, 1)

            def heads_pe(pe):
                for i in range(N + 2):
                    if i < N:
                        scores(pe, i)
                    if 1 <= i <= N:
                        weigh(pe, i - 1)
                    if 2 <= i:
                        mix(pe, i - 2)

            def heads_act(act):
                for i in range(N):
                    qt, pair = divmod(i, 8)
                    keys = (qt + 1) * P
                    act.wait_ge(biased, i + 1)
                    if i >= 2:
                        act.wait_ge(turned, i - 1)
                    for j in range(2):
                        act.activation(probs[:, i % 2, j, 0:keys], ps[:, 2 * (i % 2) + j, 0:keys], ACT.Exp,
                                       scale=0.125, bias=nb[:, i, j:j + 1], accum_out=rs[:, i, j:j + 1]).then_inc(exped, 1)

            def heads_dve(dve):
                v = chain["dve"]
                for i in range(N + 2):
                    if i < N:
                        qt, pair = divmod(i, 8)
                        keys = (qt + 1) * P
                        dve.wait_ge(scored, i + 1)
                        s = ps[:, 2 * (i % 2):2 * (i % 2) + 2, 0:keys]
                        v(dve.tensor_reduce(mx[:, i, :], s, AX.X, ALU.max))
                        Fq = F[:, qt, 2 * pair:2 * pair + 2]
                        v(dve.scalar_tensor_tensor(out=top[:, i, :], in0=mx[:, i, :], scalar=0.125, in1=Fq,
                                                   op0=ALU.mult, op1=ALU.add))
                        dve.tensor_tensor(nb[:, i, :], Fq, top[:, i, :], ALU.subtract).then_inc(biased, 1)
                    if 1 <= i <= N:
                        m = i - 1
                        keys = (m // 8 + 1) * P
                        dve.wait_ge(exped, 2 * m + 2)
                        v(dve.reciprocal(ri[:, m, :], rs[:, m, :]))
                        for j in range(2):
                            ins = dve.tensor_scalar(probs[:, m % 2, j, 0:keys], probs[:, m % 2, j, 0:keys], ri[:, m, j:j + 1],
                                                    None, ALU.mult)
                        ins.then_inc(normed, 1)
                        n = 2 * keys
                        dve.wait_ge(turned, m + 1)
                        if m >= 2:
                            dve.wait_ge(mixed, m - 1)
                        dve.tensor_copy(probsT[:, m % 2, 0:n], ps[:, 4 + m % 2, 0:n]).then_inc(copied, 1)
                    if 2 <= i:
                        m = i - 2
                        qt, pair = divmod(m, 8)
                        dve.wait_ge(mixed, m + 1)
                        dve.tensor_copy(oT[:, pair, qt * P:(qt + 1) * P], ps[:, 6 + m % 2, 0:P]).then_inc(stored, 1)

            stage(heads_pe, heads_act, heads_dve)
            gated_output("attn_out", oT, gates[:, 0, :])

        def gated_output(tag, fT, gate):
            ready = sem(f"{tag}_ready")
            scratch = xn

            def pe_(pe):
                for c in range(2):
                    w = ring.take(pe, (tag, c))
                    for t in range(TT):
                        for k in range(KD):
                            ins = pe.matmul(ps[:, 2 * c + t, :], fT[:, k, t * P:(t + 1) * P], w[:, k, :],
                                            start=(k == 0), stop=(k == KD - 1))
                        ins.then_inc(ready, 1)
                    release(pe)

            def dve_(dve):
                v = chain["dve"]
                for c in range(2):
                    for t in range(TT):
                        half = slice(512 * c, 512 * c + 512)
                        dve.wait_ge(ready, 2 * c + t + 1)
                        v(dve.tensor_tensor(scratch[:, t, half], ps[:, 2 * c + t, :], gate[:, half], ALU.mult))
                        dve.tensor_tensor(x[:, t, half], x[:, t, half], scratch[:, t, half], ALU.add)

            stage(pe_, None, dve_)

        route_signals = [sem("route_" + n) for n in (
            "router_loaded", "logits_ready", "scores_ready", "member_ready", "ranked", "table_ready")]
        pair_signals = [sem("pair_" + n) for n in (
            "picked", "weighted", "w_turned", "w_copied", "g_ready", "u_ready", "silu_done", "prod_done", "xa_ready",
            "xb_ready", "xa_taken", "xb_taken", "p_turned", "p_copied", "ya_ready", "yb_ready", "ya_taken", "yb_taken",
            "combined", "step")]

        def experts(layer):
            norm(gain[:, 1, :], mod[:, 3, :])
            G, H = gain[:, 1, :], mod[:, 3, :]
            take = carve()
            router = take(KD, N_EXPERTS)
            rbias = take(N_EXPERTS)
            scores = take(TT, N_EXPERTS)
            sel = take(TT, N_EXPERTS)
            top_in_group = take(TT, N_GROUPS, 8)
            group_score = take(TT, 8)
            top_group = take(TT, 8)
            group_at = take(TT, 8, dt=U32)
            group_f = take(TT)
            group_mask, penalty = take(TT, N_GROUPS), take(TT, N_GROUPS)
            chosen = take(TT, 8)
            chosen_at = take(TT, 8, dt=U32)
            chosen_f = take(TT, 2)
            hot = take(TT, 2, N_EXPERTS)
            junk = take(N_EXPERTS)
            raw_gate, gate = take(TT, 2), take(TT, 2)
            gate_sum, gate_inv = take(TT), take(TT)
            member = take(TT, N_EXPERTS)
            n_blocks, block_end, block_slot = take(N_EXPERTS), take(N_EXPERTS), take(N_EXPERTS)
            slot_of = take(TT, N_EXPERTS)
            dest = take(TT, 2)
            ended = take(BLOCKS, N_EXPERTS)
            block_expert = take(BLOCKS)
            table = take(2, BLOCKS, dt=I32)
            pick, pick_w, part, part2 = take(TT, P), take(TT, P), take(TT, P), take(TT, P)
            pick_wT = take(TT, P)
            xgT = take(KD, P)
            silu_g, prod = take(512), take(512)
            prodT = take(4, P)
            y = take(D)

            small_loaded, logits_ready, scores_ready, member_ready, ranked, table_ready = route_signals
            r0 = layer + 1

            def route_act(act):
                act.dma_start(router, A["router_w"].rearrange("(k p) e -> p k e", p=P)).then_inc(small_loaded, 16)
                act.dma_start(rbias, A["router_bias"].partition_broadcast(P)).then_inc(small_loaded, 16)
                act.wait_ge(logits_ready, r0)
                act.activation(scores, ps[:, 0, 0:TT * N_EXPERTS].rearrange("p (t e) -> p t e", t=TT), ACT.Sigmoid)\
                    .then_inc(scores_ready, 1)

            def route_pe(pe):
                pe.wait_ge(small_loaded, 32 * r0)
                for t in range(TT):
                    for k in range(KD):
                        ins = pe.matmul(ps[:, 0, t * 32:(t + 1) * 32], hT[:, k, t * P:(t + 1) * P], router[:, k, :],
                                        start=(k == 0), stop=(k == KD - 1))
                ins.then_inc(logits_ready, 1)
                pe.wait_ge(member_ready, r0)
                pe.matmul(ps[:, 1, 0:32], const("before"), member[:, 0, :], start=True, stop=True)
                pe.matmul(ps[:, 1, 32:64], ones, member[:, 0, :], start=True, stop=False)
                pe.matmul(ps[:, 1, 32:64], const("before"), member[:, 1, :], start=False, stop=True)
                pe.matmul(ps[:, 1, 64:96], ones, member[:, 0, :], start=True, stop=False)
                pe.matmul(ps[:, 1, 64:96], ones, member[:, 1, :], start=False, stop=True).then_inc(ranked, 1)

            def route_dve(dve):
                v = chain["dve"]
                iota_e = const("iota")[:, 0:N_EXPERTS]
                dve.wait_ge(scores_ready, r0)
                dve.wait_ge(small_loaded, 32 * r0)
                dve.memset(group_score, NEG)
                v(dve.tensor_tensor(sel, scores, rbias.unsqueeze(1).to_broadcast([P, TT, N_EXPERTS]), ALU.add))
                for t in range(TT):
                    for g in range(N_GROUPS):
                        ins = dve.max(top_in_group[:, t, g, :], sel[:, t, g * GROUP:(g + 1) * GROUP])
                v(ins)
                v(dve.tensor_tensor(group_score[:, :, 0:4], top_in_group[:, :, :, 0], top_in_group[:, :, :, 1], ALU.add))
                for t in range(TT):
                    v(dve.max(top_group[:, t, :], group_score[:, t, :]))
                    v(dve.max_index(group_at[:, t, :], top_group[:, t, :], group_score[:, t, :]))
                v(dve.tensor_copy(group_f, group_at[:, :, 0]))
                for t in range(TT):
                    ins = dve.tensor_scalar(group_mask[:, t, :], const("iota4"), group_f[:, t:t + 1], None, ALU.is_equal)
                v(ins)
                v(dve.tensor_scalar(penalty, group_mask, -NEG, NEG, ALU.mult, ALU.add))
                def by_group(a):
                    return a.rearrange("p t (g e) -> p t g e", g=N_GROUPS)
                wide = [P, TT, N_GROUPS, GROUP]
                v(dve.tensor_tensor(by_group(sel), by_group(sel), group_mask.unsqueeze(3).to_broadcast(wide), ALU.mult))
                v(dve.tensor_tensor(by_group(sel), by_group(sel), penalty.unsqueeze(3).to_broadcast(wide), ALU.add))
                for t in range(TT):
                    v(dve.max(chosen[:, t, :], sel[:, t, :]))
                    v(dve.max_index(chosen_at[:, t, :], chosen[:, t, :], sel[:, t, :]))
                v(dve.tensor_copy(chosen_f, chosen_at[:, :, 0:2]))
                for t in range(TT):
                    for i in range(2):
                        ins = dve.tensor_scalar(hot[:, t, i, :], iota_e, chosen_f[:, t, i:i + 1], None, ALU.is_equal)
                v(ins)
                dve.tensor_tensor(member, hot[:, :, 0, :], hot[:, :, 1, :], ALU.add).then_inc(member_ready, 1)
                for t in range(TT):
                    for i in range(2):
                        v(dve.tensor_tensor_reduce(junk, hot[:, t, i, :], scores[:, t, :], 1.0, 0.0, ALU.mult, ALU.add,
                                                   raw_gate[:, t, i:i + 1]))
                v(dve.tensor_tensor(gate_sum, raw_gate[:, :, 0], raw_gate[:, :, 1], ALU.add))
                v(dve.reciprocal(gate_inv, gate_sum))
                v(dve.tensor_tensor(gate, raw_gate, gate_inv.unsqueeze(2).to_broadcast([P, TT, 2]), ALU.mult))
                dve.wait_ge(ranked, r0)
                count = ps[:, 1, 64:96]
                v(dve.tensor_scalar(n_blocks, count, 0.0, None, ALU.is_gt))
                for j in range(1, S // SLOTS):
                    v(dve.scalar_tensor_tensor(out=n_blocks, in0=count, scalar=float(SLOTS * j), in1=n_blocks,
                                               op0=ALU.is_gt, op1=ALU.add))
                v(dve.tensor_tensor_scan(block_end, ones[:, 0:N_EXPERTS], n_blocks, 0.0, ALU.mult, ALU.add))
                v(dve.tensor_tensor(block_slot, block_end, n_blocks, ALU.subtract))
                for t in range(TT):
                    ins = dve.scalar_tensor_tensor(out=slot_of[:, t, :], in0=block_slot, scalar=float(SLOTS),
                                                   in1=ps[:, 1, t * 32:(t + 1) * 32], op0=ALU.mult, op1=ALU.add)
                v(ins)
                for t in range(TT):
                    for i in range(2):
                        v(dve.tensor_tensor_reduce(junk, hot[:, t, i, :], slot_of[:, t, :], 1.0, 0.0, ALU.mult, ALU.add,
                                                   dest[:, t, i:i + 1]))
                shape = [P, BLOCKS, N_EXPERTS]
                v(dve.tensor_tensor(ended, const("iota40").unsqueeze(2).to_broadcast(shape),
                                    block_end.unsqueeze(1).to_broadcast(shape), ALU.is_ge))
                v(dve.tensor_reduce(block_expert, ended, AX.X, ALU.add))
                dve.tensor_scalar(table[:, 0, :], block_expert, float(N_EXPERTS - 1), None, ALU.min)
                v(dve.tensor_scalar(table[:, 1, :], block_expert, float(N_EXPERTS), None, ALU.is_lt))
                dve.memset(y, 0.0).then_inc(table_ready, 1)

            stage(route_pe, route_act, route_dve)

            n0 = len(ring.units)
            assert n0 >= RING
            slots = [(n0 + u) % RING for u in range(RING)]
            landed_before = [16 * ((n0 + u) // RING) for u in range(RING)]
            for i in range(PAIRS):
                for u in range(RING):
                    ring.add(("moe", layer, i, u), None, KD if u < 4 else 4, 512 if u < 4 else D)

            def load_experts(sp):
                sp.wait_ge(table_ready, r0)
                with sp.Fori(0, PAIRS) as i:
                    expert = [sp.value_load(table[0:1, 0, bass.ds(2 * i + j, 1)], min_val=0, max_val=N_EXPERTS - 1)
                              for j in range(2)]
                    live = [sp.value_load(table[0:1, 1, bass.ds(2 * i + j, 1)], min_val=0, max_val=1) for j in range(2)]
                    for u in range(RING):
                        w = A[("exp_w1", "exp_w3", "exp_w2")[u // 2]][layer]
                        source = w[bass.ds(expert[u % 2], 1)].rearrange("a (k p) n -> p (a k) n", p=P)
                        sp.wait_ge(weights_used, n0 + u - RING + 1 + RING * i)
                        sp.dma_start(ring.view(slots[u], *ring.units[n0 + u][2:]), source, cond=(live[u % 2] > 0))\
                            .then_inc(weights_landed[slots[u]], 16)
            stream.append(load_experts)

            (picked, weighted, w_turned, w_copied, g_ready, u_ready, silu_done, prod_done, xa_ready, xb_ready, xa_taken,
             xb_taken, p_turned, p_copied, ya_ready, yb_ready, ya_taken, yb_taken, combined, pair_step) = pair_signals
            i0 = PAIRS * layer
            j0 = (PAIRS + 1) * layer
            BXA, BXB, BG, BU = 4, 5, 6, 7

            def gather(pe, n):
                for k in range(KD):
                    for t in range(TT):
                        ins = pe.matmul(ps[:, BXA + k // 4, (k % 4) * P:(k % 4 + 1) * P], xn[:, t, k * P:(k + 1) * P],
                                        pick[:, t, :], start=(t == 0), stop=(t == TT - 1))
                        if n is not None and k == 0 and t == 0:
                            ins.then_inc(weights_used, 1)
                    if k == 3:
                        ins.then_inc(xa_ready, 1)
                ins.then_inc(xb_ready, 1)

            def pairs_pe(pe):
                for b in range(4):
                    ins = pe.matmul(ps[:, b, :], ident, y[:, 0:512], start=True, stop=False, skip_group_check=True)
                ins.then_inc(combined, 1)
                pe.wait_ge(picked, j0 + 1)
                gather(pe, None)

                def up(i, u, bank, ready):
                    ws = []
                    for j in range(2):
                        pe.wait_ge(weights_landed[slots[u + j]], landed_before[u + j] + 16 + 16 * i)
                        ws.append(ring.view(slots[u + j], KD, 512))
                    for k in range(KD):
                        for j in range(2):
                            ins = pe.matmul(ps[64 * j:64 * j + 64, bank, :], xgT[:, k, 64 * j:64 * j + 64], ws[j][:, k, :],
                                            start=(k == 0), stop=(k == KD - 1))
                            if u == 2 and k == 0 and j == 0:
                                ins.then_inc(weights_used, 1)
                            if k == KD - 1 and j == 0:
                                ins.then_inc(weights_used, 1)
                    ins.then_inc(ready, 1)

                ring.next += RING * PAIRS
                with pe.Fori(0, PAIRS) as i:
                    pe.wait_ge(weighted, j0 + i + 1)
                    pe.wait_ge(xa_taken, j0 + i + 1)
                    for t in range(TT):
                        ins = pe.transpose(ps[:, BXA, t * P:(t + 1) * P], pick_w[:, t, :], ident)
                    ins.then_inc(w_turned, 1)
                    pe.wait_ge(xb_taken, j0 + i + 1)
                    pe.wait_ge(yb_taken, j0 + i + 1)
                    up(i, 0, BG, g_ready)
                    pe.wait_ge(ya_taken, j0 + i + 1)
                    up(i, 2, BU, u_ready)
                    pe.wait_ge(w_copied, i0 + i + 1)
                    pe.wait_ge(picked, j0 + i + 2)
                    gather(pe, i)
                    pe.wait_ge(prod_done, i0 + i + 1)
                    for f in range(4):
                        ins = pe.transpose(ps[:, BG, f * P:(f + 1) * P], prod[:, f * P:(f + 1) * P], ident)
                    ins.then_inc(p_turned, 1)
                    pe.wait_ge(p_copied, i0 + i + 1)
                    ws = []
                    for j in range(2):
                        pe.wait_ge(weights_landed[slots[4 + j]], landed_before[4 + j] + 16 + 16 * i)
                        ws.append(ring.view(slots[4 + j], 4, D))
                    for half, (bank, ready) in enumerate(((BU, ya_ready), (BG, yb_ready))):
                        for f in range(4):
                            for j in range(2):
                                ins = pe.matmul(ps[64 * j:64 * j + 64, bank, :], prodT[:, f, 64 * j:64 * j + 64],
                                                ws[j][:, f, half * 512:(half + 1) * 512], start=(f == 0), stop=(f == 3))
                                if half == 1 and f == 3 and j == 0:
                                    ins.then_inc(weights_used, 1)
                        ins.then_inc(ready, 1)
                    for half, taken in enumerate((ya_taken, yb_taken)):
                        pe.wait_ge(taken, j0 + i + 2)
                        for t in range(TT):
                            ins = pe.matmul(ps[:, 2 * half + t, :], pick_wT[:, t, :], y[:, half * 512:(half + 1) * 512],
                                            start=False, stop=False, skip_group_check=True)
                            if half == 0 and t == 0:
                                ins.then_inc(weights_used, 1)
                    ins.then_inc(combined, 1)

            def taken_x(eng, i, k, on_act):
                o, src = xgT[:, k, :], ps[:, BXA + k // 4, (k % 4) * P:(k % 4 + 1) * P]
                if on_act:
                    return eng.activation(o, src, ACT.Identity, scale=G[:, k:k + 1], bias=H[:, k:k + 1])
                return eng.tensor_scalar(o, src, G[:, k:k + 1], H[:, k:k + 1], ALU.mult, ALU.add)

            def pairs_act(act):
                act.wait_ge(xb_ready, j0 + 1)
                for k in range(4, 8):
                    ins = taken_x(act, 0, k, True)
                    if k == 4:
                        ins.then_inc(ya_taken, 1)
                ins.then_inc(xb_taken, 1)
                with act.Fori(0, PAIRS) as i:
                    act.wait_ge(g_ready, i0 + i + 1)
                    act.activation(silu_g, ps[:, BG, :], ACT.Silu).then_inc(silu_done, 1)
                    act.wait_ge(xb_ready, j0 + i + 2)
                    for k in range(4, 8):
                        ins = taken_x(act, i, k, True)
                    ins.then_inc(xb_taken, 1)
                    act.wait_ge(combined, j0 + i + 1)
                    act.wait_ge(ya_ready, i0 + i + 1)
                    act.copy(y[:, 0:512], ps[:, BU, :]).then_inc(ya_taken, 1)

            def pairs_dve(dve):
                shape = [P, TT, P]
                slot = const("iota").unsqueeze(1).to_broadcast(shape)

                step0 = (4 + 5 * PAIRS) * layer

                def step(ins, count):
                    ins.then_inc(pair_step, 1)
                    dve.wait_ge(pair_step, step0 + count)

                def build(count):
                    for n, a in enumerate((part, part2)):
                        step(dve.tensor_tensor(a, slot, dest[:, :, n:n + 1].to_broadcast(shape), ALU.is_equal), count + n + 1)
                    dve.tensor_tensor(pick, part, part2, ALU.add).then_inc(picked, 1)
                    for n, a in enumerate((part, part2)):
                        step(dve.tensor_tensor(a, a, gate[:, :, n:n + 1].to_broadcast(shape), ALU.mult), count + n + 3)
                    dve.tensor_tensor(pick_w, part, part2, ALU.add).then_inc(weighted, 1)

                build(0)
                dve.wait_ge(xa_ready, j0 + 1)
                for k in range(4):
                    ins = taken_x(dve, 0, k, False)
                    if k == 0:
                        ins.then_inc(yb_taken, 1)
                ins.then_inc(xa_taken, 1)
                with dve.Fori(0, PAIRS) as i:
                    dve.wait_ge(combined, j0 + i + 1)
                    dve.wait_ge(w_turned, i0 + i + 1)
                    dve.tensor_copy(pick_wT, ps[:, BXA, 0:2 * P].rearrange("p (t c) -> p t c", t=TT)).then_inc(w_copied, 1)
                    count = 4 + 5 * i
                    step(dve.tensor_scalar(dest, dest, float(-P), None, ALU.add), count + 1)
                    dve.wait_ge(xb_ready, j0 + i + 1)
                    build(count + 1)
                    dve.wait_ge(silu_done, i0 + i + 1)
                    dve.wait_ge(u_ready, i0 + i + 1)
                    dve.tensor_tensor(prod, silu_g, ps[:, BU, :], ALU.mult).then_inc(prod_done, 1)
                    dve.wait_ge(xa_ready, j0 + i + 2)
                    for k in range(4):
                        ins = taken_x(dve, i, k, False)
                    ins.then_inc(xa_taken, 1)
                    dve.wait_ge(p_turned, i0 + i + 1)
                    dve.tensor_copy(prodT, ps[:, BG, :].rearrange("p (f c) -> p f c", f=4)).then_inc(p_copied, 1)
                    dve.wait_ge(yb_ready, i0 + i + 1)
                    dve.tensor_copy(y[:, 512:1024], ps[:, BG, :]).then_inc(yb_taken, 1)

            stage(pairs_pe, pairs_act, pairs_dve)

            def add_dve(dve):
                v = chain["dve"]
                g = gates[:, 1, :]
                for t in range(TT):
                    for half in range(2):
                        cols_ = slice(512 * half, 512 * half + 512)
                        v(dve.tensor_tensor(xn[:, t, cols_], ps[:, 2 * half + t, :], g[:, cols_], ALU.mult))
                        dve.tensor_tensor(x[:, t, cols_], x[:, t, cols_], xn[:, t, cols_], ALU.add)
            stage(None, None, add_dve)

        def pooling():
            ring.add(("pool_w",), A["pool_w"][0].rearrange("g (k p) e -> p (g k) e", p=P), KD, 256)
            stream.append(stream_units(len(ring.units) - 1, len(ring.units)))
            take = carve()
            PAD = 16
            sums = [take(2, PAD + S) for _ in range(2)]
            pooledT = take(KD, S)
            row_scale = take(D)
            scale_loaded, pooled, y_ready = sem("pool_scale_loaded"), sem("pool_pooled"), sem("pool_y_ready")

            def act_(act):
                act.dma_start(row_scale, A["pool_scale"][0].partition_broadcast(P)).then_inc(scale_loaded, 16)

            def pe_(pe):
                w = ring.take(pe, ("pool_w",))
                for g in range(4):
                    pe.wait_ge(pooled, g + 1)
                    for t in range(TT):
                        for k in range(2):
                            ins = pe.matmul(ps[:, 4 * (g % 2) + 2 * t + g // 2, 0:256], pooledT[:, 2 * g + k, t * P:(t + 1) * P],
                                            w[:, 2 * g + k, :], start=(k == 0), stop=(k == 1))
                    ins.then_inc(y_ready, 1)
                release(pe)

            def dve_(dve):
                v = chain["dve"]
                for s in sums:
                    dve.memset(s[:, :, 0:PAD], 0.0)
                for g, window in enumerate(WINDOWS):
                    h = hT[:, 2 * g:2 * g + 2, :]
                    v(dve.tensor_copy(sums[0][:, :, PAD:], h))
                    step, at = 1, 0
                    while step < window:
                        v(dve.tensor_tensor(sums[1 - at][:, :, PAD:], sums[at][:, :, PAD:],
                                            sums[at][:, :, PAD - step:PAD + S - step], ALU.add))
                        step, at = 2 * step, 1 - at
                    inverse = const("inverse_count")[:, g * S:(g + 1) * S]
                    v(dve.tensor_tensor(sums[at][:, :, PAD:], sums[at][:, :, PAD:],
                                        inverse.unsqueeze(1).to_broadcast([P, 2, S]), ALU.mult))
                    dve.tensor_tensor(pooledT[:, 2 * g:2 * g + 2, :], sums[at][:, :, PAD:], h, ALU.subtract).then_inc(pooled, 1)
                    dve.wait_ge(pooled, g + 1)
                dve.wait_ge(scale_loaded, 16)
                v(dve.tensor_tensor(row_scale, row_scale, gates[:, 0, :], ALU.mult))
                dve.wait_ge(y_ready, 4)
                for g in range(4):
                    for t in range(TT):
                        cols_ = slice(256 * g, 256 * g + 256)
                        v(dve.tensor_tensor(xn[:, t, cols_], ps[:, 4 * (g % 2) + 2 * t + g // 2, 0:256],
                                            row_scale[:, cols_], ALU.mult))
                        dve.tensor_tensor(x[:, t, cols_], x[:, t, cols_], xn[:, t, cols_], ALU.add)

            stage(pe_, act_, dve_)

        def final_norm():
            norm(None, turn=False)
            row_gain = carve()(D)
            loaded_g = sem("final_gain_loaded")

            def act_(act):
                act.dma_start(row_gain, A["norm_final_g"].partition_broadcast(P)).then_inc(loaded_g, 16)

            def dve_(dve):
                dve.wait_ge(loaded_g, 16)
                for t in range(TT):
                    dve.tensor_tensor(x[:, t, :], xn[:, t, :], row_gain, ALU.mult)

            stage(None, act_, dve_)

        residual_signals = [sem(f"residual_{n}") for n in ("gain_loaded", "summed", "meaned", "rooted")]

        def normed_residual(ready, ready0, gain_row):
            gain_loaded, summed, meaned, rooted = residual_signals
            u = uses["normed residual"]
            uses["normed residual"] += 1
            ssq, ms, rt, rstd = small[:, 8:12], small[:, 12:14], small[:, 14:16], small[:, 16:18]
            row_gain = hT[:, 0:4, :].rearrange("p k s -> p (k s)")

            def act_(act):
                act.wait_ge(ready, ready0 + 4)
                act.dma_start(row_gain, gain_row.partition_broadcast(P)).then_inc(gain_loaded, 16)
                for half in range(2):
                    for t in range(TT):
                        act.activation(xn[:, t, 512 * half:512 * half + 512], ps[:, 2 * half + t, :], ACT.Square,
                                       accum_out=ssq[:, 2 * half + t:2 * half + t + 1]).then_inc(summed, 1)
                act.wait_ge(meaned, u + 1)
                act.activation(rt, ms, ACT.Sqrt).then_inc(rooted, 1)

            def dve_(dve):
                v = chain["dve"]
                dve.wait_ge(summed, 4 * (u + 1))
                v(dve.tensor_tensor(ms, ssq[:, 0:2], ssq[:, 2:4], ALU.add))
                dve.tensor_scalar(ms, ms, 1.0 / D, EPS, ALU.mult, ALU.add).then_inc(meaned, 1)
                dve.wait_ge(rooted, u + 1)
                v(dve.reciprocal(rstd, rt))
                dve.wait_ge(gain_loaded, 16 * (u + 1))
                for half in range(2):
                    for t in range(TT):
                        cols_ = slice(512 * half, 512 * half + 512)
                        v(dve.scalar_tensor_tensor(out=xn[:, t, cols_], in0=ps[:, 2 * half + t, :], scalar=rstd[:, t:t + 1],
                                                   in1=row_gain[:, cols_], op0=ALU.mult, op1=ALU.mult))
                        dve.tensor_tensor(x[:, t, cols_], x[:, t, cols_], xn[:, t, cols_], ALU.add)
            return act_, dve_

        def project_out(tag, fT, gain_row):
            ready = sem(f"{tag}_ready")

            def pe_(pe):
                for c in range(2):
                    w = ring.take(pe, (tag, c))
                    for t in range(TT):
                        for k in range(KD):
                            ins = pe.matmul(ps[:, 2 * c + t, :], fT[:, k, t * P:(t + 1) * P], w[:, k, :],
                                            start=(k == 0), stop=(k == KD - 1))
                        ins.then_inc(ready, 1)
                    release(pe)
            act_, dve_ = normed_residual(ready, 0, gain_row)
            stage(pe_, act_, dve_)

        ffn_signals = [sem(f"ffn_{n}") for n in ("up_ready", "silu_done", "act_ready", "ready")]

        def feed_forward(layer):
            norm(col("norm_g_2", 32 * layer + 16, 8))
            w1, w3, w2 = A["ffn_w1_2"][layer], A["ffn_w3_2"][layer], A["ffn_w2_2"][layer]
            FT = F_FF // P
            chunks = [(c, min(512, F_FF - c)) for c in range(0, F_FF, 512)]
            rows = [(r, min(4, FT - r)) for r in range(0, FT, 4)]
            n0 = len(ring.units)
            for c, n in chunks:
                ring.add(("w1", c), columns(w1, c, n), KD, n)
                ring.add(("w3", c), columns(w3, c, n), KD, n)
            for r, n in rows:
                ring.add(("w2", r), w2[r * P:(r + n) * P, :].rearrange("(k p) n -> p k n", p=P), n, D)
            stream.append(stream_units(n0, len(ring.units)))
            take = carve()
            aT = take(FT, S)
            silu = take(2, S)
            up_ready, silu_done, act_ready, ready = ffn_signals
            f0 = FT * layer

            def pe_(pe):
                f = 0
                for c, n in chunks:
                    a = ring.take(pe, ("w1", c))
                    b = ring.take(pe, ("w3", c))
                    for j in range(n // P):
                        if f >= 8:
                            pe.wait_ge(act_ready, f0 + f - 7)
                        for i, w in enumerate((a, b)):
                            for k in range(KD):
                                ins = pe.matmul(ps[:, f % 8, i * S:(i + 1) * S], w[:, k, j * P:(j + 1) * P], hT[:, k, :],
                                                start=(k == 0), stop=(k == KD - 1))
                        ins.then_inc(up_ready, 1)
                        f += 1
                    pe.drain().then_inc(weights_used, 2)
                pe.wait_ge(act_ready, f0 + FT)
                for r, n in rows:
                    w = ring.take(pe, ("w2", r))
                    for k in range(n):
                        for half in range(2):
                            for t in range(TT):
                                ins = pe.matmul(ps[:, 2 * half + t, :], aT[:, r + k, t * P:(t + 1) * P],
                                                w[:, k, 512 * half:512 * half + 512], start=(r + k == 0), stop=(r + k == FT - 1))
                                if r + k == FT - 1:
                                    ins.then_inc(ready, 1)
                    release(pe)

            act_after, dve_after = normed_residual(ready, 4 * layer, A["norm_g_2"][layer, 3])

            def act_(act):
                for f in range(FT):
                    act.wait_ge(up_ready, f0 + f + 1)
                    if f >= 2:
                        act.wait_ge(act_ready, f0 + f - 1)
                    act.activation(silu[:, f % 2, :], ps[:, f % 8, 0:S], ACT.Silu).then_inc(silu_done, 1)
                act_after(act)

            def dve_(dve):
                for f in range(FT):
                    dve.wait_ge(silu_done, f0 + f + 1)
                    dve.tensor_tensor(aT[:, f, :], silu[:, f % 2, :], ps[:, f % 8, S:2 * S], ALU.mult).then_inc(act_ready, 1)
                dve_after(dve)

            stage(pe_, act_, dve_)
        def log_sigmoid_act(act, tag, negative_abs, e, out):
            step = sem(tag)
            act.activation(e, negative_abs, ACT.Exp).then_inc(step, 1)
            act.wait_ge(step, 1)
            return act.activation(out, e, ACT.Ln, bias=1.0)

        def mixer_ab():
            norm(col("norm_g_2", 0, 8))
            n0 = len(ring.units)
            for c in range(3):
                ring.add(("ab_in", c), columns(A["ab_w_in_2"][0], 512 * c, 512), KD, 512)
            ring.add(("glu",), A["ab_w_glu_2"][0].rearrange("(k p) n -> p k n", p=P), 4, 512)
            for c in range(2):
                ring.add(("ab_out", c), columns(A["ab_w_out_2"][0], 512 * c, 512), KD, 512)
            stream.append(stream_units(n0, len(ring.units)))
            take = carve()
            usT = take(4, S)
            after_us = carve()
            after_us(4, S)
            PAD = M_CONV - 1
            xm = take(4, PAD + S + 1)
            szT = take(4, S)
            xcT = take(4, S)
            conv = take(4, S)
            qkvT = take(12, S)
            v_ext = take(TT, M_HEADS, M_DIM + 1)
            h_tok = take(TT, M_HEADS, M_DIM)
            quad_w = take(3, 4, 4)
            spread = take(3, 4, P)
            w_if = take(12, 8)
            b_if = take(8)
            mixT = hT

            loads, proj_ready, xm_taken = (sem("ab_" + n) for n in ("loads", "proj_ready", "xm_taken"))

            def proj_pe(pe):
                for c in range(3):
                    w = ring.take(pe, ("ab_in", c))
                    for j in range(4):
                        n = 4 * c + j
                        if n >= 8:
                            pe.wait_ge(xm_taken, n - 7)
                        for k in range(KD):
                            ins = pe.matmul(ps[:, n % 8, 0:S], w[:, k, j * P:(j + 1) * P], hT[:, k, :],
                                            start=(k == 0), stop=(k == KD - 1))
                        ins.then_inc(proj_ready, 1)
                    release(pe)

            def proj_act(act):
                for n, name in enumerate(("ab_wq_2", "ab_wk_2", "ab_wv_2")):
                    act.dma_start(quad_w[:, n, :, :], A[name][0].rearrange("(c n) d e -> (n d) c e", c=4)).then_inc(loads, 16)
                act.dma_start(w_if, A["ab_w_if_2"][0].rearrange("(k p) n -> p k n", p=P)).then_inc(loads, 16)
                act.dma_start(b_if, A["ab_b_if_2"][0].partition_broadcast(P)).then_inc(loads, 16)
                for n in range(4, 8):
                    act.wait_ge(proj_ready, n + 1)
                    act.activation(szT[:, n - 4, :], ps[:, n, 0:S], ACT.Silu)

            def proj_dve(dve):
                v = chain["dve"]
                dve.memset(xm[:, :, 0:PAD], 0.0)
                v(dve.memset(v_ext[:, :, :, M_DIM:M_DIM + 1], 1.0))
                for n in range(4):
                    dve.wait_ge(proj_ready, n + 1)
                    dve.tensor_copy(xm[:, n, PAD:PAD + S], ps[:, n, 0:S]).then_inc(xm_taken, 1)
                dve.wait_ge(xm_taken, 4)
                for n in range(4):
                    v(dve.tensor_scalar(conv[:, n, :], xm[:, n, 0:S], col("ab_conv_w_2", n), col("ab_conv_b_2", n),
                                        ALU.mult, ALU.add))
                    for j in range(1, M_CONV):
                        v(dve.scalar_tensor_tensor(out=conv[:, n, :], in0=xm[:, n, j:j + S], scalar=col("ab_conv_w_2", 4 * j + n),
                                                   in1=conv[:, n, :], op0=ALU.mult, op1=ALU.add))
                for n in range(8, 12):
                    dve.wait_ge(proj_ready, n + 1)
                    dve.tensor_copy(usT[:, n - 8, :], ps[:, n % 8, 0:S])
                dve.wait_ge(loads, 80)
                for n in range(3):
                    shape = [P, 4, 32, 4]
                    dve.tensor_tensor(spread[:, n, :, :].rearrange("p c (n e) -> p c n e", e=4),
                                      const("quads").rearrange("p (a n) -> p a n", a=1).rearrange("p a (n e) -> p a n e", e=4).to_broadcast(shape),
                                      quad_w[:, n, :, :].unsqueeze(2).to_broadcast(shape), ALU.mult)

            stage(proj_pe, proj_act, proj_dve)

            conv_done, qkv_ready, v_ready, taken_q, taken_v, gates_ready = (
                sem("ab_" + n) for n in ("conv_done", "qkv_ready", "v_ready", "qkv_taken", "v_taken", "gates_ready"))
            pre = small[:, 20:36].rearrange("p (t n) -> p t n", t=TT)

            def qkv_act(act):
                act.activation(xcT, conv, ACT.Silu).then_inc(conv_done, 1)

            def qkv_pe(pe):
                pe.wait_ge(conv_done, 1)
                for n in range(12):
                    which, c = divmod(n, 4)
                    if n >= 6:
                        pe.wait_ge(taken_q, n - 5)
                    source = xcT[:, c, :] if which < 2 else xm[:, c, PAD:PAD + S]
                    pe.matmul(ps[:, n % 6, 0:S], spread[:, which, c, :], source, start=True, stop=True).then_inc(qkv_ready, 1)
                for c in range(4):
                    for t in range(TT):
                        ins = pe.matmul(ps[:, 6 + t, c * P:(c + 1) * P], xm[:, c, PAD + t * P:PAD + (t + 1) * P],
                                        spread[:, 2, c, :], start=True, stop=True)
                ins.then_inc(v_ready, 1)
                pe.wait_ge(taken_q, 12)
                for t in range(TT):
                    for n in range(12):
                        ins = pe.matmul(ps[:, 0, 8 * t:8 * t + 8], qkvT[:, n, t * P:(t + 1) * P], w_if[:, n, :],
                                        start=(n == 0), stop=(n == 11))
                ins.then_inc(gates_ready, 1)

            def qkv_dve(dve):
                v = chain["dve"]
                for n in range(12):
                    dve.wait_ge(qkv_ready, n + 1)
                    dve.tensor_scalar(qkvT[:, n, :], ps[:, n % 6, 0:S], M_DIM ** -0.5 if 4 <= n < 8 else 1.0, None,
                                      ALU.mult).then_inc(taken_q, 1)
                dve.wait_ge(v_ready, 1)
                for t in range(TT):
                    dve.tensor_copy(v_ext[:, t, :, 0:M_DIM], ps[:, 6 + t, :].rearrange("p (h d) -> p h d", h=4))
                dve.wait_ge(gates_ready, 1)
                dve.tensor_tensor(pre, ps[:, 0, 0:16].rearrange("p (t n) -> p t n", t=TT),
                                  b_if.unsqueeze(1).to_broadcast([P, TT, 8]), ALU.add)

            stage(qkv_pe, qkv_act, qkv_dve)

            t1, t2, t3, b_tok, a_tok, m_tok = (take(TT, 4) for _ in range(6))
            a_rows, m_rows = take(S), take(S)
            abs_ready, ln_ready, lf_ready, b_ready, a_ready, aT_ready, m_ready, mT_ready, em_ready = (
                sem("ab_" + n) for n in ("abs_ready", "ln_ready", "lf_ready", "b_ready", "a_ready", "aT_ready", "m_ready",
                                         "mT_ready", "em_ready"))

            def gate_act(act):
                act.wait_ge(abs_ready, 1)
                log_sigmoid_act(act, "ab_exp_ready", t2, t3, t2).then_inc(ln_ready, 1)
                act.wait_ge(em_ready, 1)
                act.activation(m_tok, t1, ACT.Exp, scale=-1.0)

            def gate_dve(dve):
                v = chain["dve"]
                f = pre[:, :, 4:8]
                v(dve.memset(m_rows, 0.0))
                v(dve.tensor_scalar(t2, f, -1.0, None, ALU.mult))
                dve.tensor_tensor(t2, f, t2, ALU.min).then_inc(abs_ready, 1)
                v(dve.tensor_scalar(t1, f, 0.0, None, ALU.min))
                dve.wait_ge(ln_ready, 1)
                dve.tensor_tensor(t1, t1, t2, ALU.subtract).then_inc(lf_ready, 1)
                dve.wait_ge(b_ready, 1)
                v(dve.tensor_copy(b_tok, ps[:, 0, 0:8].rearrange("p (t h) -> p t h", t=TT)))
                dve.tensor_tensor(a_tok, pre[:, :, 0:4], b_tok, ALU.subtract).then_inc(a_ready, 1)
                dve.wait_ge(aT_ready, 1)
                v(dve.tensor_copy(a_rows[0:4, :], ps[0:4, 1, 0:S]))
                v(dve.tensor_tensor_scan(m_rows[0:4, :], CONST_ONES_ROW(4), a_rows[0:4, :], 0.0, ALU.mult, ALU.max))
                dve.tensor_scalar(m_rows[0:4, :], m_rows[0:4, :], -1.0, None, ALU.mult).then_inc(m_ready, 1)
                dve.wait_ge(mT_ready, 1)
                dve.tensor_tensor(t1, b_tok, ps[:, 2, 0:2 * P].rearrange("p (t h) -> p t h", t=TT)[:, :, 0:4],
                                  ALU.subtract).then_inc(em_ready, 1)

            def gate_pe(pe):
                pe.wait_ge(lf_ready, 1)
                pe.matmul(ps[:, 0, 0:4], const("upto"), t1[:, 0, :], start=True, stop=True)
                pe.matmul(ps[:, 0, 4:8], ones, t1[:, 0, :], start=True, stop=False)
                pe.matmul(ps[:, 0, 4:8], const("upto"), t1[:, 1, :], start=False, stop=True).then_inc(b_ready, 1)
                pe.wait_ge(a_ready, 1)
                for t in range(TT):
                    ins = pe.transpose(ps[0:4, 1, t * P:(t + 1) * P], a_tok[:, t, :], ident)
                ins.then_inc(aT_ready, 1)
                pe.wait_ge(m_ready, 1)
                for t in range(TT):
                    ins = pe.transpose(ps[:, 2, t * P:(t + 1) * P], m_rows[:, t * P:(t + 1) * P], ident)
                ins.then_inc(mT_ready, 1)

            def CONST_ONES_ROW(n):
                return ones[0:n, 0:1].to_broadcast([n, S])

            stage(gate_pe, gate_act, gate_dve)

            W = 3 * P
            expd = xn[:, 0, 0:2 * W].rearrange("p (b w) -> p b w", b=2)
            weight = xn[:, 1, 0:2 * W].rearrange("p (b w) -> p b w", b=2)
            den = small[:, 36:52].rearrange("p (h t b) -> p h t b", h=4, t=2)
            qk_ready, ex_ready, w_ready, num_ready, num_taken = (
                sem("ab_" + n) for n in ("qk_ready", "ex_ready", "w_ready", "num_ready", "num_taken"))

            def heads_pe(pe):
                def scores(h):
                    if h >= 2:
                        pe.wait_ge(w_ready, h - 1)
                    qk, lg = ps[:, 2 * (h % 2), :], ps[:, 2 * (h % 2) + 1, :]
                    q, k = qkvT[:, h, :], qkvT[:, 4 + h, :]
                    pe.matmul(qk[:, 0:S], k[:, 0:P], q, start=True, stop=True)
                    pe.matmul(qk[:, S:W], k[:, P:S], q[:, P:S], start=True, stop=True)
                    head = ident[:, h:h + 1].to_broadcast([P, P])
                    pe.matmul(lg[:, 0:S], head, m_rows, start=True, stop=False)
                    pe.matmul(lg[:, 0:P], ident, const("mask_st"), start=False, stop=True)
                    pe.matmul(lg[:, S:W], head, m_rows[:, P:S], start=True, stop=False)
                    pe.matmul(lg[:, S:W], ident, const("mask_st"), start=False, stop=True).then_inc(qk_ready, 1)

                def mix(h):
                    pe.wait_ge(w_ready, h + 1)
                    if h >= 2:
                        pe.wait_ge(num_taken, h - 1)
                    o, w = ps[:, 4 + h % 2, :], weight[:, h % 2, :]
                    n = M_DIM + 1
                    pe.matmul(o[:, 0:n], w[:, 0:P], v_ext[:, 0, h, :], start=True, stop=True)
                    pe.matmul(o[:, 256:256 + n], w[:, P:S], v_ext[:, 0, h, :], start=True, stop=False)
                    pe.matmul(o[:, 256:256 + n], w[:, S:W], v_ext[:, 1, h, :], start=False, stop=True).then_inc(num_ready, 1)
                scores(0)
                for h in range(4):
                    if h < 3:
                        scores(h + 1)
                    mix(h)

            def heads_act(act):
                for h in range(4):
                    act.wait_ge(qk_ready, h + 1)
                    if h >= 2:
                        act.wait_ge(w_ready, h - 1)
                    lg = ps[:, 2 * (h % 2) + 1, :]
                    act.activation(expd[:, h % 2, 0:S], lg[:, 0:S], ACT.Exp, bias=a_tok[:, 0, h:h + 1])
                    act.activation(expd[:, h % 2, S:W], lg[:, S:W], ACT.Exp, bias=a_tok[:, 1, h:h + 1]).then_inc(ex_ready, 1)

            def heads_dve(dve):
                v = chain["dve"]

                def finish(h):
                    dve.wait_ge(num_ready, h + 1)
                    o = ps[:, 4 + h % 2, :].rearrange("p (t n) -> p t n", t=TT)
                    d, r = den[:, h, :, 0], den[:, h, :, 1]
                    v(dve.tensor_copy(r, o[:, :, M_DIM]))
                    v(dve.scalar_tensor_tensor(out=d, in0=r, scalar=-1.0, in1=r, op0=ALU.mult, op1=ALU.max))
                    v(dve.tensor_tensor(d, d, m_tok[:, :, h], ALU.max))
                    v(dve.reciprocal(r, d))
                    for t in range(TT):
                        ins = dve.tensor_scalar(h_tok[:, t, h, :], o[:, t, 0:M_DIM], r[:, t:t + 1], None, ALU.mult)
                    ins.then_inc(num_taken, 1)
                for h in range(4):
                    dve.wait_ge(ex_ready, h + 1)
                    if h >= 2:
                        dve.wait_ge(num_ready, h - 1)
                    dve.tensor_tensor(weight[:, h % 2, :], expd[:, h % 2, :], ps[:, 2 * (h % 2), 0:W], ALU.mult).then_inc(w_ready, 1)
                    if h:
                        finish(h - 1)
                finish(3)

            stage(heads_pe, heads_act, heads_dve)

            stats = xn[:, 0, 0:48].rearrange("p (t h n) -> p t h n", t=2, h=4)
            mean_var = xn[:, 0, 64:80].rearrange("p (t h n) -> p t h n", t=2, h=4)
            sd = xn[:, 0, 96:104].rearrange("p (t h) -> p t h", t=2)
            rstd = xn[:, 0, 112:120].rearrange("p (t h) -> p t h", t=2)
            var_ready, sd_ready, hn_ready, hnT_ready = (sem("ab_" + n) for n in ("var_ready", "sd_ready", "hn_ready", "hnT_ready"))

            def ln_dve(dve):
                v = chain["dve"]
                for t in range(TT):
                    for h in range(4):
                        v(dve.bn_stats(stats[:, t, h, :], h_tok[:, t, h, :]))
                        v(dve.bn_aggr(mean_var[:, t, h, :], stats[:, t, h, :]))
                dve.tensor_scalar(sd, mean_var[:, :, :, 1], EPS, None, ALU.add).then_inc(var_ready, 1)
                dve.wait_ge(sd_ready, 1)
                v(dve.reciprocal(rstd, sd))
                for t in range(TT):
                    for h in range(4):
                        dve.tensor_scalar(h_tok[:, t, h, :], h_tok[:, t, h, :], mean_var[:, t, h, 0:1], rstd[:, t, h:h + 1],
                                          ALU.subtract, ALU.mult).then_inc(hn_ready, 1)
                for h in range(4):
                    ins = dve.tensor_scalar(conv[:, h, :], xcT[:, h, :], col("ab_skip_2", h), None, ALU.mult)
                v(ins)
                dve.wait_ge(hnT_ready, 1)
                for h in range(4):
                    v(dve.scalar_tensor_tensor(out=conv[:, h, :], in0=ps[:, h, 0:S], scalar=col("ab_mh_gain_2", h),
                                               in1=conv[:, h, :], op0=ALU.mult, op1=ALU.add))
                    dve.tensor_tensor(mixT[:, h, :], conv[:, h, :], szT[:, h, :], ALU.mult)

            def ln_act(act):
                act.wait_ge(var_ready, 1)
                act.activation(sd, sd, ACT.Sqrt).then_inc(sd_ready, 1)

            def ln_pe(pe):
                pe.wait_ge(hn_ready, 8)
                for h in range(4):
                    for t in range(TT):
                        ins = pe.transpose(ps[:, h, t * P:(t + 1) * P], h_tok[:, t, h, :], ident)
                ins.then_inc(hnT_ready, 1)

            stage(ln_pe, ln_act, ln_dve)

            take = after_us
            cosT, sinT = take(S_PAIRS, S), take(S_PAIRS, S)
            half_tmp = take(S_PAIRS, P)
            BT = take(2, 4, P)
            CT = take(2, 4, P)
            par = take(5, P)
            pc = take(5, S_PAIRS)
            turn_c, turn_s, turn_t = take(S_PAIRS), take(S_PAIRS), take(S_PAIRS)
            yT = xn[:, 1, :].rearrange("p (k s) -> p k s", k=4)
            r16 = xn[:, 0, :].rearrange("p (n c) -> p n c", n=8)
            b_in = cosT[:, 0:2, :].rearrange("p a (g n) -> p a g n", n=S_GROUP)
            bb = cosT[:, 2:4, :].rearrange("p a (g n) -> p a g n", n=S_GROUP)
            b_tmp = cosT[:, 4, :].rearrange("p (g n) -> p g n", n=S_GROUP)
            b_wide = cosT[:, 6:10, :].rearrange("p (a b) s -> p a (b s)", a=2)
            c_in = cosT[:, 10:12, :].rearrange("p a (g n) -> p a g n", n=S_STATE)
            c_wide = sinT[:, 0:4, :].rearrange("p (a b) s -> p a (b s)", a=2)
            (s5_loaded, dt_ready, args_ready, sc_ready, par_ready, par_turned, wide_ready, wide_turned) = (
                sem("s5_" + n) for n in ("loaded", "dt_ready", "args_ready", "sc_ready", "par_ready", "par_turned",
                                         "wide_ready", "wide_turned"))
            R = S_PAIRS
            a_re, a_im, ldt, dt, x1, x2, x3, x4 = (r16[0:R, n, :] for n in range(8))
            rowp = [par[0:R, n, :] for n in range(5)]

            def s5_act(act):
                act.dma_start(a_re, A["ab_a_re_2"][0].rearrange("(r g) n -> r (g n)", g=2)).then_inc(s5_loaded, 16)
                act.dma_start(a_im, A["ab_a_im_2"][0].rearrange("(r g) n -> r (g n)", g=2)).then_inc(s5_loaded, 16)
                act.dma_start(ldt[:, 0:2], A["ab_log_dt_2"][0].rearrange("(r g) -> r g", g=2)).then_inc(s5_loaded, 16)
                for n, name in enumerate(("ab_b_re_2", "ab_b_im_2")):
                    act.dma_start(b_in[:, n, :, :], A[name][0].rearrange("(r g) n p -> (g n) r p", g=2)).then_inc(s5_loaded, 16)
                for n, name in enumerate(("ab_c_re_2", "ab_c_im_2")):
                    act.dma_start(c_in[:, n, :, :], A[name][0].rearrange("(c g) p n -> (g p) c n", c=4)).then_inc(s5_loaded, 16)
                act.wait_ge(s5_loaded, 112)
                act.activation(ldt[:, 2:4], ldt[:, 0:2], ACT.Exp).then_inc(dt_ready, 1)
                act.wait_ge(args_ready, 1)
                act.activation(rowp[0], x1, ACT.Exp)
                act.activation(rowp[2], x2, ACT.Sin)
                act.activation(rowp[1], x3, ACT.Sin).then_inc(sc_ready, 1)

            TWO_PI = 2 * np.pi
            C1 = 6.28125
            C2 = float(np.float32(np.round((TWO_PI - C1) * 2 ** 20) / 2 ** 20))
            C3 = float(np.float32(TWO_PI - C1 - C2))
            ROUND = 1.5 * 2 ** 23
            PI_DOWN = 3.1415925

            def s5_dve(dve):
                v = chain["dve"]
                v(dve.memset(par, 0.0))
                dve.wait_ge(dt_ready, 1)
                v(dve.tensor_copy(dt.rearrange("p (g n) -> p g n", g=2), ldt[:, 2:4].unsqueeze(2).to_broadcast([R, 2, S_STATE])))
                v(dve.tensor_tensor(x1, a_re, dt, ALU.mult))
                v(dve.tensor_tensor(x2, a_im, dt, ALU.mult))
                v(dve.tensor_scalar(x3, x2, 1.0 / TWO_PI, None, ALU.mult))
                v(dve.tensor_scalar(x3, x3, ROUND, None, ALU.add))
                v(dve.tensor_scalar(x3, x3, -ROUND, None, ALU.add))
                for c in (C1, C2, C3):
                    v(dve.scalar_tensor_tensor(out=x2, in0=x3, scalar=-c, in1=x2, op0=ALU.mult, op1=ALU.add))
                v(dve.tensor_scalar(x2, x2, PI_DOWN, -PI_DOWN, ALU.min, ALU.max))
                v(dve.scalar_tensor_tensor(out=x3, in0=x2, scalar=-1.0, in1=x2, op0=ALU.mult, op1=ALU.max))
                dve.tensor_scalar(x3, x3, -1.0, float(np.pi / 2), ALU.mult, ALU.add).then_inc(args_ready, 1)
                dve.wait_ge(sc_ready, 1)
                v(dve.tensor_tensor(x1, rowp[0], rowp[1], ALU.mult))
                v(dve.tensor_scalar(x1, x1, -1.0, None, ALU.add))
                v(dve.tensor_tensor(x2, rowp[0], rowp[2], ALU.mult))
                v(dve.tensor_tensor(x3, a_re, a_re, ALU.mult))
                v(dve.tensor_tensor(x4, a_im, a_im, ALU.mult))
                v(dve.tensor_tensor(x3, x3, x4, ALU.add))
                v(dve.reciprocal(dt, x3))
                v(dve.tensor_tensor(x3, x1, a_re, ALU.mult))
                v(dve.tensor_tensor(x4, x2, a_im, ALU.mult))
                v(dve.tensor_tensor(x3, x3, x4, ALU.add))
                v(dve.tensor_tensor(rowp[3], x3, dt, ALU.mult))
                v(dve.tensor_tensor(x3, x2, a_re, ALU.mult))
                v(dve.tensor_tensor(x4, x1, a_im, ALU.mult))
                v(dve.tensor_tensor(x3, x3, x4, ALU.subtract))
                dve.tensor_tensor(rowp[4], x3, dt, ALU.mult).then_inc(par_ready, 1)
                dve.wait_ge(par_turned, 1)
                v(dve.tensor_copy(pc[:, 0:4, :], ps[:, 0, :].rearrange("p (n c) -> p n c", n=4)[:, :, 0:R]))
                v(dve.tensor_copy(pc[:, 4, :], ps[:, 1, 0:R]))
                shape = [P, R, S_GROUP]
                g_re, g_im = (pc[:, n, :].unsqueeze(2).to_broadcast(shape) for n in (3, 4))
                v(dve.tensor_tensor(bb[:, 0], b_in[:, 0], g_re, ALU.mult))
                v(dve.tensor_tensor(b_tmp, b_in[:, 1], g_im, ALU.mult))
                v(dve.tensor_tensor(bb[:, 0], bb[:, 0], b_tmp, ALU.subtract))
                v(dve.tensor_tensor(bb[:, 1], b_in[:, 1], g_re, ALU.mult))
                v(dve.tensor_tensor(b_tmp, b_in[:, 0], g_im, ALU.mult))
                v(dve.tensor_tensor(bb[:, 1], bb[:, 1], b_tmp, ALU.add))
                for n in range(2):
                    wide = b_wide[:, n, :].rearrange("p (r g c) -> p r g c", r=R, g=2)
                    for g in range(2):
                        v(dve.tensor_scalar(wide[:, :, g, :], bb[:, n], const("half")[:, g:g + 1], None, ALU.mult))
                    wide = c_wide[:, n, :].rearrange("p (c g n) -> p c g n", c=4, g=2)
                    for g in range(2):
                        ins = dve.tensor_scalar(wide[:, :, g, :], c_in[:, n], const("odd16")[:, g:g + 1], 1.0 - 2.0 * n,
                                                ALU.mult, ALU.mult)
                        if n or g:
                            pass
                        v(ins) if not (n and g) else ins.then_inc(wide_ready, 1)
                dve.wait_ge(wide_turned, 1)
                for n in range(2):
                    dve.tensor_copy(BT[:, n], ps[:, 2 + n, :].rearrange("p (c n) -> p c n", c=4))
                    ins = dve.tensor_copy(CT[:, n], ps[:, 4 + n, :].rearrange("p (c n) -> p c n", c=4))
                v(ins)
                v(dve.memset(cosT[:, :, 0:1], 1.0))
                v(dve.memset(sinT[:, :, 0:1], 0.0))
                v(dve.tensor_copy(turn_c, pc[:, 1, :]))
                v(dve.tensor_copy(turn_s, pc[:, 2, :]))
                m = 1
                while m < S:
                    shape = [P, R, m]
                    c, s = (a.unsqueeze(2).to_broadcast(shape) for a in (turn_c, turn_s))
                    co, si, tmp = cosT[:, :, 0:m], sinT[:, :, 0:m], half_tmp[:, :, 0:m]
                    v(dve.tensor_tensor(tmp, si, s, ALU.mult))
                    v(dve.tensor_tensor(cosT[:, :, m:2 * m], co, c, ALU.mult))
                    v(dve.tensor_tensor(cosT[:, :, m:2 * m], cosT[:, :, m:2 * m], tmp, ALU.subtract))
                    v(dve.tensor_tensor(tmp, co, s, ALU.mult))
                    v(dve.tensor_tensor(sinT[:, :, m:2 * m], si, c, ALU.mult))
                    v(dve.tensor_tensor(sinT[:, :, m:2 * m], sinT[:, :, m:2 * m], tmp, ALU.add))
                    m *= 2
                    if m < S:
                        v(dve.tensor_tensor(turn_t, turn_s, turn_c, ALU.mult))
                        v(dve.tensor_tensor(turn_c, turn_c, turn_c, ALU.mult))
                        v(dve.tensor_tensor(turn_s, turn_s, turn_s, ALU.mult))
                        v(dve.tensor_tensor(turn_c, turn_c, turn_s, ALU.subtract))
                        v(dve.tensor_scalar(turn_s, turn_t, 2.0, None, ALU.mult))

            def s5_pe(pe):
                pe.wait_ge(par_ready, 1)
                for n in range(5):
                    ins = pe.transpose(ps[:, n // 4, (n % 4) * P:(n % 4 + 1) * P], par[:, n, :], ident)
                ins.then_inc(par_turned, 1)
                pe.wait_ge(wide_ready, 1)
                for n in range(2):
                    for c in range(4):
                        pe.transpose(ps[:, 2 + n, c * P:(c + 1) * P], b_wide[:, n, c * P:(c + 1) * P], ident)
                        ins = pe.transpose(ps[:, 4 + n, c * P:(c + 1) * P], c_wide[:, n, c * P:(c + 1) * P], ident)
                ins.then_inc(wide_turned, 1)

            stage(s5_pe, s5_act, s5_dve)

            take = after_us
            z = half_tmp.rearrange("p (a q) s -> p a (q s)", a=2).rearrange("p a (q s) -> p a q s", q=4)
            bu_ready, bu_taken, x_ready, y_ready, g_in, g_done = (
                sem("s5_" + n) for n in ("bu_ready", "bu_taken", "x_ready", "y_ready", "gelu_in", "gelu_done"))
            t_re, t_im = (xn[:, 0, 0:4 * S].rearrange("p (q s) -> p q s", q=4), arena_tail(4, S))
            y_in = gates[:, 0, 0:2 * S].rearrange("p (b s) -> p b s", b=2)

            def quarter_pe(pe):
                def states(c):
                    if c:
                        pe.wait_ge(bu_taken, c)
                    for q in range(4):
                        rows = slice(32 * q, 32 * q + 32)
                        for n in range(2):
                            ins = pe.matmul(ps[:, q, n * S:(n + 1) * S], BT[rows, n, c, :], usT[rows, c, :], start=True, stop=True)
                    ins.then_inc(bu_ready, 1)

                def outputs(c):
                    pe.wait_ge(x_ready, c + 1)
                    if c >= 2:
                        pe.wait_ge(g_in, c - 1)
                    for q in range(4):
                        o = ps[32 * q:32 * q + 32, 4 + c % 2, 0:S]
                        pe.matmul(o, CT[:, 0, c, 32 * q:32 * q + 32], z[:, 0, q, :], start=True, stop=False)
                        ins = pe.matmul(o, CT[:, 1, c, 32 * q:32 * q + 32], z[:, 1, q, :], start=False, stop=True)
                    ins.then_inc(y_ready, 1)
                states(0)
                for c in range(4):
                    if c < 3:
                        states(c + 1)
                    outputs(c)

            def quarter_dve(dve):
                v = chain["dve"]
                for c in range(4):
                    co, si = cosT[:, 4 * c:4 * c + 4, :], sinT[:, 4 * c:4 * c + 4, :]
                    re, im = ps[:, 0:4, 0:S], ps[:, 0:4, S:2 * S]
                    if c:
                        dve.wait_ge(y_ready, c)
                    dve.wait_ge(bu_ready, c + 1)
                    dve.tensor_tensor(z[:, 0], re, co, ALU.mult)
                    dve.tensor_tensor(z[:, 1], im, co, ALU.mult)
                    dve.tensor_tensor(t_re, im, si, ALU.mult)
                    dve.tensor_tensor(t_im, re, si, ALU.mult).then_inc(bu_taken, 1)
                    dve.wait_ge(bu_taken, c + 1)
                    dve.tensor_tensor(z[:, 0], z[:, 0], t_re, ALU.add)
                    v(dve.tensor_tensor(z[:, 1], z[:, 1], t_im, ALU.subtract))
                    for q in range(4):
                        decay = pc[:, 0, 4 * c + q:4 * c + q + 1].to_broadcast([P, S])
                        dve.tensor_tensor_scan(t_re[:, q, :], decay, z[:, 0, q, :], 0.0, ALU.mult, ALU.add)
                        ins = dve.tensor_tensor_scan(t_im[:, q, :], decay, z[:, 1, q, :], 0.0, ALU.mult, ALU.add)
                    v(ins)
                    dve.tensor_tensor(z[:, 0], t_re, co, ALU.mult)
                    v(dve.tensor_tensor(z[:, 1], t_im, co, ALU.mult))
                    v(dve.tensor_tensor(t_re, t_re, si, ALU.mult))
                    v(dve.tensor_tensor(t_im, t_im, si, ALU.mult))
                    v(dve.tensor_tensor(z[:, 0], z[:, 0], t_im, ALU.subtract))
                    dve.tensor_tensor(z[:, 1], z[:, 1], t_re, ALU.add).then_inc(x_ready, 1)
                    dve.wait_ge(y_ready, c + 1)
                    if c >= 2:
                        dve.wait_ge(g_done, c - 1)
                    dve.scalar_tensor_tensor(out=y_in[:, c % 2, :], in0=usT[:, c, :], scalar=col("ab_d_2", c),
                                             in1=ps[:, 4 + c % 2, 0:S], op0=ALU.mult, op1=ALU.add).then_inc(g_in, 1)

            def quarter_act(act):
                for c in range(4):
                    act.wait_ge(g_in, c + 1)
                    act.activation(yT[:, c, :], y_in[:, c % 2, :], ACT.Gelu_apprx_tanh).then_inc(g_done, 1)

            stage(quarter_pe, quarter_act, quarter_dve)

            glu_ready, sig_ready = sem("glu_ready"), sem("glu_sig_ready")
            sig = xn[:, 0, :].rearrange("p (k s) -> p k s", k=4)

            def glu_pe(pe):
                w = ring.take(pe, ("glu",))
                for n in range(4):
                    for k in range(4):
                        ins = pe.matmul(ps[:, n, 0:S], w[:, k, n * P:(n + 1) * P], yT[:, k, :], start=(k == 0), stop=(k == 3))
                    ins.then_inc(glu_ready, 1)
                release(pe)

            def glu_act(act):
                for n in range(4):
                    act.wait_ge(glu_ready, n + 1)
                    act.activation(sig[:, n, :], ps[:, n, 0:S], ACT.Sigmoid, bias=col("ab_b_glu_2", n)).then_inc(sig_ready, 1)

            def glu_dve(dve):
                for n in range(4):
                    dve.wait_ge(sig_ready, n + 1)
                    dve.tensor_tensor(mixT[:, 4 + n, :], yT[:, n, :], sig[:, n, :], ALU.mult)

            stage(glu_pe, glu_act, glu_dve)
            project_out("ab_out", mixT, A["norm_g_2"][0, 1])

        def arena_tail(*shape):
            n = int(np.prod(shape))
            return arena[:, 17 * 1024 - n:17 * 1024].rearrange("p (a b) -> p a b", a=shape[0])

        def mixer_c():
            norm(col("norm_g_2", 32, 8))
            n0 = len(ring.units)
            for c in range(8):
                ring.add(("c_in", c), columns(A["c_w_in_2"][0], 512 * c, 512), KD, 512)
            for c in range(2):
                ring.add(("c_out", c), columns(A["c_w_out_2"][0], 512 * c, 512), KD, 512)
            stream.append(stream_units(n0, len(ring.units)))
            take = carve()
            qT, kT, v_tok, gT, b = (take(8, S), take(8, S), take(TT, D), take(8, S), take(8, S))
            e_in, e_state, e_intra = (take(8, S) for _ in range(3))
            lb, lb1, p0, p1, pm = (take(8) for _ in range(5))
            b_last, decay = take(8, 4), take(8, 4)
            ready, taken_a, taken_d, lb_in, lb_exp = (sem("c_" + n) for n in ("proj_ready", "taken_act", "taken_dve", "lb_in", "lb_exp"))
            tiles = [("q", n) for n in range(8)] + [("f", n) for n in range(8)] + \
                    [("i", n) for n in range(4)] + [("g", n) for n in range(8)]
            by_act = [n for n, (kind, _) in enumerate(tiles) if kind != "i"]
            by_dve = [n for n, (kind, _) in enumerate(tiles) if kind == "i"]

            def wait_bank(pe, n):
                if n >= 8:
                    m = n - 8
                    if m in by_act:
                        pe.wait_ge(taken_a, by_act.index(m) + 1)
                    else:
                        pe.wait_ge(taken_d, by_dve.index(m) + 1)

            def proj_pe(pe):
                n = 0
                for c in range(8):
                    w = ring.take(pe, ("c_in", c))
                    if c in (4, 5):
                        for t in range(TT):
                            wait_bank(pe, n)
                            for k in range(KD):
                                ins = pe.matmul(ps[:, n % 8, :], hT[:, k, t * P:(t + 1) * P], w[:, k, :],
                                                start=(k == 0), stop=(k == KD - 1))
                            ins.then_inc(ready, 1)
                            n += 1
                    else:
                        for j in range(4):
                            wait_bank(pe, n)
                            for k in range(KD):
                                ins = pe.matmul(ps[:, n % 8, 0:S], w[:, k, j * P:(j + 1) * P], hT[:, k, :],
                                                start=(k == 0), stop=(k == KD - 1))
                            ins.then_inc(ready, 1)
                            n += 1
                    release(pe)

            def proj_act(act):
                act.wait_ge(lb_in, 1)
                act.activation(p0, p0, ACT.Exp)
                act.activation(p1, p1, ACT.Exp).then_inc(lb_exp, 1)
                for n in by_act:
                    kind, i = tiles[n]
                    act.wait_ge(ready, n + 1)
                    o, f = {"q": (qT, ACT.Silu), "f": (kT, ACT.Sigmoid), "g": (gT, ACT.Silu)}[kind]
                    act.activation(o[:, i, :], ps[:, n % 8, 0:S], f).then_inc(taken_a, 1)

            def proj_dve(dve):
                v = chain["dve"]
                r0, r1 = col("c_lb_raw_2", 0, 8), col("c_lb_raw_2", 8, 8)
                v(dve.tensor_tensor(pm, r0, r1, ALU.max))
                v(dve.tensor_tensor(p0, r0, pm, ALU.subtract))
                dve.tensor_tensor(p1, r1, pm, ALU.subtract).then_inc(lb_in, 1)
                dve.wait_ge(lb_exp, 1)
                v(dve.tensor_tensor(pm, p0, p1, ALU.add))
                v(dve.reciprocal(pm, pm))
                v(dve.tensor_tensor(p0, p0, pm, ALU.mult))
                v(dve.tensor_tensor(p1, p1, pm, ALU.mult))
                v(dve.tensor_tensor(lb, p0, p1, ALU.add))
                v(dve.tensor_tensor(lb, lb, p0, ALU.subtract))
                v(dve.tensor_scalar(lb1, lb, -1.0, 1.0, ALU.mult, ALU.add))
                dve.wait_ge(taken_a, 16)
                for h in range(8):
                    ins = dve.tensor_scalar(b[:, h, :], kT[:, h, :], lb1[:, h:h + 1], lb[:, h:h + 1], ALU.mult, ALU.add)
                v(ins)
                v(dve.tensor_scalar(kT, b, -1.0, 1.0, ALU.mult, ALU.add))
                for n in by_dve:
                    _, i = tiles[n]
                    dve.wait_ge(ready, n + 1)
                    c, t = divmod(i, 2)
                    dve.tensor_copy(v_tok[:, t, c * 512:(c + 1) * 512], ps[:, n % 8, :]).then_inc(taken_d, 1)
                dve.wait_ge(taken_a, 24)
                for h in range(8):
                    dve.tensor_scalar(gT[:, h, :], gT[:, h, :], col("c_g_gain_2", h), None, ALU.mult)

            stage(proj_pe, proj_act, proj_dve)

            log_ready, b_ready, e_ready, d_ready = (sem("c_" + n) for n in ("log_ready", "b_ready", "e_ready", "d_ready"))
            chunks = "p h (c s) -> p h c s"

            def decay_act(act):
                for h in range(8):
                    act.activation(e_in[:, h, :], b[:, h, :], ACT.Ln).then_inc(log_ready, 1)
                act.wait_ge(b_ready, 1)
                act.activation(e_in, b, ACT.Exp)
                act.activation(decay, b_last, ACT.Exp).then_inc(e_ready, 1)
                act.wait_ge(d_ready, 1)
                act.activation(e_state, b, ACT.Exp, scale=-1.0).then_inc(e_ready, 1)
                act.activation(e_intra, b, ACT.Exp).then_inc(e_ready, 1)

            def decay_dve(dve):
                v = chain["dve"]
                for h in range(8):
                    dve.wait_ge(log_ready, h + 1)
                    ins = dve.tensor_tensor_scan(b[:, h, :], const("restart"), e_in[:, h, :], 0.0, ALU.mult, ALU.add)
                v(ins)
                wide = b.rearrange(chunks, c=4)
                dve.tensor_copy(b_last, wide[:, :, :, H_CHUNK - 1]).then_inc(b_ready, 1)
                dve.wait_ge(e_ready, 1)
                for h in range(8):
                    ins = dve.tensor_tensor(wide[:, h], wide[:, h], b_last[:, h, :].unsqueeze(2).to_broadcast([P, 4, H_CHUNK]),
                                            ALU.subtract)
                ins.then_inc(d_ready, 1)
                dve.tensor_tensor(e_in, e_in, qT, ALU.mult)
                dve.wait_ge(e_ready, 2)
                dve.tensor_tensor(e_state, e_state, kT, ALU.mult)
                dve.wait_ge(e_ready, 3)
                v(dve.tensor_tensor(e_intra, e_intra, qT, ALU.mult))
                dve.memset(b, 0.0)

            stage(None, decay_act, decay_dve)

            flat = b.rearrange("p h s -> p (h s)")
            sc = flat[:, 0:512].rearrange("p (b t c) -> p b t c", b=2, t=TT)
            state = flat[:, 512:512 + 768].rearrange("p (b n c) -> p b n c", b=2, n=3)
            k_tok = flat[:, 1280:1280 + 512].rearrange("p (b t c) -> p b t c", b=2, t=TT)
            ssq = small[:, 0:16].rearrange("p (t h) -> p t h", t=TT)
            mask = const("bits_chunk").bitcast(U32)
            k_ready, k_taken, s_ready, s_taken, u_ready, states, o_ready, o_summed, o_taken = (
                sem("c_" + n) for n in ("k_ready", "k_taken", "s_ready", "s_taken", "u_ready", "states", "o_ready", "o_summed",
                                        "o_taken"))

            def heads_pe(pe):
                def first(h):
                    if h >= 2:
                        pe.wait_ge(k_taken, h - 1)
                        pe.wait_ge(s_taken, h - 1)
                    for t in range(TT):
                        ins = pe.transpose(ps[:, h % 2, t * P:(t + 1) * P], e_state[:, h, t * P:(t + 1) * P], ident)
                    ins.then_inc(k_ready, 1)
                    for t in range(TT):
                        cols_ = slice(t * P, t * P + P)
                        ins = pe.matmul(ps[:, 2 + h % 2, cols_], e_state[:, h, cols_], e_intra[:, h, cols_], start=True, stop=True)
                    ins.then_inc(s_ready, 1)

                def second(h):
                    head = slice(h * P, (h + 1) * P)
                    pe.wait_ge(k_taken, h + 1)
                    if h:
                        pe.wait_ge(states, h)
                    for c, (bank, at) in enumerate(((4, 0), (5, 0), (4, P))):
                        rows = slice(64 * (c % 2), 64 * (c % 2) + 64)
                        ins = pe.matmul(ps[:, bank, at:at + P], k_tok[rows, h % 2, c // 2, :], v_tok[rows, c // 2, head],
                                        start=True, stop=True)
                    ins.then_inc(u_ready, 1)
                    pe.wait_ge(s_taken, h + 1)
                    if h >= 2:
                        pe.wait_ge(o_taken, h - 1)
                    pe.wait_ge(states, h + 1)
                    for t in range(TT):
                        o = ps[:, 6 + h % 2, t * P:(t + 1) * P]
                        pe.matmul(o, sc[:, h % 2, t, :], v_tok[:, t, head], start=True, stop=False, skip_group_check=True)
                        for c in range(2 * t, 2 * t + 2):
                            if c:
                                r = 64 * (c % 2)
                                ins = pe.matmul(ps[r:r + 64, 6 + h % 2, t * P:(t + 1) * P], e_in[:, h, c * 64:(c + 1) * 64],
                                                state[:, h % 2, c - 1, :], start=False, stop=True, skip_group_check=True)
                    ins.then_inc(o_ready, 1)

                first(0)
                for h in range(8):
                    if h < 7:
                        first(h + 1)
                    second(h)

            def heads_act(act):
                for h in range(8):
                    act.wait_ge(k_ready, h + 1)
                    if h >= 2:
                        act.wait_ge(u_ready, h - 1)
                    act.copy(k_tok[:, h % 2], ps[:, h % 2, 0:S].rearrange("p (t c) -> p t c", t=TT)).then_inc(k_taken, 1)
                    if h:
                        square(act, h - 1)
                square(act, 7)

            def square(act, h):
                act.wait_ge(o_ready, h + 1)
                if h:
                    act.wait_ge(o_summed, h)
                for t in range(TT):
                    ins = act.activation(flat[:, 1792 + t * P:1792 + (t + 1) * P], ps[:, 6 + h % 2, t * P:(t + 1) * P], ACT.Square,
                                         accum_out=ssq[:, t, h:h + 1])
                ins.then_inc(o_summed, 1)

            def heads_dve(dve):
                v = chain["dve"]

                def finish(h):
                    dve.wait_ge(o_summed, h + 1)
                    dve.tensor_copy(xn[:, :, h * P:(h + 1) * P], ps[:, 6 + h % 2, 0:S].rearrange("p (t c) -> p t c", t=TT))\
                        .then_inc(o_taken, 1)
                for h in range(8):
                    dve.wait_ge(s_ready, h + 1)
                    if h >= 2:
                        dve.wait_ge(o_ready, h - 1)
                    for t in range(TT):
                        ins = dve.copy_predicated(sc[:, h % 2, t, :], mask, ps[:, 2 + h % 2, t * P:(t + 1) * P])
                    ins.then_inc(s_taken, 1)
                    dve.wait_ge(u_ready, h + 1)
                    st = state[:, h % 2]
                    v(dve.tensor_copy(st[:, 0, :], ps[:, 4, 0:P]))
                    v(dve.scalar_tensor_tensor(out=st[:, 1, :], in0=st[:, 0, :], scalar=decay[:, h, 1:2], in1=ps[:, 5, 0:P],
                                               op0=ALU.mult, op1=ALU.add))
                    dve.scalar_tensor_tensor(out=st[:, 2, :], in0=st[:, 1, :], scalar=decay[:, h, 2:3], in1=ps[:, 4, P:2 * P],
                                             op0=ALU.mult, op1=ALU.add).then_inc(states, 1)
                    if h:
                        finish(h - 1)
                finish(7)

            stage(heads_pe, heads_act, heads_dve)

            ms = small[:, 16:32].rearrange("p (t h) -> p t h", t=TT)
            rstd = small[:, 32:48].rearrange("p (t h) -> p t h", t=TT)
            ms_ready, rt_ready, o_scaled, oT_ready = (sem("c_" + n) for n in ("ms_ready", "rt_ready", "o_scaled", "oT_ready"))

            def out_dve(dve):
                v = chain["dve"]
                dve.tensor_scalar(ms, ssq, 1.0 / P, EPS, ALU.mult, ALU.add).then_inc(ms_ready, 1)
                dve.wait_ge(rt_ready, 1)
                v(dve.reciprocal(rstd, ms))
                for t in range(TT):
                    o = xn[:, t, :].rearrange("p (h c) -> p h c", h=8)
                    dve.tensor_tensor(o, o, rstd[:, t, :].unsqueeze(2).to_broadcast([P, 8, P]), ALU.mult).then_inc(o_scaled, 1)
                for bank in range(4):
                    dve.wait_ge(oT_ready, bank + 1)
                    dve.tensor_tensor(hT[:, 2 * bank:2 * bank + 2, :], ps[:, bank, :].rearrange("p (k s) -> p k s", k=2),
                                      gT[:, 2 * bank:2 * bank + 2, :], ALU.mult)

            def out_act(act):
                act.wait_ge(ms_ready, 1)
                act.activation(ms, ms, ACT.Sqrt).then_inc(rt_ready, 1)

            def out_pe(pe):
                pe.wait_ge(o_scaled, 2)
                for k in range(KD):
                    for t in range(TT):
                        ins = pe.transpose(ps[:, k // 2, (k % 2) * S + t * P:(k % 2) * S + (t + 1) * P],
                                           xn[:, t, k * P:(k + 1) * P], ident)
                    if k % 2:
                        ins.then_inc(oT_ready, 1)

            stage(out_pe, out_act, out_dve)
            project_out("c_out", hT, A["norm_g_2"][1, 1])

        for name in STAGES:
            if name == "layer0":
                conditioning(0)
                norm(gain[:, 0, :], mod[:, 0, :])
                attention()
            elif name == "moe0":
                experts(0)
            elif name == "layer1":
                conditioning(1)
                norm(gain[:, 0, :], mod[:, 0, :])
                pooling()
            elif name == "moe1":
                experts(1)
            elif name == "final":
                final_norm()
            elif name == "mixer_ab":
                mixer_ab()
            elif name == "ffn0":
                feed_forward(0)
            elif name == "mixer_c":
                mixer_c()
            elif name == "ffn1":
                feed_forward(1)

        out_written = sem("out_written")
        n_stages = len(programs["pe"])
        block = ctx.enter_context(nc.Block())

        @block.sync
        def _(sp):
            for step in stream:
                step(sp)
            sp.wait_ge(stage_done, 4 * n_stages)
            sp.dma_start(out[0].rearrange("(t p) d -> p t d", p=P), x[:, :, :]).then_inc(out_written, 16)
            sp.wait_ge(out_written, 16)

        @block.tensor
        def _(pe):
            run_stages("pe", pe)

        @block.scalar
        def _(act):
            run_stages("act", act)

        @block.vector
        def _(dve):
            chain["dve"] = Chain(dve, dve_step)
            run_stages("dve", dve)

        @block.gpsimd
        def _(pool):
            run_stages("pool", pool)


STAGES = ["layer0", "moe0", "layer1", "moe1", "final", "mixer_ab", "ffn0", "mixer_c", "ffn1"]
INPUTS = [
    "x", "c", "norm_mix_g", "norm_ffn_g", "ada_w", "ada_b", "attn_w_in", "attn_f_bias", "attn_w_o", "pool_w",
    "pool_scale", "router_w", "router_bias", "exp_w1", "exp_w3", "exp_w2", "norm_final_g", "norm_g_2",
    "ab_w_in_2", "ab_conv_w_2", "ab_conv_b_2", "ab_wq_2", "ab_wk_2", "ab_wv_2", "ab_w_if_2", "ab_b_if_2",
    "ab_mh_gain_2", "ab_skip_2", "ab_a_re_2", "ab_a_im_2", "ab_log_dt_2", "ab_b_re_2", "ab_b_im_2",
    "ab_c_re_2", "ab_c_im_2", "ab_d_2", "ab_w_glu_2", "ab_b_glu_2", "ab_w_out_2", "c_w_in_2", "c_lb_raw_2",
    "c_g_gain_2", "c_w_out_2", "ffn_w1_2", "ffn_w3_2", "ffn_w2_2",
]


def kernel(**inputs):
    import concourse.bacc as bacc
    from concourse.bass_utils import run_bass_kernel_spmd

    nc = bacc.Bacc("TRN2", target_bir_lowering=False, num_devices=1)
    arrays, aps = {}, {}
    for name in INPUTS:
        a = np.ascontiguousarray(inputs[name])
        arrays[f"in_{name}"] = a
        aps[name] = nc.dram_tensor(f"in_{name}", a.shape, mybir.dt.from_np(a.dtype), kind="ExternalInput").ap()
    arrays["in_consts"] = CONSTANTS
    aps["consts"] = nc.dram_tensor("in_consts", CONSTANTS.shape, mybir.dt.float32, kind="ExternalInput").ap()
    out = nc.dram_tensor("out", (1, S, D), mybir.dt.float32, kind="ExternalOutput").ap()
    build_program(nc, aps, out)
    r = run_bass_kernel_spmd(nc, [arrays], core_ids=[0])
    return r.results[0]["out"]
```

```python
from contextlib import ExitStack

import numpy as np
import concourse.bass as bass
from concourse import mybir

ALU = mybir.AluOpType
ACT = mybir.ActivationFunctionType
F32 = mybir.dt.float32
I32 = mybir.dt.int32
U32 = mybir.dt.uint32
AX = mybir.AxisListType

P = 128
D = 1024
S = 256
TT = S // P
KD = D // P
N_HEADS, HEAD_DIM = 16, 64
WINDOWS = (2, 4, 8, 16)
N_EXPERTS, N_GROUPS, D_FF = 32, 4, 512
GROUP = N_EXPERTS // N_GROUPS
SLOTS = 32
QUAD = P // SLOTS
FIRST_QUADS = N_EXPERTS // QUAD
MORE = 2 * S // SLOTS
QUADS = FIRST_QUADS + MORE // QUAD
M_WIDTH, M_HEADS, M_CONV = 512, 4, 4
M_DIM = M_WIDTH // M_HEADS
S_WIDTH, S_GROUPS, S_STATE, S_GROUP = 512, 32, 64, 16
S_PAIRS = S_GROUPS // 2
H_HEADS, H_CHUNK = 8, 64
F_FF = 2816
EPS = 1e-6
NEG = -1e30
UNIT = 4096
RING = 6


def shape_constants():
    p = np.arange(P)[:, None]
    c = np.arange(P)[None, :]
    t = np.arange(S)
    parts = {
        "ident": np.eye(P),
        "chunk_rows": np.arange(P)[:, None] % (P // 4) == np.arange(12),
        "ones": np.ones((P, P)),
        "upto": (p <= c),
        "before": (p < c),
        "mask_ts": np.where(c > p, NEG, 0.0),
        "mask_st": np.where(p > c, NEG, 0.0),
        "iota": np.broadcast_to(c, (P, P)),
        "inverse_count": np.broadcast_to(
            np.stack([1.0 / np.minimum(t + 1, w) for w in WINDOWS]).reshape(1, -1), (P, 4 * S)),
        "quads": (np.repeat(np.arange(32), 4)[None, :] == p // 4),
        "half": (np.arange(2)[None, :] == p // 64),
        "odd16": (np.arange(2)[None, :] == (p // 16) % 2),
        "restart": np.broadcast_to((t % H_CHUNK != 0), (P, S)),
        "bits_chunk": ((p // H_CHUNK == c // H_CHUNK) & (p <= c)),
    }
    at, where = 0, {}
    for name, a in parts.items():
        where[name] = (at, a.shape[1])
        at += a.shape[1]
    return np.concatenate([np.asarray(a, np.float32) for a in parts.values()], 1), where


CONSTANTS, CONSTANT_AT = shape_constants()

VECTORS = [
    ("norm_mix_g", 16), ("norm_ffn_g", 16), ("c", 8), ("ab_conv_w_2", 16), ("ab_conv_b_2", 4),
    ("ab_mh_gain_2", 4), ("ab_skip_2", 4), ("ab_d_2", 4), ("ab_b_glu_2", 4), ("c_g_gain_2", 8),
    ("c_lb_raw_2", 16), ("norm_g_2", 64), ("ada_b", 96),
]


class Chain:

    def __init__(self, eng, sem):
        self.eng, self.sem, self.n = eng, sem, 0

    def __call__(self, ins):
        self.n += 1
        ins.then_inc(self.sem, 1)
        self.eng.wait_ge(self.sem, self.n)
        return ins


class WeightRing:

    def __init__(self, buffer, landed, used):
        self.buffer, self.landed, self.used = buffer, landed, used
        self.units = []
        self.landed_at = []
        self.total = [0] * RING
        self.next = 0

    def add(self, key, source, k, n, loads=1):
        slot = len(self.units) % RING
        self.total[slot] += 16 * loads
        self.units.append((key, source, k, n))
        self.landed_at.append(self.total[slot])

    def view(self, n, k, m):
        return self.buffer[:, n % RING, 0:k * m].rearrange("p (k m) -> p k m", k=k)

    def take(self, pe, key):
        n = self.next
        self.next += 1
        want, _, k, m = self.units[n]
        assert want == key, (want, key)
        pe.wait_ge(self.landed[n % RING], self.landed_at[n])
        return self.view(n, k, m)


def columns(w, c0, n):
    return w[:, c0:c0 + n].rearrange("(k p) n -> p k n", p=P)


def build_program(nc, A, out):
    with ExitStack() as ctx:
        def sb(name, shape, dt=F32):
            return ctx.enter_context(nc.sbuf_tensor(name, shape, dt))

        def sem(name):
            return ctx.enter_context(nc.semaphore(name))

        consts = sb("consts", [P, CONSTANTS.shape[1]])
        ring_buffer = sb("ring_buffer", [P, RING, UNIT])
        x = sb("x", [P, TT, D])
        xn = sb("xn", [P, TT, D])
        hT = sb("hT", [P, KD, S])
        arena = sb("arena", [P, 17 * 1024])
        cols = sb("cols", [P, 3 * P])
        mod = sb("mod", [P, 2, 6, KD])
        gain = sb("gain", [P, 2, 2, KD])
        gates = sb("gates", [P, 2, D])
        small = sb("small", [P, 64])
        ps = ctx.enter_context(nc.psum_tensor("ps", [P, 8, 512], F32))

        def const(name, rows=P):
            at, n = CONSTANT_AT[name]
            return consts[0:rows, at:at + n]

        ident, ones = const("ident"), const("ones")
        col_at, n = {}, 0
        for name, rows in VECTORS:
            if n % P + rows > P:
                n += P - n % P
            col_at[name] = n
            n += rows

        def col(name, i, n=1):
            return cols[:, col_at[name] + i:col_at[name] + i + n]

        def carve():
            at = [0]

            def take(*shape, dt=F32):
                n = int(np.prod(shape))
                v = arena[:, at[0]:at[0] + n]
                at[0] += n
                assert at[0] <= 17 * 1024, at
                if dt is not F32:
                    v = v.bitcast(dt)
                names = "abcd"[:len(shape)]
                return v.rearrange(f"p ({' '.join(names)}) -> p {' '.join(names)}",
                                   **dict(zip(names, shape))) if len(shape) > 1 else v
            return take

        weights_landed = [sem(f"weights_landed{i}") for i in range(RING)]
        weights_used = sem("weights_used")
        stage_done = sem("stage_done")
        dve_step = sem("dve_step")
        ring = WeightRing(ring_buffer, weights_landed, weights_used)
        chain = {}
        uses = {"norm": 0, "turned norm": 0, "normed residual": 0}
        programs = {"pe": [], "act": [], "dve": [], "pool": []}
        stream = []

        def stage(pe=None, act=None, dve=None, pool=None):
            for name, f in (("pe", pe), ("act", act), ("dve", dve), ("pool", pool)):
                programs[name].append(f)

        def run_stages(name, eng):
            for n, f in enumerate(programs[name]):
                if n:
                    eng.wait_ge(stage_done, 4 * n)
                if f is not None:
                    f(eng)
                eng.drain().then_inc(stage_done, 1)

        def release(pe):
            pe.drain().then_inc(weights_used, 1)

        def stream_units(first, last):
            def f(sp):
                for n in range(first, last):
                    _, source, k, m = ring.units[n]
                    if n >= RING:
                        sp.wait_ge(weights_used, n - RING + 1)
                    sp.dma_start(ring.view(n, k, m), source).then_inc(weights_landed[n % RING], 16)
            return f

        loaded = sem("loaded")
        rows_turned, cols_ready = sem("rows_turned"), sem("cols_ready")
        rows_cleared = sem("rows_cleared")
        take = carve()
        vector_rows = take(3, P)

        def load_vectors(eng, names):
            for name, rows in names:
                a = A[name]
                flat = a.rearrange(" ".join("abcd"[:len(a.shape)]) + " -> (" + " ".join("abcd"[:len(a.shape)]) + ")")
                at = col_at[name]
                eng.dma_start(vector_rows[at % P:at % P + rows, at // P, :],
                              flat.rearrange("(r n) -> r n", n=P)).then_inc(loaded, 16)

        half = len(VECTORS) // 2
        n_loads = 2 + len(VECTORS)

        def start_sp(sp):
            sp.dma_start(consts[:, :], A["consts"]).then_inc(loaded, 16)
            sp.wait_ge(rows_cleared, 1)
            load_vectors(sp, VECTORS[:half])

        stream.append(start_sp)

        def start_act(act):
            act.dma_start(x[:, :, :], A["x"][0].rearrange("(t p) d -> p t d", p=P)).then_inc(loaded, 16)
            act.wait_ge(rows_cleared, 1)
            load_vectors(act, VECTORS[half:])
            act.wait_ge(cols_ready, 1)
            act.activation(col("c", 0, 8), col("c", 0, 8), ACT.Silu)

        def start_pe(pe):
            pe.wait_ge(loaded, 16 * n_loads)
            for j in range(3):
                pe.transpose(ps[:, 0, j * P:(j + 1) * P], vector_rows[:, j, :], ident).then_inc(rows_turned, 1)

        def start_dve(dve):
            dve.memset(vector_rows[:, :, :], 0.0).then_inc(rows_cleared, 1)
            dve.wait_ge(rows_turned, 3)
            dve.tensor_copy(cols[:, :], ps[:, 0, 0:3 * P]).then_inc(cols_ready, 1)

        stage(start_pe, start_act, start_dve)

        c_spread, mod_summed, mod_rows_copied, mod_turned, gates_ready = (
            sem(f"cond_{n}") for n in ("c_spread", "mod_summed", "mod_rows_copied", "mod_turned", "gates_ready"))
        CHUNKS = 12

        def conditioning_steps(layer, take, bank):
            n0 = len(ring.units)
            for n in range(CHUNKS):
                ring.add(("ada", layer, n), columns(A["ada_w"][layer], 512 * n, 512), KD, 512)
            stream.append(stream_units(n0, len(ring.units)))
            WIDE = P // 4
            spread_c = take(KD, 2 * WIDE)
            rows = take(512)

            def spread(dve):
                v = chain["dve"]
                v(dve.memset(spread_c, 0.0))
                dve.tensor_copy(spread_c[:, :, WIDE - 1], col("c", 0, 8)).then_inc(c_spread, 1)

            def chunk(pe, n):
                w = ring.take(pe, ("ada", layer, n))
                if n == 0:
                    pe.wait_ge(c_spread, layer + 1)
                for k in range(KD):
                    g = k % 4
                    ins = pe.matmul(ps[g * WIDE:(g + 1) * WIDE, bank, :], spread_c[:, k, WIDE - 1 - n:2 * WIDE - 1 - n], w[:, k, :],
                                    start=(n == 0 and k < 4), stop=(n == CHUNKS - 1 and k >= 4), skip_group_check=True)
                release(pe)

            def turn(pe):
                pe.drain().then_inc(mod_summed, 1)
                pe.wait_ge(mod_rows_copied, layer + 1)
                for j in range(4):
                    ins = pe.matmul(ps[:, bank, CHUNKS * j:CHUNKS * (j + 1)], rows[:, j * P:(j + 1) * P], const("chunk_rows"),
                                    start=True, stop=True)
                ins.then_inc(mod_turned, 1)

            def finish(dve):
                v = chain["dve"]
                dve.wait_ge(mod_summed, layer + 1)
                dve.tensor_copy(rows, ps[:, bank, :]).then_inc(mod_rows_copied, 1)
                dve.wait_ge(mod_turned, layer + 1)
                v(dve.tensor_tensor(mod[:, layer].rearrange("p i k -> p (i k)").rearrange("p (n j) -> p n j", j=4),
                                    ps[:, bank, 0:4 * CHUNKS].rearrange("p (j n) -> p n j", j=4),
                                    col("ada_b", 48 * layer, 48).rearrange("p (n j) -> p n j", j=4), ALU.add))
                for j, name in enumerate(("norm_mix_g", "norm_ffn_g")):
                    dve.scalar_tensor_tensor(out=gain[:, layer, j, :], in0=mod[:, layer, 3 * j + 1, :], scalar=1.0,
                                             in1=col(name, 8 * layer, 8), op0=ALU.add, op1=ALU.mult)

            return spread, chunk, turn, finish

        def conditioning(layer):
            spread, chunk, turn, finish = conditioning_steps(layer, carve(), 0)

            def pe_(pe):
                for n in range(CHUNKS):
                    chunk(pe, n)
                turn(pe)

            def dve_(dve):
                spread(dve)
                finish(dve)

            stage(pe_, None, dve_)

        norm_signals = [sem(f"norm_{n}") for n in ("summed", "meaned", "rooted", "scaled", "turned")]

        def norm(scale_cols, shift_cols=None, turn=True, gates_of=None):
            summed, meaned, rooted, scaled, turned = norm_signals
            u, turns = uses["norm"], uses["turned norm"]
            uses["norm"] += 1
            uses["turned norm"] += turn
            ssq, ms, rt, rstd = small[:, 0:2], small[:, 2:4], small[:, 4:6], small[:, 6:8]

            def act_(act):
                for t in range(TT):
                    act.activation(xn[:, t, :], x[:, t, :], ACT.Square, accum_out=ssq[:, t:t + 1]).then_inc(summed, 1)
                act.wait_ge(meaned, u + 1)
                act.activation(rt, ms, ACT.Sqrt).then_inc(rooted, 1)
                if gates_of is not None:
                    act.wait_ge(gates_ready, 2 * gates_of + 1)
                    act.copy(gates[:, 0, :].rearrange("p (b n) -> p b n", b=2), ps[:, 4:6, :])
                if turn:
                    for k in (2, 3, 6, 7):
                        act.wait_ge(turned, 4 * turns + k // 2 + 1)
                        o, i = hT[:, k, :], ps[:, k // 2, (k % 2) * S:(k % 2 + 1) * S]
                        act.activation(o, i, ACT.Identity, scale=scale_cols[:, k:k + 1],
                                       bias=shift_cols[:, k:k + 1] if shift_cols is not None else 0.0)

            def dve_(dve):
                v = chain["dve"]
                dve.wait_ge(summed, TT * (u + 1))
                dve.tensor_scalar(ms, ssq, 1.0 / D, EPS, ALU.mult, ALU.add).then_inc(meaned, 1)
                dve.wait_ge(rooted, u + 1)
                v(dve.reciprocal(rstd, rt))
                for t in range(TT):
                    dve.tensor_scalar(xn[:, t, :], x[:, t, :], rstd[:, t:t + 1], None, ALU.mult).then_inc(scaled, 1)
                if gates_of is not None:
                    dve.wait_ge(gates_ready, 2 * gates_of + 2)
                    dve.tensor_copy(gates[:, 1, :].rearrange("p (b n) -> p b n", b=2), ps[:, 6:8, :])
                if turn:
                    for k in (0, 1, 4, 5):
                        dve.wait_ge(turned, 4 * turns + k // 2 + 1)
                        o, i = hT[:, k, :], ps[:, k // 2, (k % 2) * S:(k % 2 + 1) * S]
                        if shift_cols is not None:
                            dve.tensor_scalar(o, i, scale_cols[:, k:k + 1], shift_cols[:, k:k + 1], ALU.mult, ALU.add)
                        else:
                            dve.tensor_scalar(o, i, scale_cols[:, k:k + 1], None, ALU.mult)

            def pe_(pe):
                if gates_of is not None:
                    for g in range(2):
                        for k in range(KD):
                            ins = pe.matmul(ps[:, 4 + 2 * g + k // 4, (k % 4) * P:(k % 4 + 1) * P],
                                            mod[:, gates_of, 3 * g + 2, k:k + 1].to_broadcast([P, P]), ident,
                                            start=True, stop=True)
                        ins.then_inc(gates_ready, 1)
                if not turn:
                    return
                pe.wait_ge(scaled, TT * (u + 1))
                for k in range(KD):
                    for t in range(TT):
                        ins = pe.transpose(ps[:, k // 2, (k % 2) * S + t * P:(k % 2) * S + (t + 1) * P],
                                           xn[:, t, k * P:(k + 1) * P], ident)
                    if k % 2:
                        ins.then_inc(turned, 1)

            stage(pe_, act_, dve_)

        def attention():
            w_in, w_o = A["attn_w_in"][0], A["attn_w_o"][0]
            n0 = len(ring.units)
            for c in range(6):
                ring.add(("attn_in", c), columns(w_in, 512 * c, 512), KD, 512)
            ring.add(("attn_f",), columns(w_in, 3 * D, N_HEADS), KD, N_HEADS)
            stream.append(stream_units(n0, len(ring.units)))
            take = carve()
            spread_c, condition_chunk, condition_turn, condition_finish = conditioning_steps(1, take, 7)
            n0 = len(ring.units)
            for c in range(2):
                ring.add(("attn_out", c), columns(w_o, 512 * c, 512), KD, 512)
            stream.append(stream_units(n0, len(ring.units)))
            qkT = take(16, S)
            v_tok = take(TT, D)
            oT = take(KD, S)
            probs = take(2, 2, S)
            probsT = take(2, 512)
            lf = take(TT, N_HEADS)
            F = take(TT, N_HEADS)
            t1, t2, t3 = take(TT, N_HEADS), take(TT, N_HEADS), take(TT, N_HEADS)
            fbias = take(N_HEADS)
            nFT = take(S)
            mx, top, nb, rs, ri = (take(16, 2) for _ in range(5))

            p_ready, p_taken = sem("attn_proj_ready"), sem("attn_proj_taken")
            bias_loaded = sem("attn_bias_loaded")

            def proj_pe(pe):
                for c in range(4):
                    w = ring.take(pe, ("attn_in", c))
                    for j in range(4):
                        n = 4 * c + j
                        if n >= 8:
                            pe.wait_ge(p_taken, n - 7)
                        for k in range(KD):
                            ins = pe.matmul(ps[:, n % 8, 0:S], w[:, k, j * P:(j + 1) * P], hT[:, k, :],
                                            start=(k == 0), stop=(k == KD - 1))
                        ins.then_inc(p_ready, 1)
                    release(pe)
                for c in range(4, 6):
                    w = ring.take(pe, ("attn_in", c))
                    for t in range(TT):
                        n = 16 + 2 * (c - 4) + t
                        pe.wait_ge(p_taken, n - 7)
                        for k in range(KD):
                            ins = pe.matmul(ps[:, n % 8, :], hT[:, k, t * P:(t + 1) * P], w[:, k, :],
                                            start=(k == 0), stop=(k == KD - 1))
                        ins.then_inc(p_ready, 1)
                    release(pe)
                w = ring.take(pe, ("attn_f",))
                pe.wait_ge(p_taken, 13)
                for t in range(TT):
                    for k in range(KD):
                        ins = pe.matmul(ps[:, 4, t * 16:(t + 1) * 16], hT[:, k, t * P:(t + 1) * P], w[:, k, :],
                                        start=(k == 0), stop=(k == KD - 1))
                ins.then_inc(p_ready, 1)
                release(pe)

            def take_projection(eng, n, copy):
                eng.wait_ge(p_ready, n + 1)
                if n < 16:
                    copy(qkT[:, n, :], ps[:, n % 8, 0:S]).then_inc(p_taken, 1)
                else:
                    c, t = divmod(n - 16, 2)
                    copy(v_tok[:, t, c * 512:(c + 1) * 512], ps[:, n % 8, :]).then_inc(p_taken, 1)

            def proj_dve(dve):
                v = chain["dve"]
                for n in range(20):
                    take_projection(dve, n, dve.tensor_copy)
                dve.wait_ge(p_ready, 21)
                dve.wait_ge(bias_loaded, 16)
                v(dve.tensor_tensor(t1, ps[:, 4, 0:32].rearrange("p (t h) -> p t h", t=TT),
                                    fbias.unsqueeze(1).to_broadcast([P, TT, N_HEADS]), ALU.add))
                v(dve.tensor_scalar(t2, t1, -1.0, None, ALU.mult))
                dve.tensor_tensor(t2, t1, t2, ALU.min).then_inc(p_taken, 1)

            def proj_act(act):
                act.dma_start(fbias, A["attn_f_bias"].partition_broadcast(P).rearrange("p a h -> p (a h)")).then_inc(bias_loaded, 16)

            stage(proj_pe, proj_act, proj_dve)

            a, b, c_, d = sem("attn_exp"), sem("attn_ln"), sem("attn_logf"), sem("attn_F")
            e, f = sem("attn_F_taken"), sem("attn_FT")

            def gate_act(act):
                act.activation(t3, t2, ACT.Exp).then_inc(a, 1)
                act.wait_ge(a, 1)
                act.activation(t2, t3, ACT.Ln, bias=1.0).then_inc(b, 1)

            def gate_dve(dve):
                v = chain["dve"]
                v(dve.memset(nFT, 0.0))
                dve.wait_ge(b, 1)
                v(dve.tensor_scalar(t1, t1, 0.0, None, ALU.min))
                dve.tensor_tensor(lf, t1, t2, ALU.subtract).then_inc(c_, 1)
                dve.wait_ge(d, 1)
                dve.tensor_copy(F, ps[:, 0, 0:32].rearrange("p (t h) -> p t h", t=TT)).then_inc(e, 1)
                dve.wait_ge(f, 1)
                dve.tensor_scalar(nFT[0:N_HEADS, :], ps[0:N_HEADS, 1, 0:S], -8.0, None, ALU.mult)

            def gate_pe(pe):
                pe.wait_ge(c_, 1)
                pe.matmul(ps[:, 0, 0:16], const("upto"), lf[:, 0, :], start=True, stop=True)
                pe.matmul(ps[:, 0, 16:32], ones, lf[:, 0, :], start=True, stop=False)
                pe.matmul(ps[:, 0, 16:32], const("upto"), lf[:, 1, :], start=False, stop=True).then_inc(d, 1)
                pe.wait_ge(e, 1)
                for t in range(TT):
                    ins = pe.transpose(ps[0:N_HEADS, 1, t * P:(t + 1) * P], F[:, t, :], ident)
                ins.then_inc(f, 1)

            stage(gate_pe, gate_act, gate_dve)

            scored, biased, exped, normed = sem("attn_scored"), sem("attn_biased"), sem("attn_exped"), sem("attn_normed")
            turned, copied, mixed, stored = sem("attn_turned"), sem("attn_copied"), sem("attn_mixed"), sem("attn_stored")
            N = 16

            def scores(pe, i):
                qt, pair = divmod(i, 8)
                keys = (qt + 1) * P
                if i >= 2:
                    pe.wait_ge(exped, 2 * (i - 1))
                for j in range(2):
                    rows = slice(64 * j, 64 * j + 64)
                    bank = ps[:, 2 * (i % 2) + j, :]
                    o = bank[:, 0:keys]
                    pe.matmul(o, qkT[rows, pair, qt * P:(qt + 1) * P], qkT[rows, 8 + pair, 0:keys], start=True, stop=False)
                    h = 2 * pair + j
                    pe.matmul(o, ident[:, h:h + 1].to_broadcast([P, P]), nFT[:, 0:keys], start=False, stop=False)
                    ins = pe.matmul(bank[:, qt * P:keys], ident, const("mask_ts"), start=False, stop=True)
                ins.then_inc(scored, 1)

            def weigh(pe, i):
                qt, pair = divmod(i, 8)
                pe.wait_ge(normed, i + 1)
                if i >= 2:
                    pe.wait_ge(copied, i - 1)
                for j in range(2):
                    for kt in range(qt + 1):
                        m = j * (qt + 1) + kt
                        ins = pe.transpose(ps[:, 4 + i % 2, m * P:(m + 1) * P], probs[:, i % 2, j, kt * P:(kt + 1) * P], ident)
                ins.then_inc(turned, 1)

            def mix(pe, i):
                qt, pair = divmod(i, 8)
                pe.wait_ge(copied, i + 1)
                if i >= 1:
                    pe.wait_ge(stored, i)
                for j in range(2):
                    h = 2 * pair + j
                    for kt in range(qt + 1):
                        m = j * (qt + 1) + kt
                        ins = pe.matmul(ps[64 * j:64 * j + 64, 6, 0:P], v_tok[:, kt, h * 64:(h + 1) * 64],
                                        probsT[:, i % 2, m * P:(m + 1) * P], start=(kt == 0), stop=(kt == qt))
                ins.then_inc(mixed, 1)

            def heads_pe(pe):
                for i in range(N + 2):
                    if i < N:
                        scores(pe, i)
                    if 1 <= i <= N:
                        weigh(pe, i - 1)
                    if 2 <= i:
                        mix(pe, i - 2)
                    if 1 <= i <= CHUNKS:
                        condition_chunk(pe, i - 1)

                condition_turn(pe)

            def heads_act(act):
                for i in range(N):
                    qt, pair = divmod(i, 8)
                    keys = (qt + 1) * P
                    act.wait_ge(biased, i + 1)
                    if i >= 2:
                        act.wait_ge(turned, i - 1)
                    for j in range(2):
                        act.activation(probs[:, i % 2, j, 0:keys], ps[:, 2 * (i % 2) + j, 0:keys], ACT.Exp,
                                       scale=0.125, bias=nb[:, i, j:j + 1], accum_out=rs[:, i, j:j + 1]).then_inc(exped, 1)

            def heads_dve(dve):
                v = chain["dve"]
                spread_c(dve)
                for i in range(N + 2):
                    if i < N:
                        qt, pair = divmod(i, 8)
                        keys = (qt + 1) * P
                        dve.wait_ge(scored, i + 1)
                        s = ps[:, 2 * (i % 2):2 * (i % 2) + 2, 0:keys]
                        v(dve.tensor_reduce(mx[:, i, :], s, AX.X, ALU.max))
                        Fq = F[:, qt, 2 * pair:2 * pair + 2]
                        v(dve.scalar_tensor_tensor(out=top[:, i, :], in0=mx[:, i, :], scalar=0.125, in1=Fq,
                                                   op0=ALU.mult, op1=ALU.add))
                        dve.tensor_tensor(nb[:, i, :], Fq, top[:, i, :], ALU.subtract).then_inc(biased, 1)
                    if 1 <= i <= N:
                        m = i - 1
                        keys = (m // 8 + 1) * P
                        dve.wait_ge(exped, 2 * m + 2)
                        v(dve.reciprocal(ri[:, m, :], rs[:, m, :]))
                        for j in range(2):
                            ins = dve.tensor_scalar(probs[:, m % 2, j, 0:keys], probs[:, m % 2, j, 0:keys], ri[:, m, j:j + 1],
                                                    None, ALU.mult)
                        ins.then_inc(normed, 1)
                        n = 2 * keys
                        dve.wait_ge(turned, m + 1)
                        if m >= 2:
                            dve.wait_ge(mixed, m - 1)
                        dve.tensor_copy(probsT[:, m % 2, 0:n], ps[:, 4 + m % 2, 0:n]).then_inc(copied, 1)
                    if 2 <= i:
                        m = i - 2
                        qt, pair = divmod(m, 8)
                        dve.wait_ge(mixed, m + 1)
                        dve.tensor_copy(oT[:, pair, qt * P:(qt + 1) * P], ps[:, 6, 0:P]).then_inc(stored, 1)
                condition_finish(dve)

            stage(heads_pe, heads_act, heads_dve)
            gated_output("attn_out", oT, gates[:, 0, :])

        def gated_output(tag, fT, gate):
            ready = sem(f"{tag}_ready")
            scratch = xn

            def pe_(pe):
                for c in range(2):
                    w = ring.take(pe, (tag, c))
                    for t in range(TT):
                        for k in range(KD):
                            ins = pe.matmul(ps[:, 2 * c + t, :], fT[:, k, t * P:(t + 1) * P], w[:, k, :],
                                            start=(k == 0), stop=(k == KD - 1))
                        ins.then_inc(ready, 1)
                    release(pe)

            def dve_(dve):
                v = chain["dve"]
                for c in range(2):
                    for t in range(TT):
                        half = slice(512 * c, 512 * c + 512)
                        dve.wait_ge(ready, 2 * c + t + 1)
                        v(dve.tensor_tensor(scratch[:, t, half], ps[:, 2 * c + t, :], gate[:, half], ALU.mult))
                        dve.tensor_tensor(x[:, t, half], x[:, t, half], scratch[:, t, half], ALU.add)

            stage(pe_, None, dve_)

        route_signals = [sem("route_" + n) for n in (
            "router_loaded", "logits_ready", "scores_ready", "member_ready", "ranked", "table_ready")]
        quad_signals = [sem("quad_" + n) for n in (
            "picked", "weighted", "w_turned", "w_copied", "g_ready", "u_ready", "silu_done", "prod_done", "xa_ready",
            "xb_ready", "xa_taken", "xb_taken", "p_turned", "p_copied", "ya_ready", "yb_ready", "ya_taken", "yb_taken",
            "combined", "step")]

        def experts(layer):
            norm(gain[:, layer, 1, :], mod[:, layer, 3, :])
            G, H = gain[:, layer, 1, :], mod[:, layer, 3, :]
            take = carve()
            router = take(KD, N_EXPERTS)
            rbias = take(N_EXPERTS)
            scores = take(TT, N_EXPERTS)
            sel = take(TT, N_EXPERTS)
            top_in_group = take(TT, N_GROUPS, 8)
            group_score = take(TT, 8)
            top_group = take(TT, 8)
            group_at = take(TT, 8, dt=U32)
            group_f = take(TT)
            group_mask, penalty = take(TT, N_GROUPS), take(TT, N_GROUPS)
            chosen = take(TT, 8)
            chosen_at = take(TT, 8, dt=U32)
            chosen_f = take(TT, 2)
            hot = take(TT, 2, N_EXPERTS)
            junk = take(N_EXPERTS)
            raw_gate, gate = take(TT, 2), take(TT, 2)
            gate_sum, gate_inv = take(TT), take(TT)
            member = take(TT, N_EXPERTS)
            n_more, more_end, more_slot = take(N_EXPERTS), take(N_EXPERTS), take(N_EXPERTS)
            slot_of, beyond = take(TT, N_EXPERTS), take(TT, N_EXPERTS)
            first_slot = take(N_EXPERTS)
            dest = take(TT, 2)
            ended = take(MORE, N_EXPERTS)
            block_expert = take(MORE)
            table = take(2, MORE, dt=I32)
            quad_live = take(QUADS, dt=I32)
            pick, pick_w, part, part2 = take(TT, P), take(TT, P), take(TT, P), take(TT, P)
            pick_wT = take(TT, P)
            xgT = take(KD, P)
            silu_g, prod = take(512), take(512)
            prodT = take(4, P)
            y = take(D)

            small_loaded, logits_ready, scores_ready, member_ready, ranked, table_ready = route_signals
            r0 = layer + 1

            def route_act(act):
                act.dma_start(router, A["router_w"].rearrange("(k p) e -> p k e", p=P)).then_inc(small_loaded, 16)
                act.dma_start(rbias, A["router_bias"].partition_broadcast(P)).then_inc(small_loaded, 16)
                act.wait_ge(logits_ready, r0)
                act.activation(scores, ps[:, 0, 0:TT * N_EXPERTS].rearrange("p (t e) -> p t e", t=TT), ACT.Sigmoid)\
                    .then_inc(scores_ready, 1)

            def route_pe(pe):
                pe.wait_ge(small_loaded, 32 * r0)
                for t in range(TT):
                    for k in range(KD):
                        ins = pe.matmul(ps[:, 0, t * 32:(t + 1) * 32], hT[:, k, t * P:(t + 1) * P], router[:, k, :],
                                        start=(k == 0), stop=(k == KD - 1))
                ins.then_inc(logits_ready, 1)
                pe.wait_ge(member_ready, r0)
                pe.matmul(ps[:, 1, 0:32], const("before"), member[:, 0, :], start=True, stop=True)
                pe.matmul(ps[:, 1, 32:64], ones, member[:, 0, :], start=True, stop=False)
                pe.matmul(ps[:, 1, 32:64], const("before"), member[:, 1, :], start=False, stop=True)
                pe.matmul(ps[:, 1, 64:96], ones, member[:, 0, :], start=True, stop=False)
                pe.matmul(ps[:, 1, 64:96], ones, member[:, 1, :], start=False, stop=True).then_inc(ranked, 1)

            def route_dve(dve):
                v = chain["dve"]
                iota_e = const("iota")[:, 0:N_EXPERTS]
                dve.wait_ge(scores_ready, r0)
                dve.wait_ge(small_loaded, 32 * r0)
                dve.memset(group_score, NEG)
                v(dve.tensor_tensor(sel, scores, rbias.unsqueeze(1).to_broadcast([P, TT, N_EXPERTS]), ALU.add))
                for t in range(TT):
                    for g in range(N_GROUPS):
                        ins = dve.max(top_in_group[:, t, g, :], sel[:, t, g * GROUP:(g + 1) * GROUP])
                v(ins)
                v(dve.tensor_tensor(group_score[:, :, 0:4], top_in_group[:, :, :, 0], top_in_group[:, :, :, 1], ALU.add))
                for t in range(TT):
                    v(dve.max(top_group[:, t, :], group_score[:, t, :]))
                    v(dve.max_index(group_at[:, t, :], top_group[:, t, :], group_score[:, t, :]))
                v(dve.tensor_copy(group_f, group_at[:, :, 0]))
                for t in range(TT):
                    ins = dve.tensor_scalar(group_mask[:, t, :], const("iota")[:, 0:4], group_f[:, t:t + 1], None, ALU.is_equal)
                v(ins)
                v(dve.tensor_scalar(penalty, group_mask, -NEG, NEG, ALU.mult, ALU.add))
                def by_group(a):
                    return a.rearrange("p t (g e) -> p t g e", g=N_GROUPS)
                wide = [P, TT, N_GROUPS, GROUP]
                v(dve.tensor_tensor(by_group(sel), by_group(sel), group_mask.unsqueeze(3).to_broadcast(wide), ALU.mult))
                v(dve.tensor_tensor(by_group(sel), by_group(sel), penalty.unsqueeze(3).to_broadcast(wide), ALU.add))
                for t in range(TT):
                    v(dve.max(chosen[:, t, :], sel[:, t, :]))
                    v(dve.max_index(chosen_at[:, t, :], chosen[:, t, :], sel[:, t, :]))
                v(dve.tensor_copy(chosen_f, chosen_at[:, :, 0:2]))
                for t in range(TT):
                    for i in range(2):
                        ins = dve.tensor_scalar(hot[:, t, i, :], iota_e, chosen_f[:, t, i:i + 1], None, ALU.is_equal)
                v(ins)
                dve.tensor_tensor(member, hot[:, :, 0, :], hot[:, :, 1, :], ALU.add).then_inc(member_ready, 1)
                for t in range(TT):
                    for i in range(2):
                        v(dve.tensor_tensor_reduce(junk, hot[:, t, i, :], scores[:, t, :], 1.0, 0.0, ALU.mult, ALU.add,
                                                   raw_gate[:, t, i:i + 1]))
                v(dve.tensor_tensor(gate_sum, raw_gate[:, :, 0], raw_gate[:, :, 1], ALU.add))
                v(dve.reciprocal(gate_inv, gate_sum))
                v(dve.tensor_tensor(gate, raw_gate, gate_inv.unsqueeze(2).to_broadcast([P, TT, 2]), ALU.mult))
                dve.wait_ge(ranked, r0)
                count = ps[:, 1, 64:96]
                v(dve.tensor_scalar(n_more, count, float(SLOTS), None, ALU.is_gt))
                for j in range(2, S // SLOTS):
                    v(dve.scalar_tensor_tensor(out=n_more, in0=count, scalar=float(SLOTS * j), in1=n_more,
                                               op0=ALU.is_gt, op1=ALU.add))
                v(dve.tensor_tensor_scan(more_end, ones[:, 0:N_EXPERTS], n_more, 0.0, ALU.mult, ALU.add))
                v(dve.tensor_tensor(more_slot, more_end, n_more, ALU.subtract))
                v(dve.tensor_scalar(first_slot, iota_e, float(SLOTS), None, ALU.mult))
                v(dve.scalar_tensor_tensor(out=more_slot, in0=more_slot, scalar=float(SLOTS), in1=first_slot,
                                           op0=ALU.mult, op1=ALU.subtract))
                v(dve.tensor_scalar(more_slot, more_slot, float(SLOTS * (N_EXPERTS - 1)), None, ALU.add))
                rank = ps[:, 1, 0:TT * N_EXPERTS].rearrange("p (t e) -> p t e", t=TT)
                wide = [P, TT, N_EXPERTS]
                v(dve.tensor_scalar(beyond, rank, float(SLOTS), None, ALU.is_ge))
                v(dve.tensor_tensor(beyond, beyond, more_slot.unsqueeze(1).to_broadcast(wide), ALU.mult))
                v(dve.tensor_tensor(slot_of, rank, first_slot.unsqueeze(1).to_broadcast(wide), ALU.add))
                v(dve.tensor_tensor(slot_of, slot_of, beyond, ALU.add))
                for t in range(TT):
                    for i in range(2):
                        v(dve.tensor_tensor_reduce(junk, hot[:, t, i, :], slot_of[:, t, :], 1.0, 0.0, ALU.mult, ALU.add,
                                                   dest[:, t, i:i + 1]))
                shape = [P, MORE, N_EXPERTS]
                v(dve.tensor_tensor(ended, const("iota")[:, 0:MORE].unsqueeze(2).to_broadcast(shape),
                                    more_end.unsqueeze(1).to_broadcast(shape), ALU.is_ge))
                v(dve.tensor_reduce(block_expert, ended, AX.X, ALU.add))
                v(dve.memset(quad_live, 1))
                dve.tensor_scalar(table[:, 0, :], block_expert, float(N_EXPERTS - 1), None, ALU.min)
                dve.tensor_scalar(quad_live[:, FIRST_QUADS:QUADS],
                                  block_expert.rearrange("p (q j) -> p q j", j=QUAD)[:, :, 0], float(N_EXPERTS), None, ALU.is_lt)
                v(dve.tensor_scalar(table[:, 1, :], block_expert, float(N_EXPERTS), None, ALU.is_lt))
                dve.memset(y, 0.0).then_inc(table_ready, 1)

            stage(route_pe, route_act, route_dve)

            n0, UNITS = len(ring.units), 2 * RING
            assert n0 >= RING
            base = list(ring.total)
            for i in range(QUADS):
                for u in range(UNITS):
                    ring.add(("moe", layer, i, u), None, 8, 512, loads=2)

            def load_experts(sp):
                def half(u, j, expert):
                    phase = u // 2
                    w = A[("exp_w1", "exp_w3", "exp_w2")[phase // 2]][layer]
                    k, n = (4, 512) if phase < 4 else (2, D)
                    rows = slice((phase % 2) * k * P, (phase % 2 + 1) * k * P)
                    source = w[bass.ds(expert, 1), rows, :].rearrange("a (k p) n -> p (a k) n", p=P)
                    return ring_buffer[:, (n0 + u) % RING, j * 2048:(j + 1) * 2048].rearrange("p (k n) -> p k n", k=k), source

                def load(u, j, i, expert, **cond):
                    if j == 0:
                        sp.wait_ge(weights_used, n0 + u - RING + 1 + UNITS * i)
                    to, source = half(u, j, expert)
                    sp.dma_start(to, source, **cond).then_inc(weights_landed[(n0 + u) % RING], 16)

                with sp.Fori(0, FIRST_QUADS) as i:
                    for u in range(UNITS):
                        for j in range(2):
                            load(u, j, i, QUAD * i + 2 * (u % 2) + j)
                sp.wait_ge(table_ready, r0)
                with sp.Fori(0, QUADS - FIRST_QUADS) as i:
                    quad_is_live = sp.value_load(quad_live[0:1, bass.ds(i + FIRST_QUADS, 1)], min_val=0, max_val=1)
                    with sp.If(quad_is_live > 0):
                        at = [bass.ds(QUAD * i + j, 1) for j in range(QUAD)]
                        expert = [sp.value_load(table[0:1, 0, a], min_val=0, max_val=N_EXPERTS - 1) for a in at]
                        live = [sp.value_load(table[0:1, 1, a], min_val=0, max_val=1) for a in at]
                        for u in range(UNITS):
                            for j in range(2):
                                b = 2 * (u % 2) + j
                                load(u, j, i + FIRST_QUADS, expert[b], cond=(live[b] > 0))
                    with sp.Else():
                        sp.wait_ge(weights_used, n0 + UNITS * FIRST_QUADS + UNITS * i)
                        for slot in range(RING):
                            sp.drain().then_inc(weights_landed[slot], 64)
            stream.append(load_experts)

            (picked, weighted, w_turned, w_copied, g_ready, u_ready, silu_done, prod_done, xa_ready, xb_ready, xa_taken,
             xb_taken, p_turned, p_copied, ya_ready, yb_ready, ya_taken, yb_taken, combined, quad_step) = quad_signals
            i0 = QUADS * layer
            j0 = (QUADS + 1) * layer
            BXA, BXB, BG, BU = 4, 5, 6, 7

            def each_quad(eng, quad, signals, frees_units=False, steps=0):
                with eng.Fori(0, QUADS) as i:
                    live = eng.value_load(quad_live[0:1, bass.ds(i, 1)], min_val=0, max_val=1)
                    with eng.If(live > 0):
                        quad(i)
                    with eng.Else():
                        for s in signals:
                            eng.drain().then_inc(s, 1)
                        if frees_units:
                            for slot in range(RING):
                                eng.wait_ge(weights_landed[slot], base[slot] + 64 + 64 * i)
                            eng.drain().then_inc(weights_used, UNITS)
                        if steps:
                            eng.drain().then_inc(quad_step, steps)

            def gather(pe, n):
                for k in range(KD):
                    for t in range(TT):
                        ins = pe.matmul(ps[:, BXA + k // 4, (k % 4) * P:(k % 4 + 1) * P], xn[:, t, k * P:(k + 1) * P],
                                        pick[:, t, :], start=(t == 0), stop=(t == TT - 1))
                        if n is not None and k == 0 and t == 0:
                            ins.then_inc(weights_used, 1)
                    if k == 3:
                        ins.then_inc(xa_ready, 1)
                ins.then_inc(xb_ready, 1)

            def quads_pe(pe):
                for b in range(4):
                    ins = pe.matmul(ps[:, b, :], ident, y[:, 0:512], start=True, stop=False, skip_group_check=True)
                ins.then_inc(combined, 1)
                pe.wait_ge(picked, j0 + 1)
                gather(pe, None)

                def unit(i, u):
                    slot = (n0 + u) % RING
                    pe.wait_ge(weights_landed[slot], base[slot] + 32 * (u // RING + 1) + 64 * i)
                    return [ring_buffer[:, slot, j * 2048:(j + 1) * 2048] for j in range(2)]

                def up(i, u0, bank, ready):
                    for phase in range(2):
                        halves = [w.rearrange("p (k n) -> p k n", k=4) for h in range(2) for w in unit(i, u0 + 2 * phase + h)]
                        for k in range(4):
                            for j in range(QUAD):
                                c = slice(SLOTS * j, SLOTS * j + SLOTS)
                                ins = pe.matmul(ps[c, bank, :], xgT[:, 4 * phase + k, c], halves[j][:, k, :],
                                                start=(phase == 0 and k == 0), stop=(phase == 1 and k == 3))
                                if k == 3 and (j == 1 or j == 3 and phase == 0):
                                    ins.then_inc(weights_used, 1)
                                if u0 == 4 and phase == k == j == 0:
                                    ins.then_inc(weights_used, 1)
                    ins.then_inc(ready, 1)

                def quad(i):
                    pe.wait_ge(weighted, j0 + i + 1)
                    pe.wait_ge(xa_taken, j0 + i + 1)
                    for t in range(TT):
                        ins = pe.transpose(ps[:, BXA, t * P:(t + 1) * P], pick_w[:, t, :], ident)
                    ins.then_inc(w_turned, 1)
                    pe.wait_ge(xb_taken, j0 + i + 1)
                    pe.wait_ge(yb_taken, j0 + i + 1)
                    up(i, 0, BG, g_ready)
                    pe.wait_ge(ya_taken, j0 + i + 1)
                    up(i, 4, BU, u_ready)
                    pe.wait_ge(w_copied, i0 + i + 1)
                    pe.wait_ge(picked, j0 + i + 2)
                    gather(pe, i)
                    pe.wait_ge(prod_done, i0 + i + 1)
                    for f in range(4):
                        ins = pe.transpose(ps[:, BG, f * P:(f + 1) * P], prod[:, f * P:(f + 1) * P], ident)
                    ins.then_inc(p_turned, 1)
                    pe.wait_ge(p_copied, i0 + i + 1)
                    for phase in range(2):
                        halves = [w.rearrange("p (k n) -> p k n", k=2) for h in range(2) for w in unit(i, 8 + 2 * phase + h)]
                        for half, (bank, ready) in enumerate(((BU, ya_ready), (BG, yb_ready))):
                            for k in range(2):
                                for j in range(QUAD):
                                    c = slice(SLOTS * j, SLOTS * j + SLOTS)
                                    ins = pe.matmul(ps[c, bank, :], prodT[:, 2 * phase + k, c],
                                                    halves[j][:, k, half * 512:(half + 1) * 512],
                                                    start=(phase == 0 and k == 0), stop=(phase == 1 and k == 1))
                                    if half == k == 1 and (j == 1 or j == 3 and phase == 0):
                                        ins.then_inc(weights_used, 1)
                            if phase:
                                ins.then_inc(ready, 1)
                    for half, taken in enumerate((ya_taken, yb_taken)):
                        pe.wait_ge(taken, j0 + i + 2)
                        for t in range(TT):
                            ins = pe.matmul(ps[:, 2 * half + t, :], pick_wT[:, t, :], y[:, half * 512:(half + 1) * 512],
                                            start=False, stop=False, skip_group_check=True)
                            if half == 0 and t == 0:
                                ins.then_inc(weights_used, 1)
                    ins.then_inc(combined, 1)

                ring.next += UNITS * QUADS
                each_quad(pe, quad, (w_turned, g_ready, u_ready, xa_ready, xb_ready, p_turned, ya_ready, yb_ready, combined),
                          frees_units=True)

            def taken_x(eng, i, k, on_act):
                o, src = xgT[:, k, :], ps[:, BXA + k // 4, (k % 4) * P:(k % 4 + 1) * P]
                if on_act:
                    return eng.activation(o, src, ACT.Identity, scale=G[:, k:k + 1], bias=H[:, k:k + 1])
                return eng.tensor_scalar(o, src, G[:, k:k + 1], H[:, k:k + 1], ALU.mult, ALU.add)

            def quads_act(act):
                act.wait_ge(xb_ready, j0 + 1)
                for k in range(4, 8):
                    ins = taken_x(act, 0, k, True)
                    if k == 4:
                        ins.then_inc(ya_taken, 1)
                ins.then_inc(xb_taken, 1)
                def quad(i):
                    act.wait_ge(g_ready, i0 + i + 1)
                    act.activation(silu_g, ps[:, BG, :], ACT.Silu).then_inc(silu_done, 1)
                    act.wait_ge(xb_ready, j0 + i + 2)
                    for k in range(4, 8):
                        ins = taken_x(act, i, k, True)
                    ins.then_inc(xb_taken, 1)
                    act.wait_ge(combined, j0 + i + 1)
                    act.wait_ge(ya_ready, i0 + i + 1)
                    act.copy(y[:, 0:512], ps[:, BU, :]).then_inc(ya_taken, 1)

                each_quad(act, quad, (silu_done, xb_taken, ya_taken))

            def quads_dve(dve):
                shape = [P, TT, P]
                slot = const("iota").unsqueeze(1).to_broadcast(shape)

                step0 = (4 + 5 * QUADS) * layer

                def step(ins, count):
                    ins.then_inc(quad_step, 1)
                    dve.wait_ge(quad_step, step0 + count)

                def build(count):
                    for n, a in enumerate((part, part2)):
                        step(dve.tensor_tensor(a, slot, dest[:, :, n:n + 1].to_broadcast(shape), ALU.is_equal), count + n + 1)
                    dve.tensor_tensor(pick, part, part2, ALU.add).then_inc(picked, 1)
                    for n, a in enumerate((part, part2)):
                        step(dve.tensor_tensor(a, a, gate[:, :, n:n + 1].to_broadcast(shape), ALU.mult), count + n + 3)
                    dve.tensor_tensor(pick_w, part, part2, ALU.add).then_inc(weighted, 1)

                build(0)
                dve.wait_ge(xa_ready, j0 + 1)
                for k in range(4):
                    ins = taken_x(dve, 0, k, False)
                    if k == 0:
                        ins.then_inc(yb_taken, 1)
                ins.then_inc(xa_taken, 1)
                def quad(i):
                    dve.wait_ge(combined, j0 + i + 1)
                    dve.wait_ge(w_turned, i0 + i + 1)
                    dve.tensor_copy(pick_wT, ps[:, BXA, 0:2 * P].rearrange("p (t c) -> p t c", t=TT)).then_inc(w_copied, 1)
                    count = 4 + 5 * i
                    step(dve.tensor_scalar(dest, dest, float(-P), None, ALU.add), count + 1)
                    dve.wait_ge(xb_ready, j0 + i + 1)
                    build(count + 1)
                    dve.wait_ge(silu_done, i0 + i + 1)
                    dve.wait_ge(u_ready, i0 + i + 1)
                    dve.tensor_tensor(prod, silu_g, ps[:, BU, :], ALU.mult).then_inc(prod_done, 1)
                    dve.wait_ge(xa_ready, j0 + i + 2)
                    for k in range(4):
                        ins = taken_x(dve, i, k, False)
                    ins.then_inc(xa_taken, 1)
                    dve.wait_ge(p_turned, i0 + i + 1)
                    dve.tensor_copy(prodT, ps[:, BG, :].rearrange("p (f c) -> p f c", f=4)).then_inc(p_copied, 1)
                    dve.wait_ge(yb_ready, i0 + i + 1)
                    dve.tensor_copy(y[:, 512:1024], ps[:, BG, :]).then_inc(yb_taken, 1)

                each_quad(dve, quad, (w_copied, prod_done, xa_taken, p_copied, yb_taken, picked, weighted), steps=5)

            stage(quads_pe, quads_act, quads_dve)

            def add_dve(dve):
                v = chain["dve"]
                g = gates[:, 1, :]
                for t in range(TT):
                    for half in range(2):
                        cols_ = slice(512 * half, 512 * half + 512)
                        v(dve.tensor_tensor(xn[:, t, cols_], ps[:, 2 * half + t, :], g[:, cols_], ALU.mult))
                        dve.tensor_tensor(x[:, t, cols_], x[:, t, cols_], xn[:, t, cols_], ALU.add)
            stage(None, None, add_dve)

        def pooling():
            ring.add(("pool_w",), A["pool_w"][0].rearrange("g (k p) e -> p (g k) e", p=P), KD, 256)
            stream.append(stream_units(len(ring.units) - 1, len(ring.units)))
            take = carve()
            PAD = 16
            sums = [take(2, PAD + S) for _ in range(2)]
            pooledT = take(KD, S)
            row_scale = take(D)
            scale_loaded, pooled, y_ready = sem("pool_scale_loaded"), sem("pool_pooled"), sem("pool_y_ready")

            def act_(act):
                act.dma_start(row_scale, A["pool_scale"][0].partition_broadcast(P)).then_inc(scale_loaded, 16)

            def pe_(pe):
                w = ring.take(pe, ("pool_w",))
                for g in range(4):
                    pe.wait_ge(pooled, g + 1)
                    for t in range(TT):
                        for k in range(2):
                            ins = pe.matmul(ps[:, 4 * (g % 2) + 2 * t + g // 2, 0:256], pooledT[:, 2 * g + k, t * P:(t + 1) * P],
                                            w[:, 2 * g + k, :], start=(k == 0), stop=(k == 1))
                    ins.then_inc(y_ready, 1)
                release(pe)

            def dve_(dve):
                v = chain["dve"]
                for s in sums:
                    dve.memset(s[:, :, 0:PAD], 0.0)
                for g, window in enumerate(WINDOWS):
                    h = hT[:, 2 * g:2 * g + 2, :]
                    v(dve.tensor_copy(sums[0][:, :, PAD:], h))
                    step, at = 1, 0
                    while step < window:
                        v(dve.tensor_tensor(sums[1 - at][:, :, PAD:], sums[at][:, :, PAD:],
                                            sums[at][:, :, PAD - step:PAD + S - step], ALU.add))
                        step, at = 2 * step, 1 - at
                    inverse = const("inverse_count")[:, g * S:(g + 1) * S]
                    v(dve.tensor_tensor(sums[at][:, :, PAD:], sums[at][:, :, PAD:],
                                        inverse.unsqueeze(1).to_broadcast([P, 2, S]), ALU.mult))
                    dve.tensor_tensor(pooledT[:, 2 * g:2 * g + 2, :], sums[at][:, :, PAD:], h, ALU.subtract).then_inc(pooled, 1)
                    dve.wait_ge(pooled, g + 1)
                dve.wait_ge(scale_loaded, 16)
                v(dve.tensor_tensor(row_scale, row_scale, gates[:, 0, :], ALU.mult))
                dve.wait_ge(y_ready, 4)
                for g in range(4):
                    for t in range(TT):
                        cols_ = slice(256 * g, 256 * g + 256)
                        v(dve.tensor_tensor(xn[:, t, cols_], ps[:, 4 * (g % 2) + 2 * t + g // 2, 0:256],
                                            row_scale[:, cols_], ALU.mult))
                        dve.tensor_tensor(x[:, t, cols_], x[:, t, cols_], xn[:, t, cols_], ALU.add)

            stage(pe_, act_, dve_)

        def final_norm():
            norm(None, turn=False)
            row_gain = carve()(D)
            loaded_g = sem("final_gain_loaded")

            def act_(act):
                act.dma_start(row_gain, A["norm_final_g"].partition_broadcast(P)).then_inc(loaded_g, 16)

            def dve_(dve):
                dve.wait_ge(loaded_g, 16)
                for t in range(TT):
                    dve.tensor_tensor(x[:, t, :], xn[:, t, :], row_gain, ALU.mult)

            stage(None, act_, dve_)

        residual_signals = [sem(f"residual_{n}") for n in ("gain_loaded", "summed", "meaned", "rooted")]

        def normed_residual(ready, ready0, gain_row):
            gain_loaded, summed, meaned, rooted = residual_signals
            u = uses["normed residual"]
            uses["normed residual"] += 1
            ssq, ms, rt, rstd = small[:, 8:12], small[:, 12:14], small[:, 14:16], small[:, 16:18]
            row_gain = hT[:, 0:4, :].rearrange("p k s -> p (k s)")

            def act_(act):
                act.wait_ge(ready, ready0 + 4)
                act.dma_start(row_gain, gain_row.partition_broadcast(P)).then_inc(gain_loaded, 16)
                for half in range(2):
                    for t in range(TT):
                        act.activation(xn[:, t, 512 * half:512 * half + 512], ps[:, 2 * half + t, :], ACT.Square,
                                       accum_out=ssq[:, 2 * half + t:2 * half + t + 1]).then_inc(summed, 1)
                act.wait_ge(meaned, u + 1)
                act.activation(rt, ms, ACT.Sqrt).then_inc(rooted, 1)

            def dve_(dve):
                v = chain["dve"]
                dve.wait_ge(summed, 4 * (u + 1))
                v(dve.tensor_tensor(ms, ssq[:, 0:2], ssq[:, 2:4], ALU.add))
                dve.tensor_scalar(ms, ms, 1.0 / D, EPS, ALU.mult, ALU.add).then_inc(meaned, 1)
                dve.wait_ge(rooted, u + 1)
                v(dve.reciprocal(rstd, rt))
                dve.wait_ge(gain_loaded, 16 * (u + 1))
                for half in range(2):
                    for t in range(TT):
                        cols_ = slice(512 * half, 512 * half + 512)
                        v(dve.scalar_tensor_tensor(out=xn[:, t, cols_], in0=ps[:, 2 * half + t, :], scalar=rstd[:, t:t + 1],
                                                   in1=row_gain[:, cols_], op0=ALU.mult, op1=ALU.mult))
                        dve.tensor_tensor(x[:, t, cols_], x[:, t, cols_], xn[:, t, cols_], ALU.add)
            return act_, dve_

        def project_out(tag, fT, gain_row):
            ready = sem(f"{tag}_ready")

            def pe_(pe):
                for c in range(2):
                    w = ring.take(pe, (tag, c))
                    for t in range(TT):
                        for k in range(KD):
                            ins = pe.matmul(ps[:, 2 * c + t, :], fT[:, k, t * P:(t + 1) * P], w[:, k, :],
                                            start=(k == 0), stop=(k == KD - 1))
                        ins.then_inc(ready, 1)
                    release(pe)
            act_, dve_ = normed_residual(ready, 0, gain_row)
            stage(pe_, act_, dve_)

        ffn_signals = [sem(f"ffn_{n}") for n in ("up_ready", "silu_done", "act_ready", "ready")]

        def feed_forward(layer):
            norm(col("norm_g_2", 32 * layer + 16, 8))
            w1, w3, w2 = A["ffn_w1_2"][layer], A["ffn_w3_2"][layer], A["ffn_w2_2"][layer]
            FT = F_FF // P
            chunks = [(c, min(512, F_FF - c)) for c in range(0, F_FF, 512)]
            rows = [(r, min(4, FT - r)) for r in range(0, FT, 4)]
            n0 = len(ring.units)
            for c, n in chunks:
                ring.add(("w1", c), columns(w1, c, n), KD, n)
                ring.add(("w3", c), columns(w3, c, n), KD, n)
            for r, n in rows:
                ring.add(("w2", r), w2[r * P:(r + n) * P, :].rearrange("(k p) n -> p k n", p=P), n, D)
            stream.append(stream_units(n0, len(ring.units)))
            take = carve()
            aT = take(FT, S)
            silu = take(2, S)
            up_ready, silu_done, act_ready, ready = ffn_signals
            f0 = FT * layer

            def pe_(pe):
                f = 0
                for c, n in chunks:
                    a = ring.take(pe, ("w1", c))
                    b = ring.take(pe, ("w3", c))
                    for j in range(n // P):
                        if f >= 8:
                            pe.wait_ge(act_ready, f0 + f - 7)
                        for i, w in enumerate((a, b)):
                            for k in range(KD):
                                ins = pe.matmul(ps[:, f % 8, i * S:(i + 1) * S], w[:, k, j * P:(j + 1) * P], hT[:, k, :],
                                                start=(k == 0), stop=(k == KD - 1))
                        ins.then_inc(up_ready, 1)
                        f += 1
                    pe.drain().then_inc(weights_used, 2)
                pe.wait_ge(act_ready, f0 + FT)
                for r, n in rows:
                    w = ring.take(pe, ("w2", r))
                    for k in range(n):
                        for half in range(2):
                            for t in range(TT):
                                ins = pe.matmul(ps[:, 2 * half + t, :], aT[:, r + k, t * P:(t + 1) * P],
                                                w[:, k, 512 * half:512 * half + 512], start=(r + k == 0), stop=(r + k == FT - 1))
                                if r + k == FT - 1:
                                    ins.then_inc(ready, 1)
                    release(pe)

            act_after, dve_after = normed_residual(ready, 4 * layer, A["norm_g_2"][layer, 3])

            def act_(act):
                for f in range(FT):
                    act.wait_ge(up_ready, f0 + f + 1)
                    if f >= 2:
                        act.wait_ge(act_ready, f0 + f - 1)
                    act.activation(silu[:, f % 2, :], ps[:, f % 8, 0:S], ACT.Silu).then_inc(silu_done, 1)
                act_after(act)

            def dve_(dve):
                for f in range(FT):
                    dve.wait_ge(silu_done, f0 + f + 1)
                    dve.tensor_tensor(aT[:, f, :], silu[:, f % 2, :], ps[:, f % 8, S:2 * S], ALU.mult).then_inc(act_ready, 1)
                dve_after(dve)

            stage(pe_, act_, dve_)
        def log_sigmoid_act(act, tag, negative_abs, e, out):
            step = sem(tag)
            act.activation(e, negative_abs, ACT.Exp).then_inc(step, 1)
            act.wait_ge(step, 1)
            return act.activation(out, e, ACT.Ln, bias=1.0)

        def mixer_ab():
            norm(col("norm_g_2", 0, 8))
            n0 = len(ring.units)
            for c in range(3):
                ring.add(("ab_in", c), columns(A["ab_w_in_2"][0], 512 * c, 512), KD, 512)
            ring.add(("glu",), A["ab_w_glu_2"][0].rearrange("(k p) n -> p k n", p=P), 4, 512)
            for c in range(2):
                ring.add(("ab_out", c), columns(A["ab_w_out_2"][0], 512 * c, 512), KD, 512)
            stream.append(stream_units(n0, len(ring.units)))
            take = carve()
            usT = take(4, S)
            after_us = carve()
            after_us(4, S)
            PAD = M_CONV - 1
            xm = take(4, PAD + S + 1)
            szT = take(4, S)
            xcT = take(4, S)
            conv = take(4, S)
            qkvT = take(12, S)
            v_ext = take(TT, M_HEADS, M_DIM + 1)
            h_tok = take(TT, M_HEADS, M_DIM)
            quad_w = take(3, 4, 4)
            spread = take(3, 4, P)
            w_if = take(12, 8)
            b_if = take(8)
            mixT = hT

            loads, proj_ready, xm_taken = (sem("ab_" + n) for n in ("loads", "proj_ready", "xm_taken"))

            def proj_pe(pe):
                for c in range(3):
                    w = ring.take(pe, ("ab_in", c))
                    for j in range(4):
                        n = 4 * c + j
                        if n >= 8:
                            pe.wait_ge(xm_taken, n - 7)
                        for k in range(KD):
                            ins = pe.matmul(ps[:, n % 8, 0:S], w[:, k, j * P:(j + 1) * P], hT[:, k, :],
                                            start=(k == 0), stop=(k == KD - 1))
                        ins.then_inc(proj_ready, 1)
                    release(pe)

            def proj_act(act):
                for n, name in enumerate(("ab_wq_2", "ab_wk_2", "ab_wv_2")):
                    act.dma_start(quad_w[:, n, :, :], A[name][0].rearrange("(c n) d e -> (n d) c e", c=4)).then_inc(loads, 16)
                act.dma_start(w_if, A["ab_w_if_2"][0].rearrange("(k p) n -> p k n", p=P)).then_inc(loads, 16)
                act.dma_start(b_if, A["ab_b_if_2"][0].partition_broadcast(P)).then_inc(loads, 16)
                for n in range(4, 8):
                    act.wait_ge(proj_ready, n + 1)
                    act.activation(szT[:, n - 4, :], ps[:, n, 0:S], ACT.Silu)

            def proj_dve(dve):
                v = chain["dve"]
                dve.memset(xm[:, :, 0:PAD], 0.0)
                v(dve.memset(v_ext[:, :, :, M_DIM:M_DIM + 1], 1.0))
                for n in range(4):
                    dve.wait_ge(proj_ready, n + 1)
                    dve.tensor_copy(xm[:, n, PAD:PAD + S], ps[:, n, 0:S]).then_inc(xm_taken, 1)
                dve.wait_ge(xm_taken, 4)
                for n in range(4):
                    v(dve.tensor_scalar(conv[:, n, :], xm[:, n, 0:S], col("ab_conv_w_2", n), col("ab_conv_b_2", n),
                                        ALU.mult, ALU.add))
                    for j in range(1, M_CONV):
                        v(dve.scalar_tensor_tensor(out=conv[:, n, :], in0=xm[:, n, j:j + S], scalar=col("ab_conv_w_2", 4 * j + n),
                                                   in1=conv[:, n, :], op0=ALU.mult, op1=ALU.add))
                for n in range(8, 12):
                    dve.wait_ge(proj_ready, n + 1)
                    dve.tensor_copy(usT[:, n - 8, :], ps[:, n % 8, 0:S])
                dve.wait_ge(loads, 80)
                for n in range(3):
                    shape = [P, 4, 32, 4]
                    dve.tensor_tensor(spread[:, n, :, :].rearrange("p c (n e) -> p c n e", e=4),
                                      const("quads").rearrange("p (a n) -> p a n", a=1).rearrange("p a (n e) -> p a n e", e=4).to_broadcast(shape),
                                      quad_w[:, n, :, :].unsqueeze(2).to_broadcast(shape), ALU.mult)

            stage(proj_pe, proj_act, proj_dve)

            conv_done, qkv_ready, v_ready, taken_q, taken_v, gates_ready = (
                sem("ab_" + n) for n in ("conv_done", "qkv_ready", "v_ready", "qkv_taken", "v_taken", "gates_ready"))
            pre = small[:, 20:36].rearrange("p (t n) -> p t n", t=TT)

            def qkv_act(act):
                act.activation(xcT, conv, ACT.Silu).then_inc(conv_done, 1)

            def qkv_pe(pe):
                pe.wait_ge(conv_done, 1)
                for n in range(12):
                    which, c = divmod(n, 4)
                    if n >= 6:
                        pe.wait_ge(taken_q, n - 5)
                    source = xcT[:, c, :] if which < 2 else xm[:, c, PAD:PAD + S]
                    pe.matmul(ps[:, n % 6, 0:S], spread[:, which, c, :], source, start=True, stop=True).then_inc(qkv_ready, 1)
                for c in range(4):
                    for t in range(TT):
                        ins = pe.matmul(ps[:, 6 + t, c * P:(c + 1) * P], xm[:, c, PAD + t * P:PAD + (t + 1) * P],
                                        spread[:, 2, c, :], start=True, stop=True)
                ins.then_inc(v_ready, 1)
                pe.wait_ge(taken_q, 12)
                for t in range(TT):
                    for n in range(12):
                        ins = pe.matmul(ps[:, 0, 8 * t:8 * t + 8], qkvT[:, n, t * P:(t + 1) * P], w_if[:, n, :],
                                        start=(n == 0), stop=(n == 11))
                ins.then_inc(gates_ready, 1)

            def qkv_dve(dve):
                v = chain["dve"]
                for n in range(12):
                    dve.wait_ge(qkv_ready, n + 1)
                    dve.tensor_scalar(qkvT[:, n, :], ps[:, n % 6, 0:S], M_DIM ** -0.5 if 4 <= n < 8 else 1.0, None,
                                      ALU.mult).then_inc(taken_q, 1)
                dve.wait_ge(v_ready, 1)
                for t in range(TT):
                    dve.tensor_copy(v_ext[:, t, :, 0:M_DIM], ps[:, 6 + t, :].rearrange("p (h d) -> p h d", h=4))
                dve.wait_ge(gates_ready, 1)
                dve.tensor_tensor(pre, ps[:, 0, 0:16].rearrange("p (t n) -> p t n", t=TT),
                                  b_if.unsqueeze(1).to_broadcast([P, TT, 8]), ALU.add)

            stage(qkv_pe, qkv_act, qkv_dve)

            t1, t2, t3, b_tok, a_tok, m_tok = (take(TT, 4) for _ in range(6))
            a_rows, m_rows = take(S), take(S)
            abs_ready, ln_ready, lf_ready, b_ready, a_ready, aT_ready, m_ready, mT_ready, em_ready = (
                sem("ab_" + n) for n in ("abs_ready", "ln_ready", "lf_ready", "b_ready", "a_ready", "aT_ready", "m_ready",
                                         "mT_ready", "em_ready"))

            def gate_act(act):
                act.wait_ge(abs_ready, 1)
                log_sigmoid_act(act, "ab_exp_ready", t2, t3, t2).then_inc(ln_ready, 1)
                act.wait_ge(em_ready, 1)
                act.activation(m_tok, t1, ACT.Exp, scale=-1.0)

            def gate_dve(dve):
                v = chain["dve"]
                f = pre[:, :, 4:8]
                v(dve.memset(m_rows, 0.0))
                v(dve.tensor_scalar(t2, f, -1.0, None, ALU.mult))
                dve.tensor_tensor(t2, f, t2, ALU.min).then_inc(abs_ready, 1)
                v(dve.tensor_scalar(t1, f, 0.0, None, ALU.min))
                dve.wait_ge(ln_ready, 1)
                dve.tensor_tensor(t1, t1, t2, ALU.subtract).then_inc(lf_ready, 1)
                dve.wait_ge(b_ready, 1)
                v(dve.tensor_copy(b_tok, ps[:, 0, 0:8].rearrange("p (t h) -> p t h", t=TT)))
                dve.tensor_tensor(a_tok, pre[:, :, 0:4], b_tok, ALU.subtract).then_inc(a_ready, 1)
                dve.wait_ge(aT_ready, 1)
                v(dve.tensor_copy(a_rows[0:4, :], ps[0:4, 1, 0:S]))
                v(dve.tensor_tensor_scan(m_rows[0:4, :], CONST_ONES_ROW(4), a_rows[0:4, :], 0.0, ALU.mult, ALU.max))
                dve.tensor_scalar(m_rows[0:4, :], m_rows[0:4, :], -1.0, None, ALU.mult).then_inc(m_ready, 1)
                dve.wait_ge(mT_ready, 1)
                dve.tensor_tensor(t1, b_tok, ps[:, 2, 0:2 * P].rearrange("p (t h) -> p t h", t=TT)[:, :, 0:4],
                                  ALU.subtract).then_inc(em_ready, 1)

            def gate_pe(pe):
                pe.wait_ge(lf_ready, 1)
                pe.matmul(ps[:, 0, 0:4], const("upto"), t1[:, 0, :], start=True, stop=True)
                pe.matmul(ps[:, 0, 4:8], ones, t1[:, 0, :], start=True, stop=False)
                pe.matmul(ps[:, 0, 4:8], const("upto"), t1[:, 1, :], start=False, stop=True).then_inc(b_ready, 1)
                pe.wait_ge(a_ready, 1)
                for t in range(TT):
                    ins = pe.transpose(ps[0:4, 1, t * P:(t + 1) * P], a_tok[:, t, :], ident)
                ins.then_inc(aT_ready, 1)
                pe.wait_ge(m_ready, 1)
                for t in range(TT):
                    ins = pe.transpose(ps[:, 2, t * P:(t + 1) * P], m_rows[:, t * P:(t + 1) * P], ident)
                ins.then_inc(mT_ready, 1)

            def CONST_ONES_ROW(n):
                return ones[0:n, 0:1].to_broadcast([n, S])

            stage(gate_pe, gate_act, gate_dve)

            W = 3 * P
            expd = xn[:, 0, 0:2 * W].rearrange("p (b w) -> p b w", b=2)
            weight = xn[:, 1, 0:2 * W].rearrange("p (b w) -> p b w", b=2)
            den = small[:, 36:52].rearrange("p (h t b) -> p h t b", h=4, t=2)
            qk_ready, ex_ready, w_ready, num_ready, num_taken = (
                sem("ab_" + n) for n in ("qk_ready", "ex_ready", "w_ready", "num_ready", "num_taken"))

            def heads_pe(pe):
                def scores(h):
                    if h >= 2:
                        pe.wait_ge(w_ready, h - 1)
                    qk, lg = ps[:, 2 * (h % 2), :], ps[:, 2 * (h % 2) + 1, :]
                    q, k = qkvT[:, h, :], qkvT[:, 4 + h, :]
                    pe.matmul(qk[:, 0:S], k[:, 0:P], q, start=True, stop=True)
                    pe.matmul(qk[:, S:W], k[:, P:S], q[:, P:S], start=True, stop=True)
                    head = ident[:, h:h + 1].to_broadcast([P, P])
                    pe.matmul(lg[:, 0:S], head, m_rows, start=True, stop=False)
                    pe.matmul(lg[:, 0:P], ident, const("mask_st"), start=False, stop=True)
                    pe.matmul(lg[:, S:W], head, m_rows[:, P:S], start=True, stop=False)
                    pe.matmul(lg[:, S:W], ident, const("mask_st"), start=False, stop=True).then_inc(qk_ready, 1)

                def mix(h):
                    pe.wait_ge(w_ready, h + 1)
                    if h >= 2:
                        pe.wait_ge(num_taken, h - 1)
                    o, w = ps[:, 4 + h % 2, :], weight[:, h % 2, :]
                    n = M_DIM + 1
                    pe.matmul(o[:, 0:n], w[:, 0:P], v_ext[:, 0, h, :], start=True, stop=True)
                    pe.matmul(o[:, 256:256 + n], w[:, P:S], v_ext[:, 0, h, :], start=True, stop=False)
                    pe.matmul(o[:, 256:256 + n], w[:, S:W], v_ext[:, 1, h, :], start=False, stop=True).then_inc(num_ready, 1)
                scores(0)
                for h in range(4):
                    if h < 3:
                        scores(h + 1)
                    mix(h)

            def heads_act(act):
                for h in range(4):
                    act.wait_ge(qk_ready, h + 1)
                    if h >= 2:
                        act.wait_ge(w_ready, h - 1)
                    lg = ps[:, 2 * (h % 2) + 1, :]
                    act.activation(expd[:, h % 2, 0:S], lg[:, 0:S], ACT.Exp, bias=a_tok[:, 0, h:h + 1])
                    act.activation(expd[:, h % 2, S:W], lg[:, S:W], ACT.Exp, bias=a_tok[:, 1, h:h + 1]).then_inc(ex_ready, 1)

            def heads_dve(dve):
                v = chain["dve"]

                def finish(h):
                    dve.wait_ge(num_ready, h + 1)
                    o = ps[:, 4 + h % 2, :].rearrange("p (t n) -> p t n", t=TT)
                    d, r = den[:, h, :, 0], den[:, h, :, 1]
                    v(dve.tensor_copy(r, o[:, :, M_DIM]))
                    v(dve.scalar_tensor_tensor(out=d, in0=r, scalar=-1.0, in1=r, op0=ALU.mult, op1=ALU.max))
                    v(dve.tensor_tensor(d, d, m_tok[:, :, h], ALU.max))
                    v(dve.reciprocal(r, d))
                    for t in range(TT):
                        ins = dve.tensor_scalar(h_tok[:, t, h, :], o[:, t, 0:M_DIM], r[:, t:t + 1], None, ALU.mult)
                    ins.then_inc(num_taken, 1)
                for h in range(4):
                    dve.wait_ge(ex_ready, h + 1)
                    if h >= 2:
                        dve.wait_ge(num_ready, h - 1)
                    dve.tensor_tensor(weight[:, h % 2, :], expd[:, h % 2, :], ps[:, 2 * (h % 2), 0:W], ALU.mult).then_inc(w_ready, 1)
                    if h:
                        finish(h - 1)
                finish(3)

            stage(heads_pe, heads_act, heads_dve)

            stats = xn[:, 0, 0:48].rearrange("p (t h n) -> p t h n", t=2, h=4)
            mean_var = xn[:, 0, 64:80].rearrange("p (t h n) -> p t h n", t=2, h=4)
            sd = xn[:, 0, 96:104].rearrange("p (t h) -> p t h", t=2)
            rstd = xn[:, 0, 112:120].rearrange("p (t h) -> p t h", t=2)
            var_ready, sd_ready, hn_ready, hnT_ready = (sem("ab_" + n) for n in ("var_ready", "sd_ready", "hn_ready", "hnT_ready"))

            def ln_dve(dve):
                v = chain["dve"]
                for t in range(TT):
                    for h in range(4):
                        v(dve.bn_stats(stats[:, t, h, :], h_tok[:, t, h, :]))
                        v(dve.bn_aggr(mean_var[:, t, h, :], stats[:, t, h, :]))
                dve.tensor_scalar(sd, mean_var[:, :, :, 1], EPS, None, ALU.add).then_inc(var_ready, 1)
                dve.wait_ge(sd_ready, 1)
                v(dve.reciprocal(rstd, sd))
                for t in range(TT):
                    for h in range(4):
                        dve.tensor_scalar(h_tok[:, t, h, :], h_tok[:, t, h, :], mean_var[:, t, h, 0:1], rstd[:, t, h:h + 1],
                                          ALU.subtract, ALU.mult).then_inc(hn_ready, 1)
                for h in range(4):
                    ins = dve.tensor_scalar(conv[:, h, :], xcT[:, h, :], col("ab_skip_2", h), None, ALU.mult)
                v(ins)
                dve.wait_ge(hnT_ready, 1)
                for h in range(4):
                    v(dve.scalar_tensor_tensor(out=conv[:, h, :], in0=ps[:, h, 0:S], scalar=col("ab_mh_gain_2", h),
                                               in1=conv[:, h, :], op0=ALU.mult, op1=ALU.add))
                    dve.tensor_tensor(mixT[:, h, :], conv[:, h, :], szT[:, h, :], ALU.mult)

            def ln_act(act):
                act.wait_ge(var_ready, 1)
                act.activation(sd, sd, ACT.Sqrt).then_inc(sd_ready, 1)

            def ln_pe(pe):
                pe.wait_ge(hn_ready, 8)
                for h in range(4):
                    for t in range(TT):
                        ins = pe.transpose(ps[:, h, t * P:(t + 1) * P], h_tok[:, t, h, :], ident)
                ins.then_inc(hnT_ready, 1)

            stage(ln_pe, ln_act, ln_dve)

            take = after_us
            cosT, sinT = take(S_PAIRS, S), take(S_PAIRS, S)
            half_tmp = take(S_PAIRS, P)
            BT = take(2, 4, P)
            CT = take(2, 4, P)
            par = take(5, P)
            pc = take(5, S_PAIRS)
            turn_c, turn_s, turn_t = take(S_PAIRS), take(S_PAIRS), take(S_PAIRS)
            yT = xn[:, 1, :].rearrange("p (k s) -> p k s", k=4)
            r16 = xn[:, 0, :].rearrange("p (n c) -> p n c", n=8)
            b_in = cosT[:, 0:2, :].rearrange("p a (g n) -> p a g n", n=S_GROUP)
            bb = cosT[:, 2:4, :].rearrange("p a (g n) -> p a g n", n=S_GROUP)
            b_tmp = cosT[:, 4, :].rearrange("p (g n) -> p g n", n=S_GROUP)
            b_wide = cosT[:, 6:10, :].rearrange("p (a b) s -> p a (b s)", a=2)
            c_in = cosT[:, 10:12, :].rearrange("p a (g n) -> p a g n", n=S_STATE)
            c_wide = sinT[:, 0:4, :].rearrange("p (a b) s -> p a (b s)", a=2)
            (s5_loaded, dt_ready, args_ready, sc_ready, par_ready, par_turned, wide_ready, wide_turned) = (
                sem("s5_" + n) for n in ("loaded", "dt_ready", "args_ready", "sc_ready", "par_ready", "par_turned",
                                         "wide_ready", "wide_turned"))
            R = S_PAIRS
            a_re, a_im, ldt, dt, x1, x2, x3, x4 = (r16[0:R, n, :] for n in range(8))
            rowp = [par[0:R, n, :] for n in range(5)]

            def s5_act(act):
                act.dma_start(a_re, A["ab_a_re_2"][0].rearrange("(r g) n -> r (g n)", g=2)).then_inc(s5_loaded, 16)
                act.dma_start(a_im, A["ab_a_im_2"][0].rearrange("(r g) n -> r (g n)", g=2)).then_inc(s5_loaded, 16)
                act.dma_start(ldt[:, 0:2], A["ab_log_dt_2"][0].rearrange("(r g) -> r g", g=2)).then_inc(s5_loaded, 16)
                for n, name in enumerate(("ab_b_re_2", "ab_b_im_2")):
                    act.dma_start(b_in[:, n, :, :], A[name][0].rearrange("(r g) n p -> (g n) r p", g=2)).then_inc(s5_loaded, 16)
                for n, name in enumerate(("ab_c_re_2", "ab_c_im_2")):
                    act.dma_start(c_in[:, n, :, :], A[name][0].rearrange("(c g) p n -> (g p) c n", c=4)).then_inc(s5_loaded, 16)
                act.wait_ge(s5_loaded, 112)
                act.activation(ldt[:, 2:4], ldt[:, 0:2], ACT.Exp).then_inc(dt_ready, 1)
                act.wait_ge(args_ready, 1)
                act.activation(rowp[0], x1, ACT.Exp)
                act.activation(rowp[2], x2, ACT.Sin)
                act.activation(rowp[1], x3, ACT.Sin).then_inc(sc_ready, 1)

            TWO_PI = 2 * np.pi
            C1 = 6.28125
            C2 = float(np.float32(np.round((TWO_PI - C1) * 2 ** 20) / 2 ** 20))
            C3 = float(np.float32(TWO_PI - C1 - C2))
            ROUND = 1.5 * 2 ** 23
            PI_DOWN = 3.1415925

            def s5_dve(dve):
                v = chain["dve"]
                v(dve.memset(par, 0.0))
                dve.wait_ge(dt_ready, 1)
                v(dve.tensor_copy(dt.rearrange("p (g n) -> p g n", g=2), ldt[:, 2:4].unsqueeze(2).to_broadcast([R, 2, S_STATE])))
                v(dve.tensor_tensor(x1, a_re, dt, ALU.mult))
                v(dve.tensor_tensor(x2, a_im, dt, ALU.mult))
                v(dve.tensor_scalar(x3, x2, 1.0 / TWO_PI, None, ALU.mult))
                v(dve.tensor_scalar(x3, x3, ROUND, None, ALU.add))
                v(dve.tensor_scalar(x3, x3, -ROUND, None, ALU.add))
                for c in (C1, C2, C3):
                    v(dve.scalar_tensor_tensor(out=x2, in0=x3, scalar=-c, in1=x2, op0=ALU.mult, op1=ALU.add))
                v(dve.tensor_scalar(x2, x2, PI_DOWN, -PI_DOWN, ALU.min, ALU.max))
                v(dve.scalar_tensor_tensor(out=x3, in0=x2, scalar=-1.0, in1=x2, op0=ALU.mult, op1=ALU.max))
                dve.tensor_scalar(x3, x3, -1.0, float(np.pi / 2), ALU.mult, ALU.add).then_inc(args_ready, 1)
                dve.wait_ge(sc_ready, 1)
                v(dve.tensor_tensor(x1, rowp[0], rowp[1], ALU.mult))
                v(dve.tensor_scalar(x1, x1, -1.0, None, ALU.add))
                v(dve.tensor_tensor(x2, rowp[0], rowp[2], ALU.mult))
                v(dve.tensor_tensor(x3, a_re, a_re, ALU.mult))
                v(dve.tensor_tensor(x4, a_im, a_im, ALU.mult))
                v(dve.tensor_tensor(x3, x3, x4, ALU.add))
                v(dve.reciprocal(dt, x3))
                v(dve.tensor_tensor(x3, x1, a_re, ALU.mult))
                v(dve.tensor_tensor(x4, x2, a_im, ALU.mult))
                v(dve.tensor_tensor(x3, x3, x4, ALU.add))
                v(dve.tensor_tensor(rowp[3], x3, dt, ALU.mult))
                v(dve.tensor_tensor(x3, x2, a_re, ALU.mult))
                v(dve.tensor_tensor(x4, x1, a_im, ALU.mult))
                v(dve.tensor_tensor(x3, x3, x4, ALU.subtract))
                dve.tensor_tensor(rowp[4], x3, dt, ALU.mult).then_inc(par_ready, 1)
                dve.wait_ge(par_turned, 1)
                v(dve.tensor_copy(pc[:, 0:4, :], ps[:, 0, :].rearrange("p (n c) -> p n c", n=4)[:, :, 0:R]))
                v(dve.tensor_copy(pc[:, 4, :], ps[:, 1, 0:R]))
                shape = [P, R, S_GROUP]
                g_re, g_im = (pc[:, n, :].unsqueeze(2).to_broadcast(shape) for n in (3, 4))
                v(dve.tensor_tensor(bb[:, 0], b_in[:, 0], g_re, ALU.mult))
                v(dve.tensor_tensor(b_tmp, b_in[:, 1], g_im, ALU.mult))
                v(dve.tensor_tensor(bb[:, 0], bb[:, 0], b_tmp, ALU.subtract))
                v(dve.tensor_tensor(bb[:, 1], b_in[:, 1], g_re, ALU.mult))
                v(dve.tensor_tensor(b_tmp, b_in[:, 0], g_im, ALU.mult))
                v(dve.tensor_tensor(bb[:, 1], bb[:, 1], b_tmp, ALU.add))
                for n in range(2):
                    wide = b_wide[:, n, :].rearrange("p (r g c) -> p r g c", r=R, g=2)
                    for g in range(2):
                        v(dve.tensor_scalar(wide[:, :, g, :], bb[:, n], const("half")[:, g:g + 1], None, ALU.mult))
                    wide = c_wide[:, n, :].rearrange("p (c g n) -> p c g n", c=4, g=2)
                    for g in range(2):
                        ins = dve.tensor_scalar(wide[:, :, g, :], c_in[:, n], const("odd16")[:, g:g + 1], 1.0 - 2.0 * n,
                                                ALU.mult, ALU.mult)
                        if n or g:
                            pass
                        v(ins) if not (n and g) else ins.then_inc(wide_ready, 1)
                dve.wait_ge(wide_turned, 1)
                for n in range(2):
                    dve.tensor_copy(BT[:, n], ps[:, 2 + n, :].rearrange("p (c n) -> p c n", c=4))
                    ins = dve.tensor_copy(CT[:, n], ps[:, 4 + n, :].rearrange("p (c n) -> p c n", c=4))
                v(ins)
                v(dve.memset(cosT[:, :, 0:1], 1.0))
                v(dve.memset(sinT[:, :, 0:1], 0.0))
                v(dve.tensor_copy(turn_c, pc[:, 1, :]))
                v(dve.tensor_copy(turn_s, pc[:, 2, :]))
                m = 1
                while m < S:
                    shape = [P, R, m]
                    c, s = (a.unsqueeze(2).to_broadcast(shape) for a in (turn_c, turn_s))
                    co, si, tmp = cosT[:, :, 0:m], sinT[:, :, 0:m], half_tmp[:, :, 0:m]
                    v(dve.tensor_tensor(tmp, si, s, ALU.mult))
                    v(dve.tensor_tensor(cosT[:, :, m:2 * m], co, c, ALU.mult))
                    v(dve.tensor_tensor(cosT[:, :, m:2 * m], cosT[:, :, m:2 * m], tmp, ALU.subtract))
                    v(dve.tensor_tensor(tmp, co, s, ALU.mult))
                    v(dve.tensor_tensor(sinT[:, :, m:2 * m], si, c, ALU.mult))
                    v(dve.tensor_tensor(sinT[:, :, m:2 * m], sinT[:, :, m:2 * m], tmp, ALU.add))
                    m *= 2
                    if m < S:
                        v(dve.tensor_tensor(turn_t, turn_s, turn_c, ALU.mult))
                        v(dve.tensor_tensor(turn_c, turn_c, turn_c, ALU.mult))
                        v(dve.tensor_tensor(turn_s, turn_s, turn_s, ALU.mult))
                        v(dve.tensor_tensor(turn_c, turn_c, turn_s, ALU.subtract))
                        v(dve.tensor_scalar(turn_s, turn_t, 2.0, None, ALU.mult))

            def s5_pe(pe):
                pe.wait_ge(par_ready, 1)
                for n in range(5):
                    ins = pe.transpose(ps[:, n // 4, (n % 4) * P:(n % 4 + 1) * P], par[:, n, :], ident)
                ins.then_inc(par_turned, 1)
                pe.wait_ge(wide_ready, 1)
                for n in range(2):
                    for c in range(4):
                        pe.transpose(ps[:, 2 + n, c * P:(c + 1) * P], b_wide[:, n, c * P:(c + 1) * P], ident)
                        ins = pe.transpose(ps[:, 4 + n, c * P:(c + 1) * P], c_wide[:, n, c * P:(c + 1) * P], ident)
                ins.then_inc(wide_turned, 1)

            stage(s5_pe, s5_act, s5_dve)

            take = after_us
            z = half_tmp.rearrange("p (a q) s -> p a (q s)", a=2).rearrange("p a (q s) -> p a q s", q=4)
            bu_ready, bu_taken, x_ready, y_ready, g_in, g_done = (
                sem("s5_" + n) for n in ("bu_ready", "bu_taken", "x_ready", "y_ready", "gelu_in", "gelu_done"))
            t_re, t_im = (xn[:, 0, 0:4 * S].rearrange("p (q s) -> p q s", q=4), arena_tail(4, S))
            y_in = gates[:, 0, 0:2 * S].rearrange("p (b s) -> p b s", b=2)

            def quarter_pe(pe):
                def states(c):
                    if c:
                        pe.wait_ge(bu_taken, c)
                    for q in range(4):
                        rows = slice(32 * q, 32 * q + 32)
                        for n in range(2):
                            ins = pe.matmul(ps[:, q, n * S:(n + 1) * S], BT[rows, n, c, :], usT[rows, c, :], start=True, stop=True)
                    ins.then_inc(bu_ready, 1)

                def outputs(c):
                    pe.wait_ge(x_ready, c + 1)
                    if c >= 2:
                        pe.wait_ge(g_in, c - 1)
                    for q in range(4):
                        o = ps[32 * q:32 * q + 32, 4 + c % 2, 0:S]
                        pe.matmul(o, CT[:, 0, c, 32 * q:32 * q + 32], z[:, 0, q, :], start=True, stop=False)
                        ins = pe.matmul(o, CT[:, 1, c, 32 * q:32 * q + 32], z[:, 1, q, :], start=False, stop=True)
                    ins.then_inc(y_ready, 1)
                states(0)
                for c in range(4):
                    if c < 3:
                        states(c + 1)
                    outputs(c)

            def quarter_dve(dve):
                v = chain["dve"]
                for c in range(4):
                    co, si = cosT[:, 4 * c:4 * c + 4, :], sinT[:, 4 * c:4 * c + 4, :]
                    re, im = ps[:, 0:4, 0:S], ps[:, 0:4, S:2 * S]
                    if c:
                        dve.wait_ge(y_ready, c)
                    dve.wait_ge(bu_ready, c + 1)
                    dve.tensor_tensor(z[:, 0], re, co, ALU.mult)
                    dve.tensor_tensor(z[:, 1], im, co, ALU.mult)
                    dve.tensor_tensor(t_re, im, si, ALU.mult)
                    dve.tensor_tensor(t_im, re, si, ALU.mult).then_inc(bu_taken, 1)
                    dve.wait_ge(bu_taken, c + 1)
                    dve.tensor_tensor(z[:, 0], z[:, 0], t_re, ALU.add)
                    v(dve.tensor_tensor(z[:, 1], z[:, 1], t_im, ALU.subtract))
                    for q in range(4):
                        decay = pc[:, 0, 4 * c + q:4 * c + q + 1].to_broadcast([P, S])
                        dve.tensor_tensor_scan(t_re[:, q, :], decay, z[:, 0, q, :], 0.0, ALU.mult, ALU.add)
                        ins = dve.tensor_tensor_scan(t_im[:, q, :], decay, z[:, 1, q, :], 0.0, ALU.mult, ALU.add)
                    v(ins)
                    dve.tensor_tensor(z[:, 0], t_re, co, ALU.mult)
                    v(dve.tensor_tensor(z[:, 1], t_im, co, ALU.mult))
                    v(dve.tensor_tensor(t_re, t_re, si, ALU.mult))
                    v(dve.tensor_tensor(t_im, t_im, si, ALU.mult))
                    v(dve.tensor_tensor(z[:, 0], z[:, 0], t_im, ALU.subtract))
                    dve.tensor_tensor(z[:, 1], z[:, 1], t_re, ALU.add).then_inc(x_ready, 1)
                    dve.wait_ge(y_ready, c + 1)
                    if c >= 2:
                        dve.wait_ge(g_done, c - 1)
                    dve.scalar_tensor_tensor(out=y_in[:, c % 2, :], in0=usT[:, c, :], scalar=col("ab_d_2", c),
                                             in1=ps[:, 4 + c % 2, 0:S], op0=ALU.mult, op1=ALU.add).then_inc(g_in, 1)

            def quarter_act(act):
                for c in range(4):
                    act.wait_ge(g_in, c + 1)
                    act.activation(yT[:, c, :], y_in[:, c % 2, :], ACT.Gelu_apprx_tanh).then_inc(g_done, 1)

            stage(quarter_pe, quarter_act, quarter_dve)

            glu_ready, sig_ready = sem("glu_ready"), sem("glu_sig_ready")
            sig = xn[:, 0, :].rearrange("p (k s) -> p k s", k=4)

            def glu_pe(pe):
                w = ring.take(pe, ("glu",))
                for n in range(4):
                    for k in range(4):
                        ins = pe.matmul(ps[:, n, 0:S], w[:, k, n * P:(n + 1) * P], yT[:, k, :], start=(k == 0), stop=(k == 3))
                    ins.then_inc(glu_ready, 1)
                release(pe)

            def glu_act(act):
                for n in range(4):
                    act.wait_ge(glu_ready, n + 1)
                    act.activation(sig[:, n, :], ps[:, n, 0:S], ACT.Sigmoid, bias=col("ab_b_glu_2", n)).then_inc(sig_ready, 1)

            def glu_dve(dve):
                for n in range(4):
                    dve.wait_ge(sig_ready, n + 1)
                    dve.tensor_tensor(mixT[:, 4 + n, :], yT[:, n, :], sig[:, n, :], ALU.mult)

            stage(glu_pe, glu_act, glu_dve)
            project_out("ab_out", mixT, A["norm_g_2"][0, 1])

        def arena_tail(*shape):
            n = int(np.prod(shape))
            return arena[:, 17 * 1024 - n:17 * 1024].rearrange("p (a b) -> p a b", a=shape[0])

        def mixer_c():
            norm(col("norm_g_2", 32, 8))
            n0 = len(ring.units)
            for c in range(8):
                ring.add(("c_in", c), columns(A["c_w_in_2"][0], 512 * c, 512), KD, 512)
            for c in range(2):
                ring.add(("c_out", c), columns(A["c_w_out_2"][0], 512 * c, 512), KD, 512)
            stream.append(stream_units(n0, len(ring.units)))
            take = carve()
            qT, kT, v_tok, gT, b = (take(8, S), take(8, S), take(TT, D), take(8, S), take(8, S))
            e_in, e_state, e_intra = (take(8, S) for _ in range(3))
            lb, lb1, p0, p1, pm = (take(8) for _ in range(5))
            b_last, decay = take(8, 4), take(8, 4)
            ready, taken_a, taken_d, lb_in, lb_exp = (sem("c_" + n) for n in ("proj_ready", "taken_act", "taken_dve", "lb_in", "lb_exp"))
            tiles = [("q", n) for n in range(8)] + [("f", n) for n in range(8)] + \
                    [("i", n) for n in range(4)] + [("g", n) for n in range(8)]
            by_act = [n for n, (kind, _) in enumerate(tiles) if kind != "i"]
            by_dve = [n for n, (kind, _) in enumerate(tiles) if kind == "i"]

            def wait_bank(pe, n):
                if n >= 8:
                    m = n - 8
                    if m in by_act:
                        pe.wait_ge(taken_a, by_act.index(m) + 1)
                    else:
                        pe.wait_ge(taken_d, by_dve.index(m) + 1)

            def proj_pe(pe):
                n = 0
                for c in range(8):
                    w = ring.take(pe, ("c_in", c))
                    if c in (4, 5):
                        for t in range(TT):
                            wait_bank(pe, n)
                            for k in range(KD):
                                ins = pe.matmul(ps[:, n % 8, :], hT[:, k, t * P:(t + 1) * P], w[:, k, :],
                                                start=(k == 0), stop=(k == KD - 1))
                            ins.then_inc(ready, 1)
                            n += 1
                    else:
                        for j in range(4):
                            wait_bank(pe, n)
                            for k in range(KD):
                                ins = pe.matmul(ps[:, n % 8, 0:S], w[:, k, j * P:(j + 1) * P], hT[:, k, :],
                                                start=(k == 0), stop=(k == KD - 1))
                            ins.then_inc(ready, 1)
                            n += 1
                    release(pe)

            def proj_act(act):
                act.wait_ge(lb_in, 1)
                act.activation(p0, p0, ACT.Exp)
                act.activation(p1, p1, ACT.Exp).then_inc(lb_exp, 1)
                for n in by_act:
                    kind, i = tiles[n]
                    act.wait_ge(ready, n + 1)
                    o, f = {"q": (qT, ACT.Silu), "f": (kT, ACT.Sigmoid), "g": (gT, ACT.Silu)}[kind]
                    act.activation(o[:, i, :], ps[:, n % 8, 0:S], f).then_inc(taken_a, 1)

            def proj_dve(dve):
                v = chain["dve"]
                r0, r1 = col("c_lb_raw_2", 0, 8), col("c_lb_raw_2", 8, 8)
                v(dve.tensor_tensor(pm, r0, r1, ALU.max))
                v(dve.tensor_tensor(p0, r0, pm, ALU.subtract))
                dve.tensor_tensor(p1, r1, pm, ALU.subtract).then_inc(lb_in, 1)
                dve.wait_ge(lb_exp, 1)
                v(dve.tensor_tensor(pm, p0, p1, ALU.add))
                v(dve.reciprocal(pm, pm))
                v(dve.tensor_tensor(p0, p0, pm, ALU.mult))
                v(dve.tensor_tensor(p1, p1, pm, ALU.mult))
                v(dve.tensor_tensor(lb, p0, p1, ALU.add))
                v(dve.tensor_tensor(lb, lb, p0, ALU.subtract))
                v(dve.tensor_scalar(lb1, lb, -1.0, 1.0, ALU.mult, ALU.add))
                dve.wait_ge(taken_a, 16)
                for h in range(8):
                    ins = dve.tensor_scalar(b[:, h, :], kT[:, h, :], lb1[:, h:h + 1], lb[:, h:h + 1], ALU.mult, ALU.add)
                v(ins)
                v(dve.tensor_scalar(kT, b, -1.0, 1.0, ALU.mult, ALU.add))
                for n in by_dve:
                    _, i = tiles[n]
                    dve.wait_ge(ready, n + 1)
                    c, t = divmod(i, 2)
                    dve.tensor_copy(v_tok[:, t, c * 512:(c + 1) * 512], ps[:, n % 8, :]).then_inc(taken_d, 1)
                dve.wait_ge(taken_a, 24)
                for h in range(8):
                    dve.tensor_scalar(gT[:, h, :], gT[:, h, :], col("c_g_gain_2", h), None, ALU.mult)

            stage(proj_pe, proj_act, proj_dve)

            log_ready, b_ready, e_ready, d_ready = (sem("c_" + n) for n in ("log_ready", "b_ready", "e_ready", "d_ready"))
            chunks = "p h (c s) -> p h c s"

            def decay_act(act):
                for h in range(8):
                    act.activation(e_in[:, h, :], b[:, h, :], ACT.Ln).then_inc(log_ready, 1)
                act.wait_ge(b_ready, 1)
                act.activation(e_in, b, ACT.Exp)
                act.activation(decay, b_last, ACT.Exp).then_inc(e_ready, 1)
                act.wait_ge(d_ready, 1)
                act.activation(e_state, b, ACT.Exp, scale=-1.0).then_inc(e_ready, 1)
                act.activation(e_intra, b, ACT.Exp).then_inc(e_ready, 1)

            def decay_dve(dve):
                v = chain["dve"]
                for h in range(8):
                    dve.wait_ge(log_ready, h + 1)
                    ins = dve.tensor_tensor_scan(b[:, h, :], const("restart"), e_in[:, h, :], 0.0, ALU.mult, ALU.add)
                v(ins)
                wide = b.rearrange(chunks, c=4)
                dve.tensor_copy(b_last, wide[:, :, :, H_CHUNK - 1]).then_inc(b_ready, 1)
                dve.wait_ge(e_ready, 1)
                for h in range(8):
                    ins = dve.tensor_tensor(wide[:, h], wide[:, h], b_last[:, h, :].unsqueeze(2).to_broadcast([P, 4, H_CHUNK]),
                                            ALU.subtract)
                ins.then_inc(d_ready, 1)
                dve.tensor_tensor(e_in, e_in, qT, ALU.mult)
                dve.wait_ge(e_ready, 2)
                dve.tensor_tensor(e_state, e_state, kT, ALU.mult)
                dve.wait_ge(e_ready, 3)
                v(dve.tensor_tensor(e_intra, e_intra, qT, ALU.mult))
                dve.memset(b, 0.0)

            stage(None, decay_act, decay_dve)

            flat = b.rearrange("p h s -> p (h s)")
            sc = flat[:, 0:512].rearrange("p (b t c) -> p b t c", b=2, t=TT)
            state = flat[:, 512:512 + 768].rearrange("p (b n c) -> p b n c", b=2, n=3)
            k_tok = flat[:, 1280:1280 + 512].rearrange("p (b t c) -> p b t c", b=2, t=TT)
            ssq = small[:, 0:16].rearrange("p (t h) -> p t h", t=TT)
            mask = const("bits_chunk").bitcast(U32)
            k_ready, k_taken, s_ready, s_taken, u_ready, states, o_ready, o_summed, o_taken = (
                sem("c_" + n) for n in ("k_ready", "k_taken", "s_ready", "s_taken", "u_ready", "states", "o_ready", "o_summed",
                                        "o_taken"))

            def heads_pe(pe):
                def first(h):
                    if h >= 2:
                        pe.wait_ge(k_taken, h - 1)
                        pe.wait_ge(s_taken, h - 1)
                    for t in range(TT):
                        ins = pe.transpose(ps[:, h % 2, t * P:(t + 1) * P], e_state[:, h, t * P:(t + 1) * P], ident)
                    ins.then_inc(k_ready, 1)
                    for t in range(TT):
                        cols_ = slice(t * P, t * P + P)
                        ins = pe.matmul(ps[:, 2 + h % 2, cols_], e_state[:, h, cols_], e_intra[:, h, cols_], start=True, stop=True)
                    ins.then_inc(s_ready, 1)

                def second(h):
                    head = slice(h * P, (h + 1) * P)
                    pe.wait_ge(k_taken, h + 1)
                    if h:
                        pe.wait_ge(states, h)
                    for c, (bank, at) in enumerate(((4, 0), (5, 0), (4, P))):
                        rows = slice(64 * (c % 2), 64 * (c % 2) + 64)
                        ins = pe.matmul(ps[:, bank, at:at + P], k_tok[rows, h % 2, c // 2, :], v_tok[rows, c // 2, head],
                                        start=True, stop=True)
                    ins.then_inc(u_ready, 1)
                    pe.wait_ge(s_taken, h + 1)
                    if h >= 2:
                        pe.wait_ge(o_taken, h - 1)
                    pe.wait_ge(states, h + 1)
                    for t in range(TT):
                        o = ps[:, 6 + h % 2, t * P:(t + 1) * P]
                        pe.matmul(o, sc[:, h % 2, t, :], v_tok[:, t, head], start=True, stop=False, skip_group_check=True)
                        for c in range(2 * t, 2 * t + 2):
                            if c:
                                r = 64 * (c % 2)
                                ins = pe.matmul(ps[r:r + 64, 6 + h % 2, t * P:(t + 1) * P], e_in[:, h, c * 64:(c + 1) * 64],
                                                state[:, h % 2, c - 1, :], start=False, stop=True, skip_group_check=True)
                    ins.then_inc(o_ready, 1)

                first(0)
                for h in range(8):
                    if h < 7:
                        first(h + 1)
                    second(h)

            def heads_act(act):
                for h in range(8):
                    act.wait_ge(k_ready, h + 1)
                    if h >= 2:
                        act.wait_ge(u_ready, h - 1)
                    act.copy(k_tok[:, h % 2], ps[:, h % 2, 0:S].rearrange("p (t c) -> p t c", t=TT)).then_inc(k_taken, 1)
                    if h:
                        square(act, h - 1)
                square(act, 7)

            def square(act, h):
                act.wait_ge(o_ready, h + 1)
                if h:
                    act.wait_ge(o_summed, h)
                for t in range(TT):
                    ins = act.activation(flat[:, 1792 + t * P:1792 + (t + 1) * P], ps[:, 6 + h % 2, t * P:(t + 1) * P], ACT.Square,
                                         accum_out=ssq[:, t, h:h + 1])
                ins.then_inc(o_summed, 1)

            def heads_dve(dve):
                v = chain["dve"]

                def finish(h):
                    dve.wait_ge(o_summed, h + 1)
                    dve.tensor_copy(xn[:, :, h * P:(h + 1) * P], ps[:, 6 + h % 2, 0:S].rearrange("p (t c) -> p t c", t=TT))\
                        .then_inc(o_taken, 1)
                for h in range(8):
                    dve.wait_ge(s_ready, h + 1)
                    if h >= 2:
                        dve.wait_ge(o_ready, h - 1)
                    for t in range(TT):
                        ins = dve.copy_predicated(sc[:, h % 2, t, :], mask, ps[:, 2 + h % 2, t * P:(t + 1) * P])
                    ins.then_inc(s_taken, 1)
                    dve.wait_ge(u_ready, h + 1)
                    st = state[:, h % 2]
                    v(dve.tensor_copy(st[:, 0, :], ps[:, 4, 0:P]))
                    v(dve.scalar_tensor_tensor(out=st[:, 1, :], in0=st[:, 0, :], scalar=decay[:, h, 1:2], in1=ps[:, 5, 0:P],
                                               op0=ALU.mult, op1=ALU.add))
                    dve.scalar_tensor_tensor(out=st[:, 2, :], in0=st[:, 1, :], scalar=decay[:, h, 2:3], in1=ps[:, 4, P:2 * P],
                                             op0=ALU.mult, op1=ALU.add).then_inc(states, 1)
                    if h:
                        finish(h - 1)
                finish(7)

            stage(heads_pe, heads_act, heads_dve)

            ms = small[:, 16:32].rearrange("p (t h) -> p t h", t=TT)
            rstd = small[:, 32:48].rearrange("p (t h) -> p t h", t=TT)
            ms_ready, rt_ready, o_scaled, oT_ready = (sem("c_" + n) for n in ("ms_ready", "rt_ready", "o_scaled", "oT_ready"))

            def out_dve(dve):
                v = chain["dve"]
                dve.tensor_scalar(ms, ssq, 1.0 / P, EPS, ALU.mult, ALU.add).then_inc(ms_ready, 1)
                dve.wait_ge(rt_ready, 1)
                v(dve.reciprocal(rstd, ms))
                for t in range(TT):
                    o = xn[:, t, :].rearrange("p (h c) -> p h c", h=8)
                    dve.tensor_tensor(o, o, rstd[:, t, :].unsqueeze(2).to_broadcast([P, 8, P]), ALU.mult).then_inc(o_scaled, 1)
                for bank in range(4):
                    dve.wait_ge(oT_ready, bank + 1)
                    dve.tensor_tensor(hT[:, 2 * bank:2 * bank + 2, :], ps[:, bank, :].rearrange("p (k s) -> p k s", k=2),
                                      gT[:, 2 * bank:2 * bank + 2, :], ALU.mult)

            def out_act(act):
                act.wait_ge(ms_ready, 1)
                act.activation(ms, ms, ACT.Sqrt).then_inc(rt_ready, 1)

            def out_pe(pe):
                pe.wait_ge(o_scaled, 2)
                for k in range(KD):
                    for t in range(TT):
                        ins = pe.transpose(ps[:, k // 2, (k % 2) * S + t * P:(k % 2) * S + (t + 1) * P],
                                           xn[:, t, k * P:(k + 1) * P], ident)
                    if k % 2:
                        ins.then_inc(oT_ready, 1)

            stage(out_pe, out_act, out_dve)
            project_out("c_out", hT, A["norm_g_2"][1, 1])

        for name in STAGES:
            if name == "layer0":
                conditioning(0)
                norm(gain[:, 0, 0, :], mod[:, 0, 0, :], gates_of=0)
                attention()
            elif name == "moe0":
                experts(0)
            elif name == "layer1":
                norm(gain[:, 1, 0, :], mod[:, 1, 0, :], gates_of=1)
                pooling()
            elif name == "moe1":
                experts(1)
            elif name == "final":
                final_norm()
            elif name == "mixer_ab":
                mixer_ab()
            elif name == "ffn0":
                feed_forward(0)
            elif name == "mixer_c":
                mixer_c()
            elif name == "ffn1":
                feed_forward(1)
            elif name == "cond0":
                conditioning(0)
                norm(gain[:, 0, 0, :], mod[:, 0, 0, :], gates_of=0)
            elif name == "cond1":
                conditioning(1)
                norm(gain[:, 1, 0, :], mod[:, 1, 0, :], gates_of=1)

        out_written = sem("out_written")
        n_stages = len(programs["pe"])
        block = ctx.enter_context(nc.Block())

        @block.sync
        def _(sp):
            for step in stream:
                step(sp)
            sp.wait_ge(stage_done, 4 * n_stages)
            sp.dma_start(out[0].rearrange("(t p) d -> p t d", p=P), x[:, :, :]).then_inc(out_written, 16)
            sp.wait_ge(out_written, 16)

        @block.tensor
        def _(pe):
            run_stages("pe", pe)

        @block.scalar
        def _(act):
            run_stages("act", act)

        @block.vector
        def _(dve):
            chain["dve"] = Chain(dve, dve_step)
            run_stages("dve", dve)

        @block.gpsimd
        def _(pool):
            run_stages("pool", pool)


STAGES = ["layer0", "moe0", "layer1", "moe1", "final", "mixer_ab", "ffn0", "mixer_c", "ffn1"]
INPUTS = [
    "x", "c", "norm_mix_g", "norm_ffn_g", "ada_w", "ada_b", "attn_w_in", "attn_f_bias", "attn_w_o", "pool_w",
    "pool_scale", "router_w", "router_bias", "exp_w1", "exp_w3", "exp_w2", "norm_final_g", "norm_g_2",
    "ab_w_in_2", "ab_conv_w_2", "ab_conv_b_2", "ab_wq_2", "ab_wk_2", "ab_wv_2", "ab_w_if_2", "ab_b_if_2",
    "ab_mh_gain_2", "ab_skip_2", "ab_a_re_2", "ab_a_im_2", "ab_log_dt_2", "ab_b_re_2", "ab_b_im_2",
    "ab_c_re_2", "ab_c_im_2", "ab_d_2", "ab_w_glu_2", "ab_b_glu_2", "ab_w_out_2", "c_w_in_2", "c_lb_raw_2",
    "c_g_gain_2", "c_w_out_2", "ffn_w1_2", "ffn_w3_2", "ffn_w2_2",
]


def kernel(**inputs):
    import concourse.bacc as bacc
    from concourse.bass_utils import run_bass_kernel_spmd

    nc = bacc.Bacc("TRN2", target_bir_lowering=False, num_devices=1)
    arrays, aps = {}, {}
    for name in INPUTS:
        a = np.ascontiguousarray(inputs[name])
        arrays[f"in_{name}"] = a
        aps[name] = nc.dram_tensor(f"in_{name}", a.shape, mybir.dt.from_np(a.dtype), kind="ExternalInput").ap()
    arrays["in_consts"] = CONSTANTS
    aps["consts"] = nc.dram_tensor("in_consts", CONSTANTS.shape, mybir.dt.float32, kind="ExternalInput").ap()
    out = nc.dram_tensor("out", (1, S, D), mybir.dt.float32, kind="ExternalOutput").ap()
    build_program(nc, aps, out)
    r = run_bass_kernel_spmd(nc, [arrays], core_ids=[0])
    return r.results[0]["out"]
```
